# Optimizing a Trainium2 kernel written in Bass

```python
import jax, jax.numpy as jnp
from jax import lax
import numpy as np
import math

D_MODEL = 1024
BATCH = 1
SEQ = 256
DEPTH = 2

HEAD_DIM = 128
MOBA_HEADS = 4
RET_HEADS = 4
MOBA_BLOCK = 256
MOBA_TOPK = 3
MOBA_QCHUNK = 32
RET_CHUNK = 128
CONV_WIDTH = 3
PEER_HEADS = 8
PEER_NKEYS = 128
PEER_NEXPERTS = PEER_NKEYS * PEER_NKEYS
PEER_TOPK = 16
PEER_DKEY = 256
PEER_TOKCHUNK = 128
ROPE_THETA = 10000.0
EPS = 1e-6
N_EVEN = (DEPTH + 1) // 2
N_ODD = DEPTH // 2
MOBA_W = MOBA_HEADS * HEAD_DIM
RET_W = RET_HEADS * HEAD_DIM
EVEN_SPLITS = (MOBA_W, MOBA_W, MOBA_W, RET_W, RET_W, RET_W, RET_W)
EVEN_IN = sum(EVEN_SPLITS)
EVEN_OUT_IN = MOBA_W + RET_W


def rmsnorm(x, g):
    xf = x.astype(jnp.float32)
    y = xf * lax.rsqrt(jnp.mean(xf * xf, axis=-1, keepdims=True) + EPS)
    return (y * g.astype(jnp.float32)).astype(x.dtype)

def rope(t):
    s, dh = t.shape[2], t.shape[3]
    half = dh // 2
    inv = ROPE_THETA ** (-jnp.arange(half, dtype=jnp.float32) / half)
    ang = jnp.arange(s, dtype=jnp.float32)[:, None] * inv[None, :]
    cos = jnp.cos(ang).astype(t.dtype)
    sin = jnp.sin(ang).astype(t.dtype)
    t1, t2 = t[..., :half], t[..., half:]
    return jnp.concatenate([t1 * cos - t2 * sin, t2 * cos + t1 * sin], axis=-1)

def split_heads(t, n):
    b, s, _ = t.shape
    return t.reshape(b, s, n, HEAD_DIM).transpose(0, 2, 1, 3)

def merge_heads(t):
    b, h, s, dh = t.shape
    return t.transpose(0, 2, 1, 3).reshape(b, s, h * dh)

def moba_attention(q, k, v):
    b, h, s, dh = q.shape
    nb = -(-s // MOBA_BLOCK)
    pad = nb * MOBA_BLOCK - s
    kb = jnp.pad(k, ((0, 0), (0, 0), (0, pad), (0, 0))).reshape(b, h, nb, MOBA_BLOCK, dh)
    vb = jnp.pad(v, ((0, 0), (0, 0), (0, pad), (0, 0))).reshape(b, h, nb, MOBA_BLOCK, dh)
    counts = jnp.minimum(MOBA_BLOCK, s - jnp.arange(nb) * MOBA_BLOCK).astype(jnp.float32)
    kmean = kb.astype(jnp.float32).sum(axis=3) / counts[None, None, :, None]
    gate = jnp.einsum('bhsd,bhnd->bhsn', q.astype(jnp.float32), kmean)
    qblk = jnp.arange(s) // MOBA_BLOCK
    past = jnp.arange(nb)[None, :] < qblk[:, None]
    gate = jnp.where(past, gate, -jnp.inf)
    kk = min(MOBA_TOPK, nb)
    _, sel = lax.top_k(gate, kk)
    valid = sel < qblk[:, None]
    nq = s // MOBA_QCHUNK
    def chunked(t):
        return t.reshape(b, h, nq, MOBA_QCHUNK, *t.shape[3:]).transpose(2, 0, 1, 3, *range(4, t.ndim + 1))
    qs, sels, valids = chunked(q), chunked(sel), chunked(valid)
    scale = dh ** -0.5
    bi = jnp.arange(b)[:, None, None, None]
    hi = jnp.arange(h)[None, :, None, None]

    def step(args):
        ci, qc, selc, validc = args
        tpos = ci * MOBA_QCHUNK + jnp.arange(MOBA_QCHUNK)
        ob = (ci * MOBA_QCHUNK) // MOBA_BLOCK
        k_own = lax.dynamic_index_in_dim(kb, ob, axis=2, keepdims=False)
        v_own = lax.dynamic_index_in_dim(vb, ob, axis=2, keepdims=False)
        kpos = ob * MOBA_BLOCK + jnp.arange(MOBA_BLOCK)
        s_own = jnp.einsum('bhqd,bhkd->bhqk', qc, k_own).astype(jnp.float32) * scale
        s_own = jnp.where(kpos[None, :] <= tpos[:, None], s_own, -jnp.inf)
        kg = kb[bi, hi, selc]
        vg = vb[bi, hi, selc]
        s_sel = jnp.einsum('bhqd,bhqjkd->bhqjk', qc, kg).astype(jnp.float32) * scale
        s_sel = jnp.where(validc[..., None], s_sel, -jnp.inf)
        scores = jnp.concatenate([s_sel.reshape(b, h, MOBA_QCHUNK, kk * MOBA_BLOCK), s_own], axis=-1)
        p = jax.nn.softmax(scores, axis=-1).astype(v.dtype)
        p_sel = p[..., :kk * MOBA_BLOCK].reshape(b, h, MOBA_QCHUNK, kk, MOBA_BLOCK)
        p_own = p[..., kk * MOBA_BLOCK:]
        return (jnp.einsum('bhqjk,bhqjkd->bhqd', p_sel, vg)
                + jnp.einsum('bhqk,bhkd->bhqd', p_own, v_own))

    out = lax.map(step, (jnp.arange(nq), qs, sels, valids))
    return out.transpose(1, 2, 0, 3, 4).reshape(b, h, s, dh)

def retention(q, k, v):
    b, h, s, dh = q.shape
    c = RET_CHUNK
    nc = s // c
    log_g = jnp.log(1.0 - 2.0 ** (-5.0 - jnp.arange(h, dtype=jnp.float32)))
    idx = jnp.arange(c, dtype=jnp.float32)
    diff = idx[:, None] - idx[None, :]
    dmask = jnp.where(diff >= 0, jnp.exp(log_g[:, None, None] * jnp.maximum(diff, 0.0)), 0.0)
    xi = jnp.exp(log_g[:, None] * (idx + 1.0))[..., None]
    zeta = jnp.exp(log_g[:, None] * (c - 1.0 - idx))[..., None]
    gc = jnp.exp(log_g * c)[:, None, None]
    def chunked(t):
        return t.astype(jnp.float32).reshape(b, h, nc, c, dh).transpose(2, 0, 1, 3, 4)
    qs, ks, vs = chunked(q), chunked(k * (dh ** -0.5)), chunked(v)

    def step(state, inp):
        qc, kc, vc = inp
        inner = jnp.einsum('bhnd,bhmd->bhnm', qc, kc) * dmask
        o = jnp.einsum('bhnm,bhmd->bhnd', inner, vc) + jnp.einsum('bhnd,bhde->bhne', qc, state) * xi
        state = state * gc + jnp.einsum('bhmd,bhme->bhde', kc * zeta, vc)
        return state, o

    state0 = jnp.zeros((b, h, dh, dh), jnp.float32)
    _, outs = lax.scan(step, state0, (qs, ks, vs))
    return outs.transpose(1, 2, 0, 3, 4).reshape(b, h, s, dh)

def attn_retention_mixer(xn, w_in, w_out):
    proj = xn @ w_in
    cuts = list(np.cumsum(EVEN_SPLITS)[:-1])
    mq, mk, mv, rq, rk, rv, rg = jnp.split(proj, cuts, axis=-1)
    mq, mk, mv = split_heads(mq, MOBA_HEADS), split_heads(mk, MOBA_HEADS), split_heads(mv, MOBA_HEADS)
    rq, rk, rv = split_heads(rq, RET_HEADS), split_heads(rk, RET_HEADS), split_heads(rv, RET_HEADS)
    mo = merge_heads(moba_attention(rope(mq), rope(mk), mv))
    ro = retention(rope(rq), rope(rk), rv)
    ro = ro * lax.rsqrt(jnp.mean(ro * ro, axis=-1, keepdims=True) + EPS)
    ro = merge_heads(ro).astype(xn.dtype) * jax.nn.silu(rg)
    return jnp.concatenate([mo, ro], axis=-1) @ w_out

def short_conv_mixer(xn, w_in, conv_w, w_out):
    d = xn.shape[-1]
    bg, cg, hx = jnp.split(xn @ w_in, 3, axis=-1)
    u = cg * hx
    y = lax.conv_general_dilated(u, conv_w[:, None, :], window_strides=(1,),
                                 padding=[(CONV_WIDTH - 1, 0)],
                                 dimension_numbers=('NWC', 'WIO', 'NWC'),
                                 feature_group_count=d)
    return (bg * y) @ w_out

def peer(xn, w_q, sub_keys, u, v):
    b, s, d = xn.shape
    t = xn.reshape(b * s, d)
    n_tok = b * s
    q = (t @ w_q).reshape(n_tok, PEER_HEADS, 2, PEER_DKEY // 2)
    sc = jnp.einsum('thpd,hpnd->thpn', q, sub_keys).astype(jnp.float32)
    s1, i1 = lax.top_k(sc[:, :, 0], PEER_TOPK)
    s2, i2 = lax.top_k(sc[:, :, 1], PEER_TOPK)
    cand = (s1[..., :, None] + s2[..., None, :]).reshape(n_tok, PEER_HEADS, PEER_TOPK * PEER_TOPK)
    cidx = (i1[..., :, None] * PEER_NKEYS + i2[..., None, :]).reshape(n_tok, PEER_HEADS, PEER_TOPK * PEER_TOPK)
    top_s, pos = lax.top_k(cand, PEER_TOPK)
    eidx = jnp.take_along_axis(cidx, pos, axis=-1)
    gate = jax.nn.softmax(top_s, axis=-1).astype(xn.dtype)
    nt = n_tok // PEER_TOKCHUNK

    def step(args):
        tc, ec, gc = args
        hid = jax.nn.gelu(jnp.einsum('td,thkd->thk', tc, u[ec]), approximate=False)
        return jnp.einsum('thk,thkd->td', gc * hid, v[ec])

    out = lax.map(step, (t.reshape(nt, PEER_TOKCHUNK, d),
                         eidx.reshape(nt, PEER_TOKCHUNK, PEER_HEADS, PEER_TOPK),
                         gate.reshape(nt, PEER_TOKCHUNK, PEER_HEADS, PEER_TOPK)))
    return out.reshape(b, s, d)

def first_inputs(seed: int = 0) -> dict:
    key = jax.random.key(seed)
    ks = jax.random.split(key, 16)
    f32 = jnp.float32
    nrm = lambda k, shape, sc: jax.random.normal(k, shape, f32) * sc
    return {
        "x": nrm(ks[0], (BATCH, SEQ, D_MODEL), 1.0),
        "norm_mix": 1.0 + nrm(ks[1], (DEPTH, D_MODEL), 0.02),
        "norm_ffn": 1.0 + nrm(ks[2], (DEPTH, D_MODEL), 0.02),
        "even_w_in": nrm(ks[3], (N_EVEN, D_MODEL, EVEN_IN), D_MODEL ** -0.5),
        "even_w_out": nrm(ks[4], (N_EVEN, EVEN_OUT_IN, D_MODEL), EVEN_OUT_IN ** -0.5),
        "odd_w_in": nrm(ks[5], (N_ODD, D_MODEL, 3 * D_MODEL), D_MODEL ** -0.5),
        "odd_conv": nrm(ks[6], (N_ODD, CONV_WIDTH, D_MODEL), CONV_WIDTH ** -0.5),
        "odd_w_out": nrm(ks[7], (N_ODD, D_MODEL, D_MODEL), D_MODEL ** -0.5),
        "peer_w_q": nrm(ks[8], (DEPTH, D_MODEL, PEER_HEADS * PEER_DKEY), D_MODEL ** -0.5),
        "peer_sub_keys": nrm(ks[9], (DEPTH, PEER_HEADS, 2, PEER_NKEYS, PEER_DKEY // 2), (PEER_DKEY // 2) ** -0.5),
        "peer_u": nrm(ks[10], (DEPTH, PEER_NEXPERTS, D_MODEL), D_MODEL ** -0.5),
        "peer_v": nrm(ks[11], (DEPTH, PEER_NEXPERTS, D_MODEL), 0.1),
        "final_norm": 1.0 + nrm(ks[12], (D_MODEL,), 0.02),
    }

def first_block(x, norm_mix, norm_ffn, even_w_in, even_w_out, odd_w_in, odd_conv, odd_w_out,
              peer_w_q, peer_sub_keys, peer_u, peer_v, final_norm):
    h = x
    for layer in range(DEPTH):
        xn = rmsnorm(h, norm_mix[layer])
        i = layer // 2
        if layer % 2 == 0:
            h = h + attn_retention_mixer(xn, even_w_in[i], even_w_out[i])
        else:
            h = h + short_conv_mixer(xn, odd_w_in[i], odd_conv[i], odd_w_out[i])
        h = h + peer(rmsnorm(h, norm_ffn[layer]), peer_w_q[layer], peer_sub_keys[layer],
                     peer_u[layer], peer_v[layer])
    return rmsnorm(h, final_norm)


DEPTH_2 = 1

N_META = 16
BLOCK = 128
PAD_FRONT = BLOCK - N_META
HEAD_DIM_2 = 64
FOX_HEADS = 8
SWA_Q_HEADS = 8
SWA_KV_HEADS = 2
WINDOW = 128
N_BUCKETS = 32
MAX_DISTANCE = 128
D_FF = 2816
NEG = -1e30
FORGET_BIAS_INIT = 2.0
FOX_W = FOX_HEADS * HEAD_DIM_2
SWA_QW = SWA_Q_HEADS * HEAD_DIM_2
SWA_KVW = SWA_KV_HEADS * HEAD_DIM_2
D_IN = 3 * FOX_W + FOX_HEADS + SWA_QW + 2 * SWA_KVW + 2 * D_MODEL


def rms_norm(x, g):
    xf = x.astype(jnp.float32)
    ms = jnp.mean(xf * xf, axis=-1, keepdims=True)
    return (xf * lax.rsqrt(ms + EPS) * g.astype(jnp.float32)).astype(x.dtype)

def swiglu(h, w_in, w_out):
    gu = h @ w_in
    gate, up = jnp.split(gu, 2, axis=-1)
    return (jax.nn.silu(gate) * up) @ w_out

def t5_bucket(dist):
    n = jnp.maximum(dist, 0)
    max_exact = N_BUCKETS // 2
    nf = jnp.maximum(n, 1).astype(jnp.float32)
    large = max_exact + (jnp.log(nf / max_exact) / math.log(MAX_DISTANCE / max_exact)
                         * (N_BUCKETS - max_exact)).astype(jnp.int32)
    large = jnp.minimum(large, N_BUCKETS - 1)
    return jnp.where(n < max_exact, n, large)

def fox_attention(q, k, v, log_f):
    b, p, h, dh = q.shape
    nb = p // BLOCK
    c_k = jnp.cumsum(log_f, axis=1).transpose(0, 2, 1)
    k_pos = jnp.arange(p)
    k_valid = k_pos >= PAD_FRONT
    qb = q.reshape(b, nb, BLOCK, h, dh).transpose(1, 0, 2, 3, 4)
    cqb = c_k.reshape(b, h, nb, BLOCK).transpose(2, 0, 1, 3)
    scale = dh ** -0.5

    def one_block(args):
        qi, cqi, i = args
        q_pos = i * BLOCK + jnp.arange(BLOCK)
        s = jnp.einsum('bqhd,bkhd->bhqk', qi, k, preferred_element_type=jnp.float32) * scale
        s = s + cqi[..., :, None] - c_k[:, :, None, :]
        mask = (k_pos[None, :] <= q_pos[:, None]) & k_valid[None, :]
        s = jnp.where(mask[None, None], s, NEG)
        pr = jax.nn.softmax(s, axis=-1)
        return jnp.einsum('bhqk,bkhd->bqhd', pr.astype(v.dtype), v)

    out = lax.map(one_block, (qb, cqb, jnp.arange(nb)))
    return out.transpose(1, 0, 2, 3, 4).reshape(b, p, h * dh)

def swa_attention(q, k, v, sinks, rel_bias_table):
    b, p, hq, dh = q.shape
    kv = k.shape[2]
    r = hq // kv
    nb = p // BLOCK
    scale = dh ** -0.5
    qb = q.reshape(b, nb, BLOCK, kv, r, dh)

    def band(a):
        a_ext = jnp.concatenate([jnp.zeros_like(a[:, :BLOCK]), a], axis=1)
        a_ext = a_ext.reshape(b, nb + 1, BLOCK, kv, dh)
        return jnp.concatenate([a_ext[:, :-1], a_ext[:, 1:]], axis=2)

    kb, vb = band(k), band(v)
    km, vm = k[:, PAD_FRONT:BLOCK], v[:, PAD_FRONT:BLOCK]
    q_pos = jnp.arange(nb)[:, None] * BLOCK + jnp.arange(BLOCK)[None, :]
    band_pos = (jnp.arange(nb)[:, None] - 1) * BLOCK + jnp.arange(2 * BLOCK)[None, :]
    meta_pos = PAD_FRONT + jnp.arange(N_META)
    d_band = q_pos[:, :, None] - band_pos[:, None, :]
    m_band = (d_band >= 0) & (d_band < WINDOW) & (band_pos[:, None, :] >= PAD_FRONT)
    d_meta = q_pos[:, :, None] - meta_pos[None, None, :]
    m_meta = d_meta >= WINDOW
    table = rel_bias_table.astype(jnp.float32)
    bias_band = table[t5_bucket(d_band)].transpose(0, 3, 1, 2).reshape(nb, kv, r, BLOCK, 2 * BLOCK)
    bias_meta = table[t5_bucket(d_meta)].transpose(0, 3, 1, 2).reshape(nb, kv, r, BLOCK, N_META)

    s_band = jnp.einsum('bnqgrd,bnkgd->bngrqk', qb, kb, preferred_element_type=jnp.float32) * scale + bias_band[None]
    s_band = jnp.where(m_band[None, :, None, None], s_band, NEG)
    s_meta = jnp.einsum('bnqgrd,bmgd->bngrqm', qb, km, preferred_element_type=jnp.float32) * scale + bias_meta[None]
    s_meta = jnp.where(m_meta[None, :, None, None], s_meta, NEG)
    s = jnp.concatenate([s_band, s_meta], axis=-1)
    sink = sinks.astype(jnp.float32).reshape(kv, r)[None, None, :, :, None, None]
    mx = jnp.maximum(jnp.max(s, axis=-1, keepdims=True), sink)
    pr = jnp.exp(s - mx)
    pr = pr / (jnp.sum(pr, axis=-1, keepdims=True) + jnp.exp(sink - mx))
    pr = pr.astype(v.dtype)
    out = (jnp.einsum('bngrqk,bnkgd->bnqgrd', pr[..., :2 * BLOCK], vb)
           + jnp.einsum('bngrqm,bmgd->bnqgrd', pr[..., 2 * BLOCK:], vm))
    return out.reshape(b, p, hq * dh)

def token_mixer(h, rel_bias_table, w_in, forget_bias, fox_q_norm, fox_k_norm,
                swa_q_norm, swa_k_norm, swa_sinks, w_branch_fox, w_branch_swa, w_out):
    b, p, _ = h.shape
    proj = h @ w_in
    widths = [FOX_W, FOX_W, FOX_W, FOX_HEADS, SWA_QW, SWA_KVW, SWA_KVW, D_MODEL]
    idx = list(np.cumsum(widths))
    qa, ka, va, fa, qb, kb, vb, ga, gb = jnp.split(proj, idx, axis=-1)
    qa = rms_norm(qa.reshape(b, p, FOX_HEADS, HEAD_DIM_2), fox_q_norm)
    ka = rms_norm(ka.reshape(b, p, FOX_HEADS, HEAD_DIM_2), fox_k_norm)
    va = va.reshape(b, p, FOX_HEADS, HEAD_DIM_2)
    log_f = jax.nn.log_sigmoid(fa.astype(jnp.float32) + forget_bias.astype(jnp.float32))
    qb = rms_norm(qb.reshape(b, p, SWA_Q_HEADS, HEAD_DIM_2), swa_q_norm)
    kb = rms_norm(kb.reshape(b, p, SWA_KV_HEADS, HEAD_DIM_2), swa_k_norm)
    vb = vb.reshape(b, p, SWA_KV_HEADS, HEAD_DIM_2)
    o_fox = fox_attention(qa, ka, va, log_f)
    o_swa = swa_attention(qb, kb, vb, swa_sinks, rel_bias_table)
    y = jax.nn.sigmoid(ga) * (o_fox @ w_branch_fox) + jax.nn.sigmoid(gb) * (o_swa @ w_branch_swa)
    return y @ w_out

def second_inputs(seed: int = 0) -> dict:
    key = jax.random.key(seed)
    ks = jax.random.split(key, 24)
    f32 = jnp.float32

    def nrm(k, shape, scale):
        return jax.random.normal(k, shape, f32) * scale

    def gain(k, shape):
        return 1.0 + 0.1 * jax.random.normal(k, shape, f32)

    return {
        "x": nrm(ks[0], (BATCH, SEQ, D_MODEL), 1.0),
        "meta_tokens": nrm(ks[1], (N_META, D_MODEL), 1.0),
        "rel_bias_table": nrm(ks[2], (N_BUCKETS, SWA_Q_HEADS), 0.5),
        "ffn1_norm": gain(ks[3], (DEPTH_2, D_MODEL)),
        "ffn1_w_in": nrm(ks[4], (DEPTH_2, D_MODEL, 2 * D_FF), D_MODEL ** -0.5),
        "ffn1_w_out": nrm(ks[5], (DEPTH_2, D_FF, D_MODEL), D_FF ** -0.5),
        "mix_norm": gain(ks[6], (DEPTH_2, D_MODEL)),
        "w_in": nrm(ks[7], (DEPTH_2, D_MODEL, D_IN), D_MODEL ** -0.5),
        "forget_bias": FORGET_BIAS_INIT + 0.1 * jax.random.normal(ks[8], (DEPTH_2, FOX_HEADS), f32),
        "fox_q_norm": gain(ks[9], (DEPTH_2, HEAD_DIM_2)),
        "fox_k_norm": gain(ks[10], (DEPTH_2, HEAD_DIM_2)),
        "swa_q_norm": gain(ks[11], (DEPTH_2, HEAD_DIM_2)),
        "swa_k_norm": gain(ks[12], (DEPTH_2, HEAD_DIM_2)),
        "swa_sinks": nrm(ks[13], (DEPTH_2, SWA_Q_HEADS), 0.5),
        "w_branch_fox": nrm(ks[14], (DEPTH_2, FOX_W, D_MODEL), FOX_W ** -0.5),
        "w_branch_swa": nrm(ks[15], (DEPTH_2, SWA_QW, D_MODEL), SWA_QW ** -0.5),
        "w_out": nrm(ks[16], (DEPTH_2, D_MODEL, D_MODEL), D_MODEL ** -0.5),
        "ffn2_norm": gain(ks[17], (DEPTH_2, D_MODEL)),
        "ffn2_w_in": nrm(ks[18], (DEPTH_2, D_MODEL, 2 * D_FF), D_MODEL ** -0.5),
        "ffn2_w_out": nrm(ks[19], (DEPTH_2, D_FF, D_MODEL), D_FF ** -0.5),
    }

def second_block(x, meta_tokens, rel_bias_table, ffn1_norm, ffn1_w_in, ffn1_w_out, mix_norm,
              w_in, forget_bias, fox_q_norm, fox_k_norm, swa_q_norm, swa_k_norm, swa_sinks,
              w_branch_fox, w_branch_swa, w_out, ffn2_norm, ffn2_w_in, ffn2_w_out):
    b = x.shape[0]
    pad = jnp.zeros((b, PAD_FRONT, D_MODEL), x.dtype)
    meta = jnp.broadcast_to(meta_tokens.astype(x.dtype)[None], (b, N_META, D_MODEL))
    h = jnp.concatenate([pad, meta, x], axis=1)
    for l in range(DEPTH_2):
        h = h + 0.5 * swiglu(rms_norm(h, ffn1_norm[l]), ffn1_w_in[l], ffn1_w_out[l])
        h = h + token_mixer(rms_norm(h, mix_norm[l]), rel_bias_table, w_in[l], forget_bias[l],
                            fox_q_norm[l], fox_k_norm[l], swa_q_norm[l], swa_k_norm[l],
                            swa_sinks[l], w_branch_fox[l], w_branch_swa[l], w_out[l])
        h = h + 0.5 * swiglu(rms_norm(h, ffn2_norm[l]), ffn2_w_in[l], ffn2_w_out[l])
    return h[:, BLOCK:]


def setup_inputs(seed=0):
    out = dict(first_inputs(seed))
    for name, value in second_inputs(seed + 1).items():
        if name != "x":
            out[name + "_2"] = value
    return out


def reference(
    x, norm_mix, norm_ffn, even_w_in, even_w_out, odd_w_in, odd_conv, odd_w_out, peer_w_q,
    peer_sub_keys, peer_u, peer_v, final_norm, meta_tokens_2, rel_bias_table_2, ffn1_norm_2,
    ffn1_w_in_2, ffn1_w_out_2, mix_norm_2, w_in_2, forget_bias_2, fox_q_norm_2, fox_k_norm_2,
    swa_q_norm_2, swa_k_norm_2, swa_sinks_2, w_branch_fox_2, w_branch_swa_2, w_out_2,
    ffn2_norm_2, ffn2_w_in_2, ffn2_w_out_2,
):
    x = first_block(
        x, norm_mix, norm_ffn, even_w_in, even_w_out, odd_w_in, odd_conv, odd_w_out, peer_w_q,
        peer_sub_keys, peer_u, peer_v, final_norm,
    )
    return second_block(
        x, meta_tokens_2, rel_bias_table_2, ffn1_norm_2, ffn1_w_in_2, ffn1_w_out_2, mix_norm_2,
        w_in_2, forget_bias_2, fox_q_norm_2, fox_k_norm_2, swa_q_norm_2, swa_k_norm_2,
        swa_sinks_2, w_branch_fox_2, w_branch_swa_2, w_out_2, ffn2_norm_2, ffn2_w_in_2,
        ffn2_w_out_2,
    )


_drawn_inputs = setup_inputs


def setup_inputs(seed=0):
    import zlib

    import numpy as np

    out = dict(_drawn_inputs(seed))
    spreads = {}
    factors = {'norm_ffn': 4.555,
     'forget_bias_2': 38.912,
     'fox_q_norm_2': 3.734,
     'fox_k_norm_2': 4.102,
     'swa_q_norm_2': 5.887,
     'swa_k_norm_2': 5.759,
     'swa_sinks_2': 8.0}
    for name, (base, spread) in spreads.items():
        noise = np.random.default_rng([zlib.crc32(name.encode()), seed]).standard_normal(out[name].shape)
        drawn = base * np.exp(spread * noise) if base else spread * noise
        out[name] = __import__('jax').numpy.asarray(drawn.astype(out[name].dtype))
    for name, factor in factors.items():
        out[name] = (out[name] * factor).astype(out[name].dtype)
    return out
```

```python
from contextlib import ExitStack

import numpy as np

import concourse.bass as bass
from concourse import mybir

ALU = mybir.AluOpType
ACT = mybir.ActivationFunctionType
AX = mybir.AxisListType
F32 = mybir.dt.float32
U32 = mybir.dt.uint32

P = 128
D = 1024
K = D // P
S = 256
META = 16
TA = META + S
XS = slice(META, TA)
ALL = slice(0, TA)
NT = S // P
EPS = 1e-6
NEG = -1e30
HEADS = 4
RING = 8
NKEYS = 128
PH = 8
TOPK = 16
CHUNKS = NKEYS
FF = 2816
FC = FF // P
FOXH = 8
HD2 = 64
DX = 384
DM = 272
DTAB = DX + DM
NB = 32

EVEN_ITEMS = [("proj", 0)]
for _j in range(1, 16):
    EVEN_ITEMS += [("proj", _j), ("rot", _j - 1)]
EVEN_ITEMS += [("rot", 15)] + [("val", j) for j in range(8)] + [("gate", j) for j in range(4)]


def attention_items(units, lag=2):
    items = []
    for u in range(units + lag):
        if u < units:
            items.append(("score", u))
        if u >= lag:
            items.append(("turn", u - lag))
            if (u - lag) % NT == NT - 1:
                items.append(("mix", (u - lag) // NT))
    return items


MOBA_ITEMS = attention_items(HEADS * NT)
RET_ITEMS = [("inner", 0)]
for _j in range(1, HEADS):
    RET_ITEMS += [("inner", _j), ("outer", _j - 1)]
RET_ITEMS += [("outer", HEADS - 1)] + [("mean", j) for j in range(HEADS)]
ODD_ITEMS = [(kind, c) for c in range(K) for kind in ("cgate", "value", "bgate")]
FFN_ITEMS = [(kind, c) for c in range(FC) for kind in ("ffgate", "ffup")]
QK2 = 14
MIX_ITEMS = [("forget", 0), ("proj", 0)]
for _j in range(1, QK2):
    MIX_ITEMS += [("proj", _j), ("mean", _j - 1)]
MIX_ITEMS += [("mean", QK2 - 1)] + [("val", j) for j in range(5)] + [("table", 0), ("table", 1)]
FOX_ITEMS = attention_items(FOXH * NT)
GATE_ITEMS = [("gate", j) for j in range(2 * K)]
BRANCH_ITEMS = [(kind, c) for c in range(K) for kind in ("foxout", "swaout")]

STAGES = [("norm0", 1), ("even", len(EVEN_ITEMS)), ("moba", len(MOBA_ITEMS)), ("ret", len(RET_ITEMS)),
          ("evenout", K)]
for _l in range(2):
    if _l == 1:
        STAGES += [("norm2", 1), ("odd", len(ODD_ITEMS)), ("oddout", K)]
    STAGES += [(f"norm{2 * _l + 1}", 1), (f"query{_l}", 16), (f"subkey{_l}", 8), (f"turn{_l}", 2),
               (f"coef{_l}", S // 4), (f"expert{_l}", CHUNKS)]
STAGES += [("norm4", 1), ("norm5", 1), ("ffn1", len(FFN_ITEMS)), ("ffn1out", K),
           ("norm6", 1), ("mix", len(MIX_ITEMS)), ("gates", len(GATE_ITEMS)), ("fox", len(FOX_ITEMS)), ("swa", len(FOX_ITEMS)),
           ("branch", len(BRANCH_ITEMS)), ("mixout", K),
           ("norm7", 1), ("ffn2", len(FFN_ITEMS)), ("ffn2out", K)]
W0 = {}
_n = 0
for _name, _count in STAGES:
    W0[_name] = _n
    _n += _count


def expert_slot(q):
    if q == 0:
        return "u", 0
    if q == 2 * CHUNKS - 1:
        return "v", CHUNKS - 1
    return ("u", (q + 1) // 2) if q % 2 else ("v", (q - 2) // 2)


def plan_slots():
    slots, base = [], {}

    def linear(name, items, kinds, array, first=0):
        base[name] = len(slots)
        n = first
        for i, (kind, _) in enumerate(items):
            if kind in kinds:
                slots.append((array, n, D, ("item", W0[name] + i)))
                n += 1

    def out(name, array, widths):
        base[name] = len(slots)
        for c in range(K):
            for part, width in enumerate(widths):
                slots.append((array, (c, part), width, ("item", W0[name] + c)))

    linear("even", EVEN_ITEMS, ("proj", "val", "gate"), "even_in")
    out("evenout", "even_out", [D])
    for l in range(2):
        if l == 1:
            linear("odd", ODD_ITEMS, ("cgate", "value", "bgate"), "odd_in")
            out("oddout", "odd_out", [D])
        base[f"query{l}"] = len(slots)
        for j in range(16):
            slots.append((f"query{l}", j, D, ("item", W0[f"query{l}"] + j)))
        base[f"subkey{l}"] = len(slots)
        for j in range(2):
            slots.append((f"subkey{l}", j, D, ("item", W0[f"subkey{l}"] + 4 + 2 * j + 1)))
        base[f"expert{l}"] = len(slots)
        for q in range(2 * CHUNKS):
            kind, e = expert_slot(q)
            by = ("item", W0[f"expert{l}"] + e) if kind == "u" else ("chunk", l * CHUNKS + e)
            slots.append((f"{kind}{l}", e, D, by))
    ff_out = [D, D, (FC - 16) * P]
    linear("ffn1", FFN_ITEMS, ("ffgate", "ffup"), "ffn1_in")
    out("ffn1out", "ffn1_out", ff_out)
    linear("mix", MIX_ITEMS[:], ("proj", "val"), "mix_in")
    linear("gates", GATE_ITEMS, ("gate",), "gate_in")
    base["branch"] = len(slots)
    for c in range(K):
        slots.append(("branch", c, D, ("item", W0["branch"] + 2 * c + 1)))
    out("mixout", "mix_out", [D])
    linear("ffn2", FFN_ITEMS, ("ffgate", "ffup"), "ffn2_in")
    out("ffn2out", "ffn2_out", ff_out)
    return slots, base


SLOTS, SLOT0 = plan_slots()

CONST = {}
_n = 0
for _name, _count in [("ident", P), ("rot", P), ("inv_d", P), ("inv_head", P), ("inv_half", P), ("iota", P),
                      ("causal", S), ("gains", 8 * K),
                      ("conv", 3 * K), ("headgain", QK2)]:
    CONST[_name] = (_n, _n + _count)
    _n += _count
N_CONST = _n
EARLY = [("cos", S), ("sin", S), ("decay", HEADS * 384)]


class Tally:

    def __init__(self, sem):
        self.sem, self.n = sem, 0

    def up(self):
        self.n += 1
        return 1


def build(nc, a):
    with ExitStack() as ctx:
        def sb(name, shape, dt=F32):
            return ctx.enter_context(nc.sbuf_tensor(name, shape, dt))

        def sem(name):
            return ctx.enter_context(nc.semaphore(name))

        stream = sb("stream", [P, K, TA])
        normed = sb("normed", [P, K, TA])
        ring = sb("ring", [P, RING, D])
        arena = sb("arena", [P, S * NKEYS])
        const = sb("const", [P, N_CONST])
        rstd = sb("rstd", [P, TA])
        hots = sb("hots", [P, 2, 8, P])
        hidden = sb("hidden", [P, 4, S])
        weighed = sb("weighed", [P, 4, S])
        picks = sb("picks", [P, 3, S])
        small = sb("small", [P, 16])
        acc = ctx.enter_context(nc.psum_tensor("acc", [P, 4, 512], F32))
        work = ctx.enter_context(nc.psum_tensor("work", [P, 4, 512], F32))

        def cst(name, rows=P):
            lo, hi = CONST[name]
            return const[0:rows, lo:hi]

        ident, iota = cst("ident"), cst("iota")
        gains = cst("gains").rearrange("p (n k) -> p n k", k=K)
        conv = cst("conv").rearrange("p (w k) -> p w k", k=K)
        eps_col = small[:, 0:1]
        zero_col = small[:, 1:2]

        used = {}

        def view(group, shape):
            n = int(np.prod(shape))
            at = used.get(group, 0)
            used[group] = at + n
            assert used[group] <= S * NKEYS, group
            v = arena[:, at:at + n]
            names = "abcd"[:len(shape)]
            if len(shape) > 1:
                v = v.rearrange(f"p ({' '.join(names)}) -> p {' '.join(names)}",
                                **{x: s for x, s in zip(names[1:], shape[1:])})
            return v

        early = view("even", [2 * S + HEADS * 384])
        cos, sin = early[:, 0:S], early[:, S:2 * S]
        decay = early[:, 2 * S:].rearrange("p (h n) -> p h n", h=HEADS)
        qk1 = view("even", [16, S])
        qk1raw = view("even", [2, S])
        rot_tmp = view("even", [2, S])
        val1 = view("even", [8, NT, P])
        silu1 = view("even", [HEADS, S])
        scores1 = view("even", [4, S])
        prob1 = view("even", [2, NT, S])
        inner1 = view("even", [2, 384])
        ret1 = view("even", [HEADS, S])
        retsq = view("even", [HEADS, S])
        retms = view("even", [HEADS, S])
        att1 = view("even", [K, S])
        cg = view("odd", [2, S])
        u_pad = view("odd", [2, S + 2])
        y_tmp = view("odd", [2, 2, S])
        z2 = view("odd", [K, S])
        query = view("peer", [16, S])
        sub = view("peer", [2, 512])
        sub2 = view("peer", [512])
        best = view("peer", [NT, 16, TOPK])
        best_at = view("peer", [NT, 16, TOPK])
        best_f = view("peer", [NT, 16, TOPK])
        cand = view("peer", [PH, TOPK * TOPK])
        cand2 = view("peer", [PH, TOPK * TOPK])
        pair = view("peer", [NT, PH * TOPK])
        pair_at = view("peer", [PH * TOPK])
        pair_ab = view("peer", [2, PH * TOPK])
        pair_f = view("peer", [2, PH * TOPK])
        chosen = view("peer", [NT, 3, PH * TOPK])
        eq = view("peer", [PH * TOPK, TOPK])
        ev = view("peer", [PH * TOPK, TOPK])
        psum8 = view("peer", [NT, 2, PH])
        coef = arena[:, :].rearrange("p (t e) -> p t e", e=NKEYS)
        ff_hid = view("ffn", [FC, TA])
        ff_silu = view("ffn", [2, TA])
        qk2 = view("mix", [QK2, TA])
        qk2raw = view("mix", [2, TA])
        qk2sq = view("mix", [2, TA])
        qk2ms = view("mix", [2, TA])
        val2 = view("mix", [5, 3, P])
        gate2 = view("mix", [2 * K, S])
        scores2 = view("mix", [4, TA + 4])
        prob2 = view("mix", [2, 3, 2, P])
        att2 = view("mix", [2, 4, S])
        bias2 = view("mix", [NT, FOXH, TA])
        mask2 = view("mix", [NT, TA])
        forget = view("mix", [8, TA])
        pick_head = view("mix", [FOXH, TA])
        neg_head = view("mix", [FOXH, P])
        table = view("mix", [FOXH])
        onehot = view("mix", [DTAB])
        table_out = view("mix", [DTAB])
        sinks = view("mix", [FOXH])
        mix_y = view("mix", [K, S])
        mix_t = view("mix", [2, 2, S])
        w_forget = view("mix", [K, FOXH])

        const_in, const2_in = sem("const_in"), sem("const2_in")
        landed = [sem(f"landed{r}") for r in range(RING)]
        bank_done = [sem(f"bank_done{b}") for b in range(4)]
        bank_free = [sem(f"bank_free{b}") for b in range(4)]
        chunk_ready, chunk_used = sem("chunk_ready"), sem("chunk_used")
        squares_ready, std_ready = sem("squares_ready"), sem("std_ready")
        normed_ready, stream_ready = sem("normed_ready"), sem("stream_ready")
        turned_ready = sem("turned_ready")
        scores_ready, exp_ready, probs_ready = sem("scores_ready"), sem("exp_ready"), sem("probs_ready")
        inner_ready = sem("inner_ready")
        retsq_ready, retstd_ready = sem("retsq_ready"), sem("retstd_ready")
        mixed_ready = sem("mixed_ready")
        zy_ready = sem("zy_ready")
        gate_diff_ready, gate_exp_ready, picks_ready = sem("gate_diff_ready"), sem("gate_exp_ready"), sem("picks_ready")
        hots_ready, sub_used = sem("hots_ready"), sem("sub_used")
        ff_ready = sem("ff_ready")
        qksq_ready, qkstd_ready, qk2_ready = sem("qksq_ready"), sem("qkstd_ready"), sem("qk2_ready")
        forget_in, forget_out, forget_ready = sem("forget_in"), sem("forget_out"), sem("forget_ready")
        table_ready, table_stored, bias_in = sem("table_ready"), sem("table_stored"), sem("bias_in")
        branch_ready = sem("branch_ready")
        memset_done = sem("memset_done")
        stored = sem("stored")
        vec = Tally(sem("vec_step"))
        own = Tally(sem("act_step"))

        def done(w):
            return bank_done[w % 4], w // 4 + 1

        def freed(w):
            return bank_free[w % 4], w // 4 + 1

        def wait_bank(pe, w):
            if w >= 4:
                pe.wait_ge(*freed(w - 4))

        def slot(n):
            return ring[:, n % RING, :]

        def wait_slot(pe, n):
            pe.wait_ge(landed[n % RING], 16 * (n // RING + 1))

        def released(n):
            kind, x = SLOTS[n][3]
            return done(x) if kind == "item" else (chunk_used, x + 1)

        def source(n):
            array, index, width, _ = SLOTS[n]
            if isinstance(index, tuple):
                c, part = index
                return a[array][c][:, part * D:part * D + width], width
            return a[array][index], width

        block = ctx.enter_context(nc.Block())

        @block.sync
        def _(sp):
            def load(n):
                src, width = source(n)
                if n >= RING:
                    sp.wait_ge(*released(n - RING))
                sp.dma_start(ring[:, n % RING, 0:width], src).then_inc(landed[n % RING], 16)

            def expert_loads(l):
                base, w, c0 = SLOT0[f"expert{l}"], W0[f"expert{l}"], l * CHUNKS
                for q in range(10):
                    load(base + q)
                turns = (CHUNKS - 2 - 4) // 4
                with sp.Fori(0, turns) as i:
                    for j in range(4):
                        q = 10 + 2 * j
                        sp.wait_ge(chunk_used, i * 4 + (c0 + j + 1))
                        sp.dma_start(ring[:, (base + q) % RING, :], a[f"v{l}"][i * 4 + (4 + j)]).then_inc(
                            landed[(base + q) % RING], 16)
                        x = w + 2 + j
                        sp.wait_ge(bank_done[x % 4], i + (x // 4 + 1))
                        sp.dma_start(ring[:, (base + q + 1) % RING, :], a[f"u{l}"][i * 4 + (6 + j)]).then_inc(
                            landed[(base + q + 1) % RING], 16)
                for q in range(10 + 8 * turns, 2 * CHUNKS):
                    load(base + q)

            sp.dma_start(stream[:, :, XS], a["x"]).then_inc(const_in, 16)
            sp.dma_start(const[:, :], a["const"]).then_inc(const_in, 16)
            sp.dma_start(early, a["early"]).then_inc(const_in, 16)
            sp.dma_start(stream[:, :, 0:META], a["meta"]).then_inc(const_in, 16)
            n = 0
            for l in range(2):
                while n < SLOT0[f"expert{l}"]:
                    load(n)
                    n += 1
                expert_loads(l)
                n += 2 * CHUNKS
            while n < len(SLOTS):
                load(n)
                n += 1
            sp.wait_ge(stream_ready, 7)
            sp.dma_start(a["out"], stream[:, :, XS]).then_inc(stored, 16)
            sp.wait_ge(stored, 16)

        @block.gpsimd
        def _(pool):
            pool.memset(eps_col, EPS)
            pool.memset(zero_col, 0.0).then_inc(memset_done, 1)
            pool.wait_ge(stream_ready, 5)
            pool.memset(table[:, :], NEG).then_inc(memset_done, 1)
            pool.memset(forget[:, :, :], 0.0).then_inc(memset_done, 1)
            pool.wait_ge(memset_done, 3)
            for dst, src in [(mask2[:, :, :], a["foxmask"]), (w_forget[:, :, :], a["w_forget"]),
                             (pick_head[0:FOXH, :, :], a["pick_head"]), (neg_head[0:FOXH, :, :], a["neg_head"]),
                             (table[0:NB, :], a["table"]), (onehot[0:NB + 1, :], a["onehot"]),
                             (sinks[:, :], a["sinks"].partition_broadcast(P)),
                             (small[0:FOXH, 4:5], a["forget_bias"])]:
                pool.dma_start(dst, src).then_inc(const2_in, 16)
            pool.wait_ge(table_ready, 2)
            pool.dma_start(a["scratch"].rearrange("q h d -> h q d"),
                           table_out[0:FOXH, :].unsqueeze(1).to_broadcast([FOXH, P, DTAB])).then_inc(table_stored, 16)
            pool.wait_ge(table_stored, 16)
            for t in range(NT):
                n = P * (t + 1)
                for lo, width, first, col in ((META, n, 255 - P * t, 0), (0, META, DX + 255 - P * t, 0)):
                    src = bass.AP(a["scratch"].tensor, first, [[FOXH * DTAB - 1, P], [DTAB, FOXH], [1, width]])
                    pool.dma_start(bias2[:, t, :, lo:lo + width], src).then_inc(bias_in, 16)

        @block.tensor
        def _(pe):
            def norm(n, cols):
                w = W0[f"norm{n}"]
                pe.wait_ge(squares_ready, n + 1)
                wait_bank(pe, w)
                width = cols.stop - cols.start
                for k in range(K):
                    mm = pe.matmul(work[:, w % 4, 0:width], cst("inv_d"), normed[:, k, cols], start=(k == 0), stop=(k == K - 1))
                mm.then_inc(bank_done[w % 4], 1)

            def project(w, n, rhs, width):
                wait_bank(pe, w)
                wait_slot(pe, n)
                for k in range(K):
                    mm = pe.matmul(work[:, w % 4, 0:width], slot(n)[:, k * P:(k + 1) * P], rhs(k), start=(k == 0), stop=(k == K - 1))
                mm.then_inc(bank_done[w % 4], 1)

            def values(w, n, tiles):
                wait_bank(pe, w)
                wait_slot(pe, n)
                for t, (lo, hi) in enumerate(tiles):
                    for k in range(K):
                        mm = pe.matmul(work[0:hi - lo, w % 4, t * P:(t + 1) * P], normed[:, k, lo:hi],
                                       slot(n)[:, k * P:(k + 1) * P], start=(k == 0), stop=(k == K - 1))
                mm.then_inc(bank_done[w % 4], 1)

            x_cols = lambda k: normed[:, k, XS]
            all_cols = lambda k: normed[:, k, ALL]

            def even():
                w, n = W0["even"], SLOT0["even"]
                pe.wait_ge(normed_ready, 1)
                for kind, j in EVEN_ITEMS:
                    if kind in ("proj", "gate"):
                        project(w, n, x_cols, S)
                        n += 1
                    elif kind == "rot":
                        pe.wait_ge(*freed(W0["even"] + EVEN_ITEMS.index(("proj", j))))
                        wait_bank(pe, w)
                        pe.matmul(work[:, w % 4, 0:S], cst("rot"), qk1raw[:, j % 2, :], start=True, stop=True).then_inc(bank_done[w % 4], 1)
                    else:
                        values(w, n, [(META, META + P), (META + P, TA)])
                        n += 1
                    w += 1

            def moba():
                w0 = W0["moba"]
                for i, (kind, u) in enumerate(MOBA_ITEMS):
                    w = w0 + i
                    h, t = u // NT, u % NT
                    wait_bank(pe, w)
                    if kind == "score":
                        pe.wait_ge(turned_ready, 16)
                        pe.matmul(work[:, w % 4, 0:P * (t + 1)], qk1[:, h, t * P:(t + 1) * P], qk1[:, HEADS + h, 0:P * (t + 1)],
                                  start=True, stop=True).then_inc(bank_done[w % 4], 1)
                    elif kind == "turn":
                        pe.wait_ge(probs_ready, u + 1)
                        for b in range(t + 1):
                            mm = pe.transpose(work[:, w % 4, b * P:(b + 1) * P], scores1[:, u % 4, b * P:(b + 1) * P], ident)
                        mm.then_inc(bank_done[w % 4], 1)
                    else:
                        h = u
                        for t in range(NT):
                            pe.wait_ge(*freed(w0 + MOBA_ITEMS.index(("turn", NT * h + t))))
                        pe.wait_ge(*freed(W0["even"] + EVEN_ITEMS.index(("val", h))))
                        pe.matmul(work[:, w % 4, 0:P], val1[:, h, 0, :], prob1[:, h % 2, 0, 0:P], start=True, stop=True)
                        pe.matmul(work[:, w % 4, P:S], val1[:, h, 0, :], prob1[:, h % 2, 0, P:S], start=True, stop=False)
                        pe.matmul(work[:, w % 4, P:S], val1[:, h, 1, :], prob1[:, h % 2, 1, P:S], start=False, stop=True).then_inc(bank_done[w % 4], 1)

            def retention():
                w0 = W0["ret"]
                for i, (kind, h) in enumerate(RET_ITEMS):
                    w = w0 + i
                    wait_bank(pe, w)
                    if kind == "inner":
                        q, k = qk1[:, 2 * HEADS + h, :], qk1[:, 3 * HEADS + h, :]
                        pe.matmul(work[:, w % 4, 0:S], k[:, 0:P], q[:, 0:S], start=True, stop=True)
                        pe.matmul(work[:, w % 4, S:S + P], k[:, P:S], q[:, P:S], start=True, stop=True).then_inc(bank_done[w % 4], 1)
                    elif kind == "outer":
                        pe.wait_ge(inner_ready, h + 1)
                        v = val1[:, HEADS + h, :, :]
                        pe.matmul(work[:, w % 4, 0:P], v[:, 0, :], inner1[:, h % 2, 0:P], start=True, stop=True)
                        pe.matmul(work[:, w % 4, P:S], v[:, 0, :], inner1[:, h % 2, P:S], start=True, stop=False)
                        pe.matmul(work[:, w % 4, P:S], v[:, 1, :], inner1[:, h % 2, S:S + P], start=False, stop=True).then_inc(bank_done[w % 4], 1)
                    else:
                        pe.wait_ge(retsq_ready, h + 1)
                        pe.matmul(work[:, w % 4, 0:S], cst("inv_head"), retsq[:, h, :], start=True, stop=True).then_inc(bank_done[w % 4], 1)

            def linear(name, rhs, width, blocks=K):
                n = SLOT0[name]
                for c in range(K):
                    w = W0[name] + c
                    wait_bank(pe, w)
                    for k in range(blocks):
                        if k % K == 0:
                            wait_slot(pe, n + k // K)
                        s = slot(n + k // K)
                        mm = pe.matmul(work[:, w % 4, 0:width], s[:, (k % K) * P:(k % K + 1) * P], rhs(k), start=(k == 0), stop=(k == blocks - 1))
                    mm.then_inc(bank_done[w % 4], 1)
                    n += -(-blocks // K)

            def peer(l):
                pe.wait_ge(normed_ready, 2 * l + 2)
                for j in range(16):
                    project(W0[f"query{l}"] + j, SLOT0[f"query{l}"] + j, x_cols, S)
                for t in range(NT):
                    for g in range(4):
                        w = W0[f"subkey{l}"] + 4 * t + g
                        n = SLOT0[f"subkey{l}"] + g // 2
                        wait_bank(pe, w)
                        wait_slot(pe, n)
                        for j in range(4):
                            hp = 4 * g + j
                            pe.wait_ge(*freed(W0[f"query{l}"] + hp))
                            mm = pe.matmul(work[:, w % 4, j * P:(j + 1) * P], query[:, hp, t * P:(t + 1) * P],
                                           slot(n)[:, (hp % 8) * P:(hp % 8 + 1) * P], start=True, stop=True)
                        mm.then_inc(bank_done[w % 4], 1)
                for t in range(NT):
                    w = W0[f"turn{l}"] + t
                    wait_bank(pe, w)
                    pe.wait_ge(picks_ready, NT * l + t + 1)
                    for x in range(3):
                        mm = pe.transpose(work[:, w % 4, x * P:(x + 1) * P], chosen[:, t, x, :], ident)
                    mm.then_inc(bank_done[w % 4], 1)
                w0 = W0[f"coef{l}"]
                with pe.Fori(0, S // 16) as i:
                    for j in range(4):
                        w = w0 + j
                        pe.wait_ge(bank_free[w % 4], i + (w // 4))
                        pe.wait_ge(hots_ready, i * 4 + (l * S // 4 + j + 1))
                        for x in range(4):
                            y = 4 * (j % 2) + x
                            mm = pe.matmul(work[:, w % 4, x * P:(x + 1) * P], hots[:, 0, y, :], hots[:, 1, y, :], start=True, stop=True)
                        mm.then_inc(bank_done[w % 4], 1)
                base, w0, c0 = SLOT0[f"expert{l}"], W0[f"expert{l}"], l * CHUNKS

                def up(e, i, q):
                    w, n = w0 + e, base + q
                    pe.wait_ge(bank_free[w % 4], i + w // 4)
                    pe.wait_ge(landed[n % RING], i * 16 + 16 * (n // RING + 1))
                    for k in range(K):
                        mm = pe.matmul(work[:, w % 4, 0:S], slot(n)[:, k * P:(k + 1) * P], normed[:, k, XS], start=(k == 0), stop=(k == K - 1))
                    mm.then_inc(bank_done[w % 4], 1)

                def down(e, i, q, first=False, last=False):
                    n = base + q
                    pe.wait_ge(chunk_ready, i * 4 + (c0 + e + 1))
                    pe.wait_ge(landed[n % RING], i * 16 + 16 * (n // RING + 1))
                    for k in range(K):
                        mm = pe.matmul(acc[:, k // 2, (k % 2) * S:(k % 2 + 1) * S], slot(n)[:, k * P:(k + 1) * P],
                                       weighed[:, e % 4, :], start=(first and k % 2 == 0), stop=last, skip_group_check=True)
                    mm.then_inc(chunk_used, 1)

                up(0, 0, 0)
                up(1, 0, 1)
                down(0, 0, 2, first=True)
                turns = (CHUNKS - 3) // 4
                with pe.Fori(0, turns) as i:
                    for j in range(4):
                        up(2 + j, i, 3 + 2 * j)
                        down(1 + j, i, 4 + 2 * j)
                e = 2 + 4 * turns
                q = 3 + 8 * turns
                while e < CHUNKS:
                    up(e, 0, q)
                    down(e - 1, 0, q + 1)
                    e, q = e + 1, q + 2
                down(CHUNKS - 1, 0, q, last=True)

            def odd():
                pe.wait_ge(normed_ready, 3)
                for i in range(len(ODD_ITEMS)):
                    project(W0["odd"] + i, SLOT0["odd"] + i, x_cols, S)

            def feed_forward(x, n_norm, cols):
                pe.wait_ge(normed_ready, n_norm + 1)
                for i in range(len(FFN_ITEMS)):
                    project(W0[f"ffn{x}"] + i, SLOT0[f"ffn{x}"] + i, lambda k: normed[:, k, cols], cols.stop - cols.start)
                pe.wait_ge(ff_ready, FC * x)
                linear(f"ffn{x}out", lambda k: ff_hid[:, k, cols], cols.stop - cols.start, FC)

            def mix():
                w0, n = W0["mix"], SLOT0["mix"]
                pe.wait_ge(normed_ready, 7)
                pe.wait_ge(const2_in, 16 * 8)
                for i, (kind, j) in enumerate(MIX_ITEMS):
                    w = w0 + i
                    cols = XS if j < 4 or 8 <= j < 12 else ALL
                    width = cols.stop - cols.start
                    if kind == "forget":
                        wait_bank(pe, w)
                        for k in range(K):
                            mm = pe.matmul(work[0:FOXH, w % 4, 0:TA], w_forget[:, k, :], normed[:, k, ALL], start=(k == 0), stop=(k == K - 1))
                        mm.then_inc(bank_done[w % 4], 1)
                    elif kind == "proj":
                        project(w, n, lambda k: normed[:, k, cols], width)
                        n += 1
                    elif kind == "mean":
                        wait_bank(pe, w)
                        pe.wait_ge(qksq_ready, j + 1)
                        pe.matmul(work[:, w % 4, 0:width], cst("inv_half"), qk2sq[:, j % 2, 0:width], start=True, stop=True).then_inc(bank_done[w % 4], 1)
                    elif kind == "val":
                        values(w, n, [(0, P), (P, S), (S, TA)])
                        n += 1
                    else:
                        wait_bank(pe, w)
                        lo, hi = ((0, DX), (DX, DTAB))[j]
                        pe.matmul(work[0:FOXH, w % 4, 0:hi - lo], table[0:NB + 1, :], onehot[0:NB + 1, lo:hi], start=True, stop=True).then_inc(bank_done[w % 4], 1)

            def gates():
                for i in range(2 * K):
                    project(W0["gates"] + i, SLOT0["gates"] + i, x_cols, S)

            def attend(name, n_before):
                w0 = W0[name]
                fox = name == "fox"
                pe.wait_ge(qk2_ready, QK2)
                if fox:
                    pe.wait_ge(forget_ready, 1)
                for i, (kind, u) in enumerate(FOX_ITEMS):
                    w = w0 + i
                    h, t = u // NT, u % NT
                    keys = META + P * (t + 1)
                    half = slice((h % 2) * HD2, (h % 2 + 1) * HD2)
                    wait_bank(pe, w)
                    if kind == "score":
                        q = qk2[half, (0 if fox else 8) + h // 2, t * P:(t + 1) * P]
                        kk = qk2[half, 4 + h // 2 if fox else 12 + h // 4, 0:keys]
                        mm = pe.matmul(work[:, w % 4, 0:keys], q, kk, start=True, stop=not fox)
                        if fox:
                            pe.matmul(work[:, w % 4, 0:keys], forget[0:FOXH, 0, META + t * P:META + (t + 1) * P], pick_head[0:FOXH, h, 0:keys],
                                      start=False, stop=False)
                            mm = pe.matmul(work[:, w % 4, 0:keys], neg_head[0:FOXH, h, :], forget[0:FOXH, 0, 0:keys], start=False, stop=True)
                        mm.then_inc(bank_done[w % 4], 1)
                    elif kind == "turn":
                        pe.wait_ge(probs_ready, n_before + u + 1)
                        for b in range(t + 2):
                            lo, hi = b * P, min((b + 1) * P, keys)
                            mm = pe.transpose(work[0:hi - lo, w % 4, b * P:(b + 1) * P], scores2[:, u % 4, lo:hi], ident)
                        mm.then_inc(bank_done[w % 4], 1)
                    else:
                        h = u
                        half = slice((h % 2) * HD2, (h % 2 + 1) * HD2)
                        for t in range(NT):
                            pe.wait_ge(*freed(w0 + FOX_ITEMS.index(("turn", NT * h + t))))
                        pe.wait_ge(*freed(W0["mix"] + MIX_ITEMS.index(("val", 4))))
                        for t in range(NT):
                            keys = META + P * (t + 1)
                            for b in range(t + 2):
                                rows = min(P, keys - b * P)
                                v = val2[0:rows, h // 2, b, (h % 2) * HD2:(h % 2 + 1) * HD2] if fox else \
                                    val2[0:rows, 4, b, (h // 4) * HD2:(h // 4 + 1) * HD2]
                                mm = pe.matmul(work[half, w % 4, t * P:(t + 1) * P], v, prob2[0:rows, h % 2, b, t, :],
                                               start=(b == 0), stop=(b == t + 1))
                        mm.then_inc(bank_done[w % 4], 1)

            def branch():
                pe.wait_ge(*freed(W0["fox"] + len(FOX_ITEMS) - 1))
                pe.wait_ge(*freed(W0["swa"] + len(FOX_ITEMS) - 1))
                for c in range(K):
                    n = SLOT0["branch"] + c
                    for x in range(2):
                        w = W0["branch"] + 2 * c + x
                        wait_bank(pe, w)
                        wait_slot(pe, n)
                        for k in range(4):
                            mm = pe.matmul(work[:, w % 4, 0:S], slot(n)[:, (4 * x + k) * P:(4 * x + k + 1) * P], att2[:, x, k, :],
                                           start=(k == 0), stop=(k == 3))
                        mm.then_inc(bank_done[w % 4], 1)

            pe.wait_ge(const_in, 64)
            norm(0, XS)
            even()
            moba()
            retention()
            for h in range(HEADS):
                pe.wait_ge(*freed(W0["moba"] + MOBA_ITEMS.index(("mix", h))))
            pe.wait_ge(mixed_ready, HEADS)
            linear("evenout", lambda k: att1[:, k, :], S)
            norm(1, XS)
            peer(0)
            norm(2, XS)
            odd()
            pe.wait_ge(zy_ready, K)
            linear("oddout", lambda k: z2[:, k, :], S)
            norm(3, XS)
            peer(1)
            norm(4, XS)
            norm(5, ALL)
            feed_forward(1, 5, ALL)
            norm(6, ALL)
            mix()
            gates()
            attend("fox", HEADS * NT)
            attend("swa", HEADS * NT + FOXH * NT)
            branch()
            pe.wait_ge(branch_ready, K)
            linear("mixout", lambda k: mix_y[:, k, :], S)
            norm(7, XS)
            feed_forward(2, 7, XS)

        @block.scalar
        def _(act):
            def norm(n, cols):
                w = W0[f"norm{n}"]
                width = cols.stop - cols.start
                act.activation(normed[:, :, cols], stream[:, :, cols], ACT.Square).then_inc(squares_ready, 1)
                act.wait_ge(*done(w))
                act.activation(rstd[:, 0:width], work[:, w % 4, 0:width], ACT.Sqrt, bias=eps_col).then_inc(bank_free[w % 4], 1)

            def empty(w, dst, src, func=ACT.Copy):
                act.wait_ge(*done(w))
                act.activation(dst, src, func).then_inc(bank_free[w % 4], 1)

            def even():
                for i, (kind, j) in enumerate(EVEN_ITEMS):
                    w = W0["even"] + i
                    if kind == "proj":
                        if j >= 2:
                            act.wait_ge(*done(W0["even"] + EVEN_ITEMS.index(("rot", j - 2))))
                            act.wait_ge(turned_ready, j - 1)
                        empty(w, qk1raw[:, j % 2, :], work[:, w % 4, 0:S])
                    elif kind == "val":
                        empty(w, val1[:, j, :, :], work[:, w % 4, 0:S].rearrange("p (t d) -> p t d", t=NT))
                    elif kind == "gate":
                        empty(w, silu1[:, j, :], work[:, w % 4, 0:S], ACT.Silu)

            def softmax(items, w0, name, scores, n_before, width_of, turn_copy):
                for i, (kind, u) in enumerate(items):
                    w = w0 + i
                    if kind == "score":
                        act.wait_ge(scores_ready, n_before + u + 1)
                        row = scores[:, u % 4, 0:width_of(u)]
                        act.activation(row, row, ACT.Exp, bias=small[:, 8 + u % 4:9 + u % 4], accum_out=small[:, 12 + u % 4:13 + u % 4]).then_inc(exp_ready, 1)
                    elif kind == "turn":
                        turn_copy(w, u, i)

            def moba():
                w0 = W0["moba"]

                def turn_copy(w, u, i):
                    h, t = u // NT, u % NT
                    if h >= 2:
                        act.wait_ge(*done(w0 + MOBA_ITEMS.index(("mix", h - 2))))
                    empty(w, prob1[:, h % 2, 0:t + 1, t * P:(t + 1) * P], work[:, w % 4, 0:(t + 1) * P].rearrange("p (b q) -> p b q", q=P))

                softmax(MOBA_ITEMS, w0, "moba", scores1, 0, lambda u: P * (u % NT + 1), turn_copy)

            def retention():
                for i, (kind, h) in enumerate(RET_ITEMS):
                    w = W0["ret"] + i
                    if kind == "outer":
                        empty(w, ret1[:, h, :], work[:, w % 4, 0:S])
                        act.wait_ge(*freed(w))
                        act.activation(retsq[:, h, :], ret1[:, h, :], ACT.Square).then_inc(retsq_ready, 1)
                    elif kind == "mean":
                        act.wait_ge(*done(w))
                        act.activation(retms[:, h, :], work[:, w % 4, 0:S], ACT.Sqrt, bias=eps_col).then_inc(bank_free[w % 4], 1)

            def peer(l):
                for j in range(16):
                    w = W0[f"query{l}"] + j
                    empty(w, query[:, j, :], work[:, w % 4, 0:S])
                for t in range(NT):
                    for g in range(4):
                        w = W0[f"subkey{l}"] + 4 * t + g
                        x = l * 8 + 4 * t + g
                        if 4 * t + g >= 2:
                            act.wait_ge(sub_used, x - 1)
                        empty(w, sub[:, g % 2, :], work[:, w % 4, :])
                    act.wait_ge(gate_diff_ready, NT * l + t + 1)
                    act.activation(chosen[:, t, 2, :], pair[:, t, :], ACT.Exp).then_inc(gate_exp_ready, 1)
                for t in range(NT):
                    w = W0[f"turn{l}"] + t
                    empty(w, picks[:, :, t * P:(t + 1) * P], work[:, w % 4, 0:3 * P].rearrange("p (x q) -> p x q", x=3))
                w0 = W0[f"coef{l}"]
                with act.Fori(0, S // 16) as i:
                    for j in range(4):
                        w = w0 + j
                        act.wait_ge(bank_done[w % 4], i + (w // 4 + 1))
                        act.activation(arena[:, bass.ds(i * (16 * P) + j * 4 * P, 4 * P)], work[:, w % 4, :], ACT.Copy).then_inc(bank_free[w % 4], 1)
                w0, c0 = W0[f"expert{l}"], l * CHUNKS

                def gelu(e, i):
                    w = w0 + e
                    act.wait_ge(bank_done[w % 4], i + (w // 4 + 1))
                    if e >= 4 or l:
                        act.wait_ge(chunk_ready, i * 4 + (c0 + e - 3))
                    act.activation(hidden[:, e % 4, :], work[:, w % 4, 0:S], ACT.Gelu).then_inc(bank_free[w % 4], 1)

                for e in range(4):
                    gelu(e, 0)
                with act.Fori(0, CHUNKS // 4 - 1) as i:
                    for j in range(4):
                        gelu(4 + j, i)

            def odd():
                for i, (kind, c) in enumerate(ODD_ITEMS):
                    if kind == "cgate":
                        w = W0["odd"] + i
                        if c >= 2:
                            act.wait_ge(*freed(W0["odd"] + ODD_ITEMS.index(("value", c - 2))))
                        empty(w, cg[:, c % 2, :], work[:, w % 4, 0:S])

            def feed_forward(x, cols):
                width = cols.stop - cols.start
                for i, (kind, c) in enumerate(FFN_ITEMS):
                    if kind == "ffgate":
                        w = W0[f"ffn{x}"] + i
                        if c >= 2:
                            act.wait_ge(ff_ready, FC * (x - 1) + c - 1)
                        empty(w, ff_silu[:, c % 2, 0:width], work[:, w % 4, 0:width], ACT.Silu)

            def mix():
                w0 = W0["mix"]
                for i, (kind, j) in enumerate(MIX_ITEMS):
                    w = w0 + i
                    cols = XS if j < 4 or 8 <= j < 12 else ALL
                    width = cols.stop - cols.start
                    if kind == "forget":
                        act.wait_ge(forget_in, 1)
                        act.activation(forget[0:FOXH, 2, :], forget[0:FOXH, 1, :], ACT.Abs).then_inc(own.sem, own.up())
                        act.wait_ge(own.sem, own.n)
                        act.activation(forget[0:FOXH, 3, :], forget[0:FOXH, 2, :], ACT.Exp, scale=-1.0).then_inc(own.sem, own.up())
                        act.wait_ge(own.sem, own.n)
                        act.activation(forget[0:FOXH, 4, :], forget[0:FOXH, 3, :], ACT.Ln, bias=1.0).then_inc(forget_out, 1)
                    elif kind == "proj":
                        if j >= 2:
                            act.wait_ge(qk2_ready, j - 1)
                        empty(w, qk2raw[:, j % 2, 0:width], work[:, w % 4, 0:width])
                        act.wait_ge(*freed(w))
                        if j >= 2:
                            act.wait_ge(*done(w0 + MIX_ITEMS.index(("mean", j - 2))))
                        act.activation(qk2sq[:, j % 2, 0:width], qk2raw[:, j % 2, 0:width], ACT.Square).then_inc(qksq_ready, 1)
                    elif kind == "mean":
                        act.wait_ge(*done(w))
                        act.activation(qk2ms[:, j % 2, 0:width], work[:, w % 4, 0:width], ACT.Sqrt, bias=eps_col).then_inc(bank_free[w % 4], 1)
                    elif kind == "val":
                        act.wait_ge(*done(w))
                        act.activation(val2[:, j, 0:2, :], work[:, w % 4, 0:S].rearrange("p (t d) -> p t d", t=2), ACT.Copy)
                        act.activation(val2[0:META, j, 2, :], work[0:META, w % 4, S:S + P], ACT.Copy).then_inc(bank_free[w % 4], 1)

            def gates():
                for i in range(2 * K):
                    w = W0["gates"] + i
                    empty(w, gate2[:, i, :], work[:, w % 4, 0:S], ACT.Sigmoid)

            def attend(name, n_before):
                w0 = W0[name]
                fox = name == "fox"

                def turn_copy(w, u, i):
                    h, t = u // NT, u % NT
                    if h >= 2:
                        act.wait_ge(*done(w0 + FOX_ITEMS.index(("mix", h - 2))))
                    act.wait_ge(*done(w))
                    act.activation(prob2[:, h % 2, 0:t + 1, t, :], work[:, w % 4, 0:(t + 1) * P].rearrange("p (b q) -> p b q", q=P), ACT.Copy)
                    act.activation(prob2[0:META, h % 2, t + 1, t, :], work[0:META, w % 4, (t + 1) * P:(t + 2) * P], ACT.Copy).then_inc(bank_free[w % 4], 1)

                softmax(FOX_ITEMS, w0, name, scores2, n_before, lambda u: META + P * (u % NT + 1) + (0 if fox else 1), turn_copy)

            act.wait_ge(const_in, 64)
            act.wait_ge(memset_done, 1)
            norm(0, XS)
            even()
            moba()
            retention()
            act.wait_ge(stream_ready, 1)
            norm(1, XS)
            peer(0)
            act.wait_ge(stream_ready, 2)
            norm(2, XS)
            odd()
            act.wait_ge(stream_ready, 3)
            norm(3, XS)
            peer(1)
            act.wait_ge(stream_ready, 4)
            norm(4, XS)
            act.wait_ge(normed_ready, 5)
            norm(5, ALL)
            feed_forward(1, ALL)
            act.wait_ge(stream_ready, 5)
            norm(6, ALL)
            mix()
            gates()
            attend("fox", HEADS * NT)
            attend("swa", HEADS * NT + FOXH * NT)
            act.wait_ge(stream_ready, 6)
            norm(7, XS)
            feed_forward(2, XS)

        @block.vector
        def _(dve):
            def step():
                dve.wait_ge(vec.sem, vec.n)

            def norm(n, cols, dst=normed):
                w = W0[f"norm{n}"]
                width = cols.stop - cols.start
                dve.wait_ge(*freed(w))
                dve.reciprocal(rstd[:, 0:width], rstd[:, 0:width]).then_inc(vec.sem, vec.up())
                step()
                for k in range(K):
                    ins = dve.scalar_tensor_tensor(dst[:, k, cols], stream[:, k, cols], gains[:, n, k:k + 1], rstd[:, 0:width], ALU.mult, ALU.mult)
                ins.then_inc(normed_ready, 1)

            def even():
                dve.wait_ge(const_in, 64)
                for i, (kind, j) in enumerate(EVEN_ITEMS):
                    w = W0["even"] + i
                    if kind == "rot":
                        dve.wait_ge(*freed(W0["even"] + EVEN_ITEMS.index(("proj", j))))
                        if j >= 2:
                            dve.wait_ge(turned_ready, j - 1)
                        dve.tensor_tensor(qk1[:, j, :], qk1raw[:, j % 2, :], cos, ALU.mult).then_inc(vec.sem, vec.up())
                        dve.wait_ge(*done(w))
                        dve.tensor_tensor(rot_tmp[:, j % 2, :], work[:, w % 4, 0:S], sin, ALU.mult).then_inc(bank_free[w % 4], 1)
                        step()
                        dve.wait_ge(*freed(w))
                        dve.tensor_tensor(qk1[:, j, :], qk1[:, j, :], rot_tmp[:, j % 2, :], ALU.add).then_inc(turned_ready, 1)

            def soft_rows(items, name, scores, n_before, addend, scale, width_of, sink, out):
                w0 = W0[name]
                for i, (kind, u) in enumerate(items):
                    w = w0 + i
                    n = width_of(u)
                    row = scores[:, u % 4, 0:n]
                    if kind == "score":
                        if u >= 4:
                            dve.wait_ge(*done(w0 + items.index(("turn", u - 4))))
                        dve.wait_ge(*done(w))
                        dve.scalar_tensor_tensor(row, work[:, w % 4, 0:n], scale, addend(u), ALU.mult, ALU.add).then_inc(bank_free[w % 4], 1)
                        if sink:
                            h = u // NT
                            dve.tensor_copy(scores[:, u % 4, n:n + 1], sinks[:, h:h + 1]).then_inc(vec.sem, vec.up())
                            step()
                            row = scores[:, u % 4, 0:n + 1]
                        dve.wait_ge(*freed(w))
                        if n_before + u >= 4:
                            dve.wait_ge(exp_ready, n_before + u - 3)
                        dve.tensor_reduce(small[:, 8 + u % 4:9 + u % 4], row, AX.X, ALU.max, negate=True).then_inc(scores_ready, 1)
                    elif kind == "turn":
                        dve.wait_ge(exp_ready, n_before + u + 1)
                        total = small[:, 12 + u % 4:13 + u % 4]
                        dve.reciprocal(total, total).then_inc(vec.sem, vec.up())
                        step()
                        dve.tensor_scalar(row, row, total, None, ALU.mult).then_inc(probs_ready, 1)
                    else:
                        dve.wait_ge(*done(w))
                        out(w, u)

            def moba():
                def out(w, h):
                    dve.tensor_copy(att1[:, h, :], work[:, w % 4, 0:S]).then_inc(bank_free[w % 4], 1)

                soft_rows(MOBA_ITEMS, "moba", scores1, 0, lambda u: cst("causal")[:, (1 - u % NT) * P:S], P ** -0.5,
                          lambda u: P * (u % NT + 1), False, out)

            def retention():
                for i, (kind, h) in enumerate(RET_ITEMS):
                    w = W0["ret"] + i
                    if kind == "inner":
                        dve.wait_ge(*done(w))
                        if h >= 2:
                            dve.wait_ge(*done(W0["ret"] + RET_ITEMS.index(("outer", h - 2))))
                        dve.tensor_tensor(inner1[:, h % 2, :], work[:, w % 4, 0:384], decay[:, h, :], ALU.mult).then_inc(vec.sem, vec.up())
                        step()
                        dve.engine_nop().then_inc(bank_free[w % 4], 1)
                        dve.engine_nop().then_inc(inner_ready, 1)
                    elif kind == "mean":
                        dve.wait_ge(*freed(w))
                        dve.reciprocal(retms[:, h, :], retms[:, h, :]).then_inc(vec.sem, vec.up())
                        step()
                        dve.tensor_tensor(ret1[:, h, :], ret1[:, h, :], retms[:, h, :], ALU.mult).then_inc(vec.sem, vec.up())
                        step()
                        dve.tensor_tensor(att1[:, HEADS + h, :], ret1[:, h, :], silu1[:, h, :], ALU.mult).then_inc(mixed_ready, 1)

            def residual(name, n, cols, scale=1.0):
                width = cols.stop - cols.start
                for c in range(K):
                    w = W0[name] + c
                    dve.wait_ge(*done(w))
                    dve.scalar_tensor_tensor(stream[:, c, cols], work[:, w % 4, 0:width], scale, stream[:, c, cols], ALU.mult, ALU.add).then_inc(bank_free[w % 4], 1)
                for c in range(K - 4, K):
                    dve.wait_ge(*freed(W0[name] + c))
                dve.engine_nop().then_inc(stream_ready, 1)

            def top16(dst, at, src, tmp, n):
                for r in range(n):
                    ins = dve.max(dst(r)[:, 0:8], src(r))
                ins.then_inc(vec.sem, vec.up())
                step()
                for r in range(n):
                    dve.max_index(at(r)[:, 0:8], dst(r)[:, 0:8], src(r))
                    ins = dve.match_replace(tmp(r), dst(r)[:, 0:8], src(r), -3.0e38)
                ins.then_inc(vec.sem, vec.up())
                step()
                for r in range(n):
                    ins = dve.max(dst(r)[:, 8:16], tmp(r))
                ins.then_inc(vec.sem, vec.up())
                step()
                for r in range(n):
                    ins = dve.max_index(at(r)[:, 8:16], dst(r)[:, 8:16], tmp(r))
                return ins

            def choose(l):
                u32 = lambda v: v.bitcast(U32)
                for t in range(NT):
                    for g in range(4):
                        w = W0[f"subkey{l}"] + 4 * t + g
                        dve.wait_ge(*freed(w))
                        top16(lambda r: best[:, t, 4 * g + r, :], lambda r: u32(best_at[:, t, 4 * g + r, :]),
                              lambda r: sub[:, g % 2, r * P:(r + 1) * P], lambda r: sub2[:, r * P:(r + 1) * P], 4).then_inc(sub_used, 1)
                    dve.wait_ge(sub_used, 8 * l + 4 * t + 4)
                    dve.tensor_copy(best_f[:, t, :, :], u32(best_at[:, t, :, :])).then_inc(vec.sem, vec.up())
                    hp = best[:, t, :, :].rearrange("p (h x) k -> p h x k", x=2)
                    c4 = cand[:, :, :].rearrange("p h (i j) -> p h i j", j=TOPK)
                    shape = [P, PH, TOPK, TOPK]
                    dve.tensor_tensor(c4, hp[:, :, 0, :].unsqueeze(3).to_broadcast(shape), hp[:, :, 1, :].unsqueeze(2).to_broadcast(shape),
                                      ALU.add).then_inc(vec.sem, vec.up())
                    step()
                    top = pair[:, t, :].rearrange("p (h k) -> p h k", k=TOPK)
                    at = pair_at.rearrange("p (h k) -> p h k", k=TOPK)
                    top16(lambda r: top[:, r, :], lambda r: u32(at[:, r, :]), lambda r: cand[:, r, :], lambda r: cand2[:, r, :], PH).then_inc(vec.sem, vec.up())
                    step()
                    dve.tensor_copy(psum8[:, t, 1, :], top[:, :, 0]).then_inc(vec.sem, vec.up())
                    step()
                    dve.tensor_tensor(top, top, psum8[:, t, 1, :].unsqueeze(2).to_broadcast([P, PH, TOPK]), ALU.subtract).then_inc(gate_diff_ready, 1)
                    dve.tensor_scalar(u32(pair_ab[:, 0, :]), u32(pair_at), 4, None, ALU.logical_shift_right).then_inc(vec.sem, vec.up())
                    dve.tensor_scalar(u32(pair_ab[:, 1, :]), u32(pair_at), TOPK - 1, None, ALU.bitwise_and).then_inc(vec.sem, vec.up())
                    step()
                    dve.tensor_copy(pair_f[:, :, :], u32(pair_ab[:, :, :])).then_inc(vec.sem, vec.up())
                    step()
                    for x in range(2):
                        ranks = iota[:, 0:TOPK].unsqueeze(1).to_broadcast([P, PH * TOPK, TOPK])
                        dve.tensor_tensor(eq[:, :, :], pair_f[:, x, :].unsqueeze(2).to_broadcast([P, PH * TOPK, TOPK]), ranks, ALU.is_equal).then_inc(vec.sem, vec.up())
                        step()
                        keys = best_f[:, t, :, :].rearrange("p (h x) k -> p h x k", x=2)[:, :, x, :]
                        dve.tensor_tensor(ev[:, :, :].rearrange("p (h k) r -> p h k r", k=TOPK), eq[:, :, :].rearrange("p (h k) r -> p h k r", k=TOPK),
                                          keys.unsqueeze(2).to_broadcast(shape), ALU.mult).then_inc(vec.sem, vec.up())
                        step()
                        dve.tensor_reduce(chosen[:, t, x, :], ev[:, :, :], AX.X, ALU.add).then_inc(vec.sem, vec.up())
                        step()
                    gate = chosen[:, t, 2, :].rearrange("p (h k) -> p h k", k=TOPK)
                    dve.wait_ge(gate_exp_ready, NT * l + t + 1)
                    dve.tensor_reduce(psum8[:, t, 0, :], gate, AX.X, ALU.add).then_inc(vec.sem, vec.up())
                    step()
                    dve.reciprocal(psum8[:, t, 0, :], psum8[:, t, 0, :]).then_inc(vec.sem, vec.up())
                    step()
                    dve.tensor_tensor(gate, gate, psum8[:, t, 0, :].unsqueeze(2).to_broadcast([P, PH, TOPK]), ALU.mult).then_inc(picks_ready, 1)

            def peer(l):
                choose(l)
                for t in range(NT):
                    dve.wait_ge(*freed(W0[f"turn{l}"] + t))
                w0 = W0[f"coef{l}"]
                with dve.Fori(0, S // 16) as i:
                    for j in range(4):
                        x = w0 + j - 2
                        dve.wait_ge(bank_done[x % 4], i + (x // 4 + 1))
                        for y in range(4):
                            z, tok = 4 * (j % 2) + y, i * 16 + (4 * j + y)
                            dve.tensor_scalar(hots[:, 0, z, :], iota, picks[:, 1, bass.ds(tok, 1)], None, ALU.is_equal)
                            ins = dve.tensor_scalar(hots[:, 1, z, :], iota, picks[:, 0, bass.ds(tok, 1)], picks[:, 2, bass.ds(tok, 1)], ALU.is_equal, ALU.mult)
                        ins.then_inc(hots_ready, 1)
                w0, c0 = W0[f"expert{l}"], l * CHUNKS
                for b in range(4):
                    dve.wait_ge(*freed(w0 - 4 + b))

                def weigh(e, i):
                    w = w0 + e
                    dve.wait_ge(bank_free[w % 4], i + (w // 4 + 1))
                    if e >= 4 or l:
                        dve.wait_ge(chunk_used, i * 4 + (c0 + e - 3))
                    dve.tensor_tensor(weighed[:, e % 4, :], hidden[:, e % 4, :], coef[:, :, bass.ds(i * 4 + e, 1)].squeeze(2) if not isinstance(i, int) else coef[:, :, e],
                                      ALU.mult).then_inc(chunk_ready, 1)

                for e in range(4):
                    weigh(e, 0)
                with dve.Fori(0, CHUNKS // 4 - 1) as i:
                    for j in range(4):
                        weigh(4 + j, i)
                dve.wait_ge(chunk_used, c0 + CHUNKS)
                for k in range(K):
                    ins = dve.tensor_tensor(stream[:, k, XS], stream[:, k, XS], acc[:, k // 2, (k % 2) * S:(k % 2 + 1) * S], ALU.add)
                ins.then_inc(stream_ready, 1)

            def odd():
                for b in range(2):
                    ins = dve.memset(u_pad[:, b, 0:2], 0.0)
                ins.then_inc(vec.sem, vec.up())
                for i, (kind, c) in enumerate(ODD_ITEMS):
                    w = W0["odd"] + i
                    b = c % 2
                    if kind == "value":
                        dve.wait_ge(*freed(w - 1))
                        dve.wait_ge(*done(w))
                        if c >= 2:
                            dve.wait_ge(zy_ready, c - 1)
                        dve.tensor_tensor(u_pad[:, b, 2:S + 2], work[:, w % 4, 0:S], cg[:, b, :], ALU.mult).then_inc(bank_free[w % 4], 1)
                        step()
                        dve.wait_ge(*freed(w))
                        dve.tensor_scalar(y_tmp[:, b, 0, :], u_pad[:, b, 0:S], conv[:, 0, c:c + 1], None, ALU.mult).then_inc(vec.sem, vec.up())
                        step()
                        dve.scalar_tensor_tensor(y_tmp[:, b, 1, :], u_pad[:, b, 1:S + 1], conv[:, 1, c:c + 1], y_tmp[:, b, 0, :], ALU.mult, ALU.add).then_inc(vec.sem, vec.up())
                        step()
                        dve.scalar_tensor_tensor(y_tmp[:, b, 0, :], u_pad[:, b, 2:S + 2], conv[:, 2, c:c + 1], y_tmp[:, b, 1, :], ALU.mult, ALU.add).then_inc(vec.sem, vec.up())
                        step()
                    elif kind == "bgate":
                        dve.wait_ge(*done(w))
                        dve.tensor_tensor(z2[:, c, :], work[:, w % 4, 0:S], y_tmp[:, b, 0, :], ALU.mult).then_inc(bank_free[w % 4], 1)
                        dve.wait_ge(*freed(w))
                        dve.engine_nop().then_inc(zy_ready, 1)

            def feed_forward(x, cols):
                width = cols.stop - cols.start
                for i, (kind, c) in enumerate(FFN_ITEMS):
                    if kind == "ffup":
                        w = W0[f"ffn{x}"] + i
                        dve.wait_ge(*freed(w - 1))
                        dve.wait_ge(*done(w))
                        dve.tensor_tensor(ff_hid[:, c, cols], work[:, w % 4, 0:width], ff_silu[:, c % 2, 0:width], ALU.mult).then_inc(bank_free[w % 4], 1)
                        dve.wait_ge(*freed(w))
                        dve.engine_nop().then_inc(ff_ready, 1)

            def mix():
                w0 = W0["mix"]
                dve.wait_ge(const2_in, 16 * 8)
                for i, (kind, j) in enumerate(MIX_ITEMS):
                    w = w0 + i
                    cols = XS if j < 4 or 8 <= j < 12 else ALL
                    width = cols.stop - cols.start
                    if kind == "forget":
                        dve.wait_ge(*done(w))
                        dve.tensor_scalar(forget[0:FOXH, 1, :], work[0:FOXH, w % 4, 0:TA], small[0:FOXH, 4:5], None, ALU.add).then_inc(bank_free[w % 4], 1)
                        dve.wait_ge(*freed(w))
                        dve.engine_nop().then_inc(forget_in, 1)
                        dve.tensor_scalar(forget[0:FOXH, 5, :], forget[0:FOXH, 1, :], 0.0, None, ALU.min).then_inc(vec.sem, vec.up())
                        step()
                        dve.wait_ge(forget_out, 1)
                        dve.tensor_tensor(forget[0:FOXH, 6, :], forget[0:FOXH, 5, :], forget[0:FOXH, 4, :], ALU.subtract).then_inc(vec.sem, vec.up())
                        step()
                        dve.tensor_tensor_scan(forget[0:FOXH, 0, :], forget[0:FOXH, 6, :], forget[0:FOXH, 7, :], 0.0, ALU.add, ALU.add).then_inc(forget_ready, 1)
                    elif kind == "mean":
                        dve.wait_ge(*freed(w))
                        ms = qk2ms[:, j % 2, 0:width]
                        dve.reciprocal(ms, ms).then_inc(vec.sem, vec.up())
                        step()
                        dve.scalar_tensor_tensor(qk2[:, j, 0:width], qk2raw[:, j % 2, 0:width], cst("headgain")[:, j:j + 1], ms, ALU.mult, ALU.mult).then_inc(qk2_ready, 1)
                    elif kind == "table":
                        lo, hi = ((0, DX), (DX, DTAB))[j]
                        dve.wait_ge(*done(w))
                        dve.tensor_copy(table_out[0:FOXH, lo:hi], work[0:FOXH, w % 4, 0:hi - lo]).then_inc(bank_free[w % 4], 1)
                        dve.wait_ge(*freed(w))
                        dve.engine_nop().then_inc(table_ready, 1)

            def attend(name, n_before):
                fox = name == "fox"
                if not fox:
                    dve.wait_ge(bias_in, 64)

                def out(w, h):
                    half = slice((h % 2) * HD2, (h % 2 + 1) * HD2)
                    dve.tensor_copy(att2[half, 0 if fox else 1, h // 2, :], work[half, w % 4, 0:S]).then_inc(bank_free[w % 4], 1)

                def addend(u):
                    h, t = u // NT, u % NT
                    n = META + P * (t + 1)
                    return mask2[:, t, 0:n] if fox else bias2[:, t, h, 0:n]

                soft_rows(FOX_ITEMS, name, scores2, n_before, addend, HD2 ** -0.5, lambda u: META + P * (u % NT + 1), not fox, out)

            def branch():
                for c in range(K):
                    w = W0["branch"] + 2 * c
                    b = c % 2
                    dve.wait_ge(*freed(W0["gates"] + 2 * K - 1))
                    for x in range(2):
                        dve.wait_ge(*done(w + x))
                        dve.tensor_tensor(mix_t[:, b, x, :], work[:, (w + x) % 4, 0:S], gate2[:, x * K + c, :], ALU.mult).then_inc(bank_free[(w + x) % 4], 1)
                    for x in range(2):
                        dve.wait_ge(*freed(w + x))
                    dve.tensor_tensor(mix_y[:, c, :], mix_t[:, b, 0, :], mix_t[:, b, 1, :], ALU.add).then_inc(branch_ready, 1)

            dve.wait_ge(const_in, 64)
            norm(0, XS)
            even()
            moba()
            retention()
            residual("evenout", 1, XS)
            norm(1, XS)
            peer(0)
            norm(2, XS)
            odd()
            residual("oddout", 3, XS)
            norm(3, XS)
            peer(1)
            norm(4, XS, stream)
            norm(5, ALL)
            feed_forward(1, ALL)
            residual("ffn1out", 5, ALL, 0.5)
            norm(6, ALL)
            mix()
            attend("fox", HEADS * NT)
            attend("swa", HEADS * NT + FOXH * NT)
            branch()
            residual("mixout", 6, XS)
            norm(7, XS)
            feed_forward(2, XS)
            residual("ffn2out", 7, XS, 0.5)


def fixed_arrays():
    f = np.float32
    c = {"ident": np.eye(P, dtype=f), "inv_d": np.full((P, P), 1.0 / D, f), "inv_head": np.full((P, P), 1.0 / P, f)}
    rot = np.zeros((P, P), f)
    half = P // 2
    rot[np.arange(half) + half, np.arange(half)] = -1.0
    rot[np.arange(half), np.arange(half) + half] = 1.0
    c["rot"] = rot
    c["inv_half"] = np.kron(np.eye(2), np.full((HD2, HD2), 1.0 / HD2)).astype(f)
    c["iota"] = np.tile(np.arange(P, dtype=f), (P, 1))
    inv = f(10000.0) ** (-np.arange(half, dtype=f) / f(half))
    ang = (np.arange(S, dtype=f)[:, None] * inv[None, :]).astype(f)
    c["cos"] = np.tile(np.cos(ang).astype(f).T, (2, 1))
    c["sin"] = np.tile(np.sin(ang).astype(f).T, (2, 1))
    log_g = np.log(1.0 - 2.0 ** (-5.0 - np.arange(HEADS)))
    diff = np.arange(S)[None, :] - np.arange(P)[:, None]
    dec = np.where(diff >= 0, np.exp(log_g[:, None, None] * np.maximum(diff, 0)), 0.0) * P ** -0.5
    c["decay"] = np.concatenate([dec, dec[:, :, :P]], axis=2).transpose(1, 0, 2).reshape(P, -1).astype(f)
    q, k = np.arange(P)[:, None], np.arange(P)[None, :]
    c["causal"] = np.concatenate([np.zeros((P, P)), np.where(k <= q, 0.0, NEG)], axis=1).astype(f)
    cols = np.arange(TA)
    late = {"foxmask": np.stack([np.where(cols[None, :] <= META + P * t + q, 0.0, NEG) for t in range(NT)], axis=1).astype(f)}
    eye = np.eye(FOXH)
    late["pick_head"] = np.repeat(HD2 ** 0.5 * eye[:, :, None], TA, axis=2).astype(f)
    late["neg_head"] = np.repeat(-HD2 ** 0.5 * eye[:, :, None], P, axis=2).astype(f)

    def bucket(d):
        exact = NB // 2
        large = exact + (np.log(np.maximum(d, 1).astype(f) / f(exact)) / f(np.log(P / exact)) * (NB - exact)).astype(np.int32)
        return np.where(d < exact, d, np.minimum(large, NB - 1))

    r = np.arange(DX) - 255
    x = np.where((r <= 0) & (r > -P), bucket(np.maximum(-r, 0)), NB)
    m = bucket(np.maximum(META - (np.arange(DM) - 255), 0))
    onehot = np.zeros((NB + 1, DTAB), f)
    onehot[np.concatenate([x, m]), np.arange(DTAB)] = 1.0
    late["onehot"] = onehot
    return c, late


def kernel(**inputs):
    import concourse.bacc as bacc
    from concourse.bass_utils import run_bass_kernel_spmd

    x = {k: np.asarray(v) for k, v in inputs.items()}

    def blocks(w):
        n = w.shape[1] // P
        return w.reshape(-1, P, n, P).transpose(2, 1, 0, 3).reshape(n, P, -1)

    def cols(v):
        return v.reshape(-1, P).T

    const, late = fixed_arrays()
    gains = [x["norm_mix"][0], x["norm_ffn"][0], x["norm_mix"][1], x["norm_ffn"][1], x["final_norm"],
             x["ffn1_norm_2"][0], x["mix_norm_2"][0], x["ffn2_norm_2"][0]]
    const["gains"] = np.concatenate([cols(g) for g in gains], axis=1)
    const["conv"] = np.concatenate([cols(w) for w in x["odd_conv"][0]], axis=1)
    twice = lambda g: np.tile(g, 2)[:, None]
    const["headgain"] = np.concatenate([twice(x["fox_q_norm_2"][0])] * 4 + [twice(x["fox_k_norm_2"][0])] * 4
                                       + [twice(x["swa_q_norm_2"][0])] * 4 + [twice(x["swa_k_norm_2"][0])] * 2, axis=1)
    arrays = {"const": np.concatenate([const[name] for name in CONST], axis=1),
              "early": np.concatenate([const[name] for name, _ in EARLY], axis=1)}
    arrays.update(late)
    arrays["x"] = x["x"][0].T.reshape(K, P, S).transpose(1, 0, 2)
    arrays["meta"] = x["meta_tokens_2"].T.reshape(K, P, META).transpose(1, 0, 2)
    w = blocks(x["even_w_in"][0])
    arrays["even_in"] = w[list(range(8)) + list(range(12, 20)) + list(range(8, 12)) + list(range(20, 28))]
    arrays["even_out"] = blocks(x["even_w_out"][0])
    w = blocks(x["odd_w_in"][0])
    arrays["odd_in"] = w[[j for c in range(K) for j in (K + c, 2 * K + c, c)]]
    arrays["odd_out"] = blocks(x["odd_w_out"][0])
    for l in range(2):
        arrays[f"query{l}"] = blocks(x["peer_w_q"][l])
        arrays[f"subkey{l}"] = x["peer_sub_keys"][l].reshape(2, 8, NKEYS, P).transpose(0, 3, 1, 2).reshape(2, P, D)
        arrays[f"u{l}"] = x["peer_u"][l].reshape(CHUNKS, P, K, P).transpose(0, 3, 2, 1).reshape(CHUNKS, P, D)
        arrays[f"v{l}"] = x["peer_v"][l].reshape(CHUNKS, P, D)
    for n in (1, 2):
        w = blocks(x[f"ffn{n}_w_in_2"][0])
        arrays[f"ffn{n}_in"] = w[[j for c in range(FC) for j in (c, FC + c)]]
        arrays[f"ffn{n}_out"] = blocks(x[f"ffn{n}_w_out_2"][0])
    w = x["w_in_2"][0]
    qa, ka, va, fa, qb, kb, vb, ga, gb = np.split(w, np.cumsum([512, 512, 512, FOXH, 512, 128, 128, D]), axis=1)
    arrays["mix_in"] = blocks(np.concatenate([qa, ka, qb, kb[:, :HD2], kb[:, :HD2], kb[:, HD2:], kb[:, HD2:], va, vb], axis=1))
    arrays["gate_in"] = blocks(np.concatenate([ga, gb], axis=1))
    arrays["w_forget"] = fa.reshape(K, P, FOXH).transpose(1, 0, 2)
    arrays["forget_bias"] = x["forget_bias_2"][0][:, None]
    arrays["table"] = x["rel_bias_table_2"]
    arrays["sinks"] = x["swa_sinks_2"][0]
    arrays["branch"] = blocks(np.concatenate([x["w_branch_fox_2"][0], x["w_branch_swa_2"][0]], axis=0))
    arrays["mix_out"] = blocks(x["w_out_2"][0])

    nc = bacc.Bacc("TRN2", target_bir_lowering=False, num_devices=1)
    aps, maps = {}, {}
    for name, v in arrays.items():
        v = np.ascontiguousarray(v)
        maps["in_" + name] = v
        aps[name] = nc.dram_tensor("in_" + name, list(v.shape), mybir.dt.from_np(v.dtype), kind="ExternalInput").ap()
    aps["scratch"] = nc.dram_tensor("bias_by_distance", [P, FOXH, DTAB], F32, kind="Internal").ap()
    aps["out"] = nc.dram_tensor("out", [P, K, S], F32, kind="ExternalOutput").ap()
    build(nc, aps)
    r = run_bass_kernel_spmd(nc, [maps], core_ids=[0])
    return r.results[0]["out"].transpose(1, 0, 2).reshape(D, S).T[None]
```

```python
from contextlib import ExitStack

import numpy as np

import concourse.bass as bass
from concourse import mybir

ALU = mybir.AluOpType
ACT = mybir.ActivationFunctionType
AX = mybir.AxisListType
F32 = mybir.dt.float32
F32R = mybir.dt.float32r
BF16 = mybir.dt.bfloat16
U32 = mybir.dt.uint32

P = 128
D = 1024
K = D // P
S = 256
META = 16
TA = META + S
XS = slice(META, TA)
ALL = slice(0, TA)
NT = S // P
EPS = 1e-6
NEG = -1e30
HEADS = 4
RING = 4
AHEAD = 2
HELD = 40
HALF = 64
NKEYS = 128
PH = 8
TOPK = 16
CHUNKS = NKEYS
FF = 2816
FC = FF // P
FOXH = 8
HD2 = 64
DX = 384
DM = 272
DTAB = DX + DM
NB = 32

EVEN_ITEMS = [("proj", 0)]
for _j in range(1, 16):
    EVEN_ITEMS += [("proj", _j), ("rot", _j - 1)]
EVEN_ITEMS += [("rot", 15)] + [("val", j) for j in range(4)] + [("gate", j) for j in range(4)]


def attention_items(units, lag=3):
    items = []
    for u in range(units + lag + 1):
        if u < units:
            items.append(("score", u))
        if u > lag and (u - lag) % NT == 0:
            items.append(("mix", (u - lag) // NT - 1))
        if lag <= u < units + lag:
            items.append(("turn", u - lag))
    return items


MOBA_ITEMS = attention_items(HEADS * NT)
RET_ITEMS = [("inner", 0)]
for _j in range(1, HEADS):
    RET_ITEMS += [("inner", _j), ("outer", _j - 1)]
RET_ITEMS += [("outer", HEADS - 1)] + [("mean", j) for j in range(HEADS)]
ODD_ITEMS = [(kind, c) for c in range(K) for kind in ("cgate", "value", "bgate")]
FFN_ITEMS = [(kind, c) for c in range(FC) for kind in ("ffgate", "ffup")]
QK2 = 14
MIX_ITEMS = [("proj", 0), ("forget", 0)]
for _j in range(1, QK2):
    MIX_ITEMS += [("proj", _j), ("mean", _j - 1)]
MIX_ITEMS += [("mean", QK2 - 1), ("val", 0), ("lastval", 0), ("val", 1), ("lastval", 1), ("swaval", 0), ("table", 0), ("table", 1)]
FOX_ITEMS = attention_items(FOXH * NT)
GATE_ITEMS = [("gate", j) for j in range(2 * K)]
BRANCH_ITEMS = [(kind, c) for c in range(K) for kind in ("foxout", "swaout")]

SEGMENTS = [("up", None, 0, 24), ("upcoef", None, 24, 16), ("pair", 0, 40, 40), ("pair", 40, 80, 8),
            ("down", 48, None, 16), ("upcoef", None, 88, 16), ("pair", 64, 104, 16), ("pair", 80, 120, 8),
            ("down", 88, None, 32), ("down", 120, None, 8)]
ITEMS_OF = {"up": 1, "upcoef": 3, "pair": 1, "down": 0}
SLOTS_OF = {"up": 1, "upcoef": 1, "pair": 2, "down": 1}

STAGES = [("norm0", 1), ("even", len(EVEN_ITEMS)), ("ret", len(RET_ITEMS)), ("moba", len(MOBA_ITEMS)),
          ("evenout", K)]
for _l in range(2):
    if _l == 1:
        STAGES += [("norm2", 1), ("odd", len(ODD_ITEMS)), ("oddout", K)]
    STAGES += [(f"norm{2 * _l + 1}", 1), (f"query{_l}", 16), (f"subkey{_l}", 8)]
    for _x, (_kind, _e, _h, _steps) in enumerate(SEGMENTS):
        if _x == 1:
            STAGES += [(f"turn{_l}", 2)]
        STAGES += [(f"expert{_l}.{_x}", _steps * ITEMS_OF[_kind])]
STAGES += [("norm4", 1), ("norm5", 1), ("ffn1", len(FFN_ITEMS)), ("ffn1out", K),
           ("norm6", 1), ("mix", len(MIX_ITEMS)), ("fox", len(FOX_ITEMS)), ("swa", len(FOX_ITEMS)), ("gates", len(GATE_ITEMS)),
           ("branch", len(BRANCH_ITEMS)), ("mixout", K),
           ("norm7", 1), ("ffn2", len(FFN_ITEMS)), ("ffn2out", K)]
W0 = {}
_n = 0
for _name, _count in STAGES:
    W0[_name] = _n
    _n += _count


def plan_slots():
    slots, base = [], {}

    def linear(name, items, kinds, array, first=0):
        base[name] = len(slots)
        n = first
        for i, (kind, _) in enumerate(items):
            if kind in kinds:
                last = i + (kind == "val" and items[i + 1][0] == "lastval")
                for _ in range(2 if kind == "val" else 1):
                    slots.append((array, n, D, ("item", W0[name] + last)))
                    n += 1

    def out(name, array, widths):
        base[name] = len(slots)
        for c in range(K):
            for part, width in enumerate(widths):
                slots.append((array, (c, part), width, ("item", W0[name] + c)))

    linear("even", EVEN_ITEMS, ("proj", "val", "gate"), "even_in")
    out("evenout", "even_out", [D])
    for l in range(2):
        if l == 1:
            linear("odd", ODD_ITEMS, ("cgate", "value", "bgate"), "odd_in")
            out("oddout", "odd_out", [D])
        base[f"query{l}"] = len(slots)
        for j in range(16):
            slots.append((f"query{l}", j, D, ("item", W0[f"query{l}"] + j)))
        base[f"subkey{l}"] = len(slots)
        for j in range(2):
            slots.append((f"subkey{l}", j, D, ("item", W0[f"subkey{l}"] + 4 + 2 * j + 1)))
        for x, (kind, e, h, steps) in enumerate(SEGMENTS):
            base[f"expert{l}.{x}"] = len(slots)
            for k in range(steps):
                if e is not None:
                    slots.append((f"v{l}", e + k, D, ("chunk", l * CHUNKS + e + k)))
                if h is not None:
                    slots.append((f"u{l}", h + k, D, ("item", W0[f"expert{l}.{x}"] + k * ITEMS_OF[kind])))
    ff_out = [D, D, (FC - 16) * P]
    linear("ffn1", FFN_ITEMS, ("ffgate", "ffup"), "ffn1_in")
    out("ffn1out", "ffn1_out", ff_out)
    linear("mix", MIX_ITEMS, ("proj", "val", "swaval"), "mix_in")
    linear("gates", GATE_ITEMS, ("gate",), "gate_in")
    base["branch"] = len(slots)
    for c in range(K):
        slots.append(("branch", c, D, ("item", W0["branch"] + 2 * c + 1)))
    out("mixout", "mix_out", [D])
    linear("ffn2", FFN_ITEMS, ("ffgate", "ffup"), "ffn2_in")
    out("ffn2out", "ffn2_out", ff_out)
    return slots, base


SLOTS, SLOT0 = plan_slots()
PLAIN = ("subkey0", "subkey1")
SPLIT = {}
for _n, _slot in enumerate(SLOTS):
    if _slot[0] not in PLAIN:
        SPLIT[_n] = len(SPLIT)
SPLIT_SLOTS = list(SPLIT)
POOL_SLOTS = []
for _l in range(2):
    POOL_SLOTS += [range(SLOT0[f"expert{_l}.0"], SLOT0[f"expert{_l}.2"]),
                   range(SLOT0[f"expert{_l}.5"] + AHEAD, SLOT0[f"expert{_l}.6"] + AHEAD)]

CONST = {}
_n = 0
for _name, _count in [("ident", P), ("rot", P), ("inv_d", P), ("inv_head", P), ("inv_half", P), ("iota", P),
                      ("causal", S), ("gains", 8 * K),
                      ("conv", 3 * K), ("headgain", QK2)]:
    CONST[_name] = (_n, _n + _count)
    _n += _count
N_CONST = _n
ARENA = (HELD + HALF) * S
EARLY = [("cos", S), ("sin", S), ("decay", HEADS * 384)]


class Tally:

    def __init__(self, sem):
        self.sem, self.n = sem, 0

    def up(self):
        self.n += 1
        return 1


def build(nc, a):
    with ExitStack() as ctx:
        def sb(name, shape, dt=F32):
            return ctx.enter_context(nc.sbuf_tensor(name, shape, dt))

        def sem(name):
            return ctx.enter_context(nc.semaphore(name))

        stream = sb("stream", [P, K, TA])
        normed_parts = [sb(f"normed_{x}", [P, K * TA + P - META], F32R) for x in ("hi", "lo")]
        normed_hi, normed_lo = [x[:, 0:K * TA].rearrange("p (k t) -> p k t", k=K) for x in normed_parts]
        ring = sb("ring", [P, RING, D])
        ring_hi = sb("ring_hi", [P, RING, D], F32R)
        ring_lo = sb("ring_lo", [P, RING, D], F32R)
        const = sb("const", [P, N_CONST])
        rstd = sb("rstd", [P, TA])
        desk = sb("desk", [P, K * TA])
        normed = desk.rearrange("p (k t) -> p k t", k=K)
        hots = desk[:, 0:2 * 4 * (P + 4 * HALF) // 2].bitcast(BF16).rearrange("p (b e t) -> p b e t", b=2, t=4)
        hot_second, hot_first = hots[:, :, 0:P, :], hots[:, :, P:P + HALF, :]
        hot_gated = hots[:, :, P + HALF:, :].rearrange("p b (x e) t -> p b x e t", x=3)
        product = sb("product", [P, 2, S])
        weighed = sb("weighed", [P, 2, 4, S], F32R)
        picks = sb("picks", [P, 5, S], BF16)
        gate_rest = rstd[:, 0:S]
        keys4 = sb("keys4", [P, NKEYS, 4], BF16)
        small = sb("small", [P, 16])
        with nc.sbuf_tensor("arena", [P, ARENA], F32) as arena:
            pass
        arena_parts = sb("arena_parts", [P, ARENA], F32R)
        acc = ctx.enter_context(nc.psum_tensor("acc", [P, 4, 512], F32))
        work = ctx.enter_context(nc.psum_tensor("work", [P, 4, 512], F32))

        def cst(name, rows=P):
            lo, hi = CONST[name]
            return const[0:rows, lo:hi]

        ident, iota = cst("ident"), cst("iota")
        gains = cst("gains").rearrange("p (n k) -> p n k", k=K)
        conv = cst("conv").rearrange("p (w k) -> p w k", k=K)
        eps_col = small[:, 0:1]
        zero_col = small[:, 1:2]

        used = {}

        def view(group, shape, arena=arena):
            n = int(np.prod(shape))
            at = used.get(group, 0)
            used[group] = at + n
            assert used[group] <= ARENA, group
            v = arena[:, at:at + n]
            names = "abcd"[:len(shape)]
            if len(shape) > 1:
                v = v.rearrange(f"p ({' '.join(names)}) -> p {' '.join(names)}",
                                **{x: s for x, s in zip(names[1:], shape[1:])})
            return v

        early = view("even", [2 * S + HEADS * 384])
        cos, sin = early[:, 0:S], early[:, S:2 * S]
        decay = early[:, 2 * S:].rearrange("p (h n) -> p h n", h=HEADS)
        qk1 = view("even", [16, S])
        qk1raw = view("even", [2, S])
        rot_tmp = view("even", [2, S])
        val1 = view("even", [8, NT, P])
        silu1 = view("even", [HEADS, S])
        scores1 = view("even", [4, S])
        prob1 = view("even", [2, NT, S])
        inner1 = view("even", [2, 384])
        ret1 = view("even", [HEADS, S])
        retsq = view("even", [HEADS, S])
        retms = view("even", [HEADS, S])
        cg = view("odd", [2, S])
        u_pad = view("odd", [2, S + 2])
        y_tmp = view("odd", [2, 2, S])
        z2_hi, z2_lo = [view("odd", [K, S], arena_parts) for _ in range(2)]
        used["peer"] = HELD * S
        query = view("peer", [16, S])
        sub = view("peer", [8, 512])
        sub2 = view("peer", [512])
        best = view("peer", [NT, 16, TOPK])
        best_at = view("peer", [16, TOPK])
        best_f = view("peer", [16, TOPK])
        cand = view("peer", [PH, TOPK * TOPK])
        cand2 = view("peer", [PH, TOPK * TOPK])
        eq = cand.rearrange("p h (i r) -> p (h i) r", r=TOPK)
        ev = cand2.rearrange("p h (i r) -> p (h i) r", r=TOPK)
        pair = view("peer", [NT, PH * TOPK])
        pair_at = view("peer", [PH * TOPK])
        pair_ab = view("peer", [2, PH * TOPK])
        pair_f = view("peer", [2, PH * TOPK])
        chosen = view("peer", [NT, 3, PH * TOPK])
        psum8 = view("peer", [NT, 2, PH])
        hidden = arena[:, 0:HELD * S].rearrange("p (h t) -> p h t", t=S)
        coef = arena[:, HELD * S:].rearrange("p (t e) -> p t e", e=HALF)
        ff_hi, ff_lo = [view("ffn", [FC, TA], arena_parts) for _ in range(2)]
        ff_hid = view("ffn", [2, TA])
        ff_silu = view("ffn", [2, TA])
        qk2 = view("mix", [QK2, TA])
        qk2raw = view("mix", [2, TA])
        qk2sq = view("mix", [2, TA])
        qk2ms = view("mix", [2, TA])
        bias2 = view("mix", [NT, FOXH, TA])
        val2 = view("mix", [5, 3, P])
        scores2 = view("mix", [4, TA + 4])
        prob2 = view("mix", [2, 3, 2, P])
        att2_hi, att2_lo = [view("mix", [2, 4, S], arena_parts) for _ in range(2)]
        mask2 = view("mix", [NT, TA])
        forget = view("mix", [8, TA])
        pick_head = view("mix", [FOXH, TA])
        neg_head = view("mix", [FOXH, P])
        table = view("mix", [FOXH])
        onehot = view("mix", [DTAB])
        table_out = view("mix", [DTAB])
        sinks = view("mix", [FOXH])
        w_forget = view("mix", [K, FOXH])
        gate2 = view("after", [2 * K, S])
        mix_y = view("after", [2, S])
        mix_t = view("after", [2, 2, S])

        const_in, const2_in = sem("const_in"), sem("const2_in")
        landed = [sem(f"landed{r}") for r in range(RING)]
        bank_done = [sem(f"bank_done{b}") for b in range(4)]
        bank_free = [sem(f"bank_free{b}") for b in range(4)]
        chunk_ready, chunk_used = sem("chunk_ready"), sem("chunk_used")
        hi_ready, lo_ready = sem("hi_ready"), sem("lo_ready")
        squares_ready, plain_ready, lead_ready = sem("squares_ready"), sem("plain_ready"), sem("lead_ready")
        coef_read, hots_used = sem("coef_read"), sem("hots_used")
        stream_block = sem("stream_block")
        normed_ready, stream_ready = sem("normed_ready"), sem("stream_ready")
        turned_ready = sem("turned_ready")
        scores_ready, exp_ready, probs_ready = sem("scores_ready"), sem("exp_ready"), sem("probs_ready")
        inner_ready = sem("inner_ready")
        retsq_ready, retstd_ready = sem("retsq_ready"), sem("retstd_ready")
        mixed_ready = sem("mixed_ready")
        zy_ready = sem("zy_ready")
        gate_diff_ready, gate_exp_ready, picks_ready = sem("gate_diff_ready"), sem("gate_exp_ready"), sem("picks_ready")
        hots_ready, hots_read = sem("hots_ready"), sem("hots_read")
        ff_ready = sem("ff_ready")
        qksq_ready, qkstd_ready, qk2_ready = sem("qksq_ready"), sem("qkstd_ready"), sem("qk2_ready")
        forget_in, forget_out, forget_ready = sem("forget_in"), sem("forget_out"), sem("forget_ready")
        table_ready, table_stored, bias_in = sem("table_ready"), sem("table_stored"), sem("bias_in")
        branch_ready = sem("branch_ready")
        memset_done = sem("memset_done")
        stored = sem("stored")
        vec = Tally(sem("vec_step"))
        own = Tally(sem("act_step"))

        def done(w):
            return bank_done[w % 4], w // 4 + 1

        def freed(w):
            return bank_free[w % 4], w // 4 + 1

        def wait_bank(pe, w):
            if w >= 4:
                pe.wait_ge(*freed(w - 4))

        def slot(n):
            return ring[:, n % RING, :]

        def wait_slot(pe, n):
            pe.wait_ge(landed[n % RING], 16 * (n // RING + 1))

        def used_by_pe(n, i=0, step=1):
            kind, x = SLOTS[n][3]
            if kind == "item":
                return bank_done[x % 4], i * step + (x // 4 + 1)
            return chunk_used, i * 4 + (x + 1)

        def released(n):
            return (lo_ready, SPLIT[n] + 1) if n in SPLIT else used_by_pe(n)

        def split_hi(act, n, i=0, slots=4, step=1):
            m = SPLIT[n]
            if m >= RING:
                act.wait_ge(*used_by_pe(SPLIT_SLOTS[m - RING], i, step))
            act.wait_ge(landed[n % RING], i * (16 * slots // RING) + 16 * (n // RING + 1))
            width = SLOTS[n][2]
            act.activation(ring_hi[:, m % RING, 0:width], ring[:, n % RING, 0:width], ACT.Copy).then_inc(hi_ready, 1)

        def split_lo(eng, n, i=0, slots=4):
            m = SPLIT[n]
            eng.wait_ge(hi_ready, i * slots + (m + 1))
            width = SLOTS[n][2]
            eng.tensor_tensor(ring_lo[:, m % RING, 0:width], ring[:, n % RING, 0:width], ring_hi[:, m % RING, 0:width].bitcast(F32), ALU.subtract).then_inc(lo_ready, 1)

        def product3(pe, out, n, k, hi, lo, start, stop, **more):
            m = SPLIT[n] % RING
            w_hi, w_lo = ring_hi[:, m, k * P:(k + 1) * P], ring_lo[:, m, k * P:(k + 1) * P]
            pe.matmul(out, w_hi, hi, start=start, stop=False, **more)
            pe.matmul(out, w_hi, lo, start=False, stop=False, **more)
            return pe.matmul(out, w_lo, hi, start=False, stop=stop, **more)

        def source(n):
            array, index, width, _ = SLOTS[n]
            if isinstance(index, tuple):
                c, part = index
                return a[array][c][:, part * D:part * D + width], width
            return a[array][index], width

        block = ctx.enter_context(nc.Block())

        @block.sync
        def _(sp):
            def load(n):
                src, width = source(n)
                if n >= RING:
                    sp.wait_ge(*released(n - RING))
                sp.dma_start(ring[:, n % RING, 0:width], src).then_inc(landed[n % RING], 16)

            def expert_loads(l):
                for x, (kind, e, h, steps) in enumerate(SEGMENTS):
                    base, per = SLOT0[f"expert{l}.{x}"], 4 * SLOTS_OF[kind]
                    for q in range(per):
                        load(base + q)
                    if steps == 4:
                        continue
                    with sp.Fori(0, steps // 4 - 1) as i:
                        for q in range(per, 2 * per):
                            n = base + q
                            array, index, _, _ = SLOTS[n]
                            sp.wait_ge(lo_ready, i * per + (SPLIT[n - RING] + 1))
                            sp.dma_start(ring[:, n % RING, :], a[array][i * 4 + index]).then_inc(landed[n % RING], 16)

            sp.dma_start(stream[:, :, XS], a["x"]).then_inc(const_in, 16)
            sp.dma_start(const[:, :], a["const"]).then_inc(const_in, 16)
            sp.dma_start(early, a["early"]).then_inc(const_in, 16)
            sp.dma_start(stream[:, :, 0:META], a["meta"]).then_inc(const_in, 16)
            n = 0
            for l in range(2):
                while n < SLOT0[f"expert{l}.0"]:
                    load(n)
                    n += 1
                expert_loads(l)
                n += 2 * CHUNKS
            while n < len(SLOTS):
                load(n)
                n += 1
            sp.wait_ge(stream_ready, 7)
            sp.dma_start(a["out"], stream[:, :, XS]).then_inc(stored, 16)
            sp.wait_ge(stored, 16)

        @block.gpsimd
        def _(pool):
            pool.memset(eps_col, EPS)
            pool.memset(zero_col, 0.0).then_inc(memset_done, 1)
            for slots in POOL_SLOTS:
                first, last = slots[0], slots[-1]
                pool.wait_ge(lo_ready, SPLIT[first])
                with pool.Fori(0, len(slots) // RING) as i:
                    for q in range(RING):
                        split_lo(pool, first + q, i)
            pool.wait_ge(stream_ready, 5)
            pool.memset(table[:, :], NEG).then_inc(memset_done, 1)
            pool.memset(forget[:, :, :], 0.0).then_inc(memset_done, 1)
            pool.wait_ge(memset_done, 3)
            for dst, src in [(mask2[:, :, :], a["foxmask"]), (w_forget[:, :, :], a["w_forget"]),
                             (pick_head[0:FOXH, :, :], a["pick_head"]), (neg_head[0:FOXH, :, :], a["neg_head"]),
                             (table[0:NB, :], a["table"]), (onehot[0:NB + 1, :], a["onehot"]),
                             (sinks[:, :], a["sinks"].partition_broadcast(P)),
                             (small[0:FOXH, 4:5], a["forget_bias"])]:
                pool.dma_start(dst, src).then_inc(const2_in, 16)
            pool.wait_ge(table_ready, 2)
            pool.dma_start(a["scratch"].rearrange("q h d -> h q d"),
                           table_out[0:FOXH, :].unsqueeze(1).to_broadcast([FOXH, P, DTAB])).then_inc(table_stored, 16)
            pool.wait_ge(table_stored, 16)
            for t in range(NT):
                n = P * (t + 1)
                for lo, width, first, col in ((META, n, 255 - P * t, 0), (0, META, DX + 255 - P * t, 0)):
                    src = bass.AP(a["scratch"].tensor, first, [[FOXH * DTAB - 1, P], [DTAB, FOXH], [1, width]])
                    pool.dma_start(bias2[:, t, :, lo:lo + width], src).then_inc(bias_in, 16)

        @block.tensor
        def _(pe):
            def norm(n, cols):
                w = W0[f"norm{n}"]
                wait_bank(pe, w)
                width = cols.stop - cols.start
                for k in range(K):
                    pe.wait_ge(squares_ready, K * n + k + 1)
                    mm = pe.matmul(work[:, w % 4, 0:width], cst("inv_d"), normed[:, k, cols], start=(k == 0), stop=(k == K - 1))
                mm.then_inc(bank_done[w % 4], 1)

            def project(w, n, cols, fresh=None):
                width = cols.stop - cols.start
                wait_bank(pe, w)
                pe.wait_ge(lo_ready, SPLIT[n] + 1)
                for k in range(K):
                    if fresh is not None:
                        pe.wait_ge(normed_ready, K * fresh + k + 1)
                    mm = product3(pe, work[:, w % 4, 0:width], n, k, normed_hi[:, k, cols], normed_lo[:, k, cols], k == 0, k == K - 1)
                mm.then_inc(bank_done[w % 4], 1)

            def values(w, n, slots, tiles):
                wait_bank(pe, w)
                pe.wait_ge(lo_ready, SPLIT[n] + slots)
                m = SPLIT[n] % RING
                assert m + slots <= RING
                for t, lo in enumerate(tiles):
                    for k in range(K):
                        w_hi, w_lo = [x[:, m:m + slots, k * P:(k + 1) * P] for x in (ring_hi, ring_lo)]
                        out = work[:, w % 4, t * slots * P:(t + 1) * slots * P]
                        x_hi, x_lo = [x[:, k * TA + lo:k * TA + lo + P] for x in normed_parts]
                        pe.matmul(out, x_hi, w_hi, start=(k == 0), stop=False)
                        pe.matmul(out, x_hi, w_lo, start=False, stop=False)
                        mm = pe.matmul(out, x_lo, w_hi, start=False, stop=(k == K - 1))
                mm.then_inc(bank_done[w % 4], 1)

            def even():
                w, n = W0["even"], SLOT0["even"]
                for kind, j in EVEN_ITEMS:
                    if kind in ("proj", "gate"):
                        project(w, n, XS, 0 if w == W0["even"] else None)
                        n += 1
                    elif kind == "rot":
                        pe.wait_ge(*freed(W0["even"] + EVEN_ITEMS.index(("proj", j))))
                        wait_bank(pe, w)
                        pe.matmul(work[:, w % 4, 0:S], cst("rot"), qk1raw[:, j % 2, :], start=True, stop=True).then_inc(bank_done[w % 4], 1)
                    else:
                        values(w, n, 2, [META, META + P])
                        n += 2
                    w += 1

            def moba():
                w0 = W0["moba"]
                for i, (kind, u) in enumerate(MOBA_ITEMS):
                    w = w0 + i
                    h, t = u // NT, u % NT
                    wait_bank(pe, w)
                    if kind == "score":
                        pe.matmul(work[:, w % 4, 0:P * (t + 1)], qk1[:, h, t * P:(t + 1) * P], qk1[:, HEADS + h, 0:P * (t + 1)],
                                  start=True, stop=True).then_inc(bank_done[w % 4], 1)
                    elif kind == "turn":
                        pe.wait_ge(probs_ready, u + 1)
                        for b in range(t + 1):
                            mm = pe.transpose(work[:, w % 4, b * P:(b + 1) * P], scores1[:, u % 4, b * P:(b + 1) * P], ident)
                        mm.then_inc(bank_done[w % 4], 1)
                    else:
                        h = u
                        for t in range(NT):
                            pe.wait_ge(*freed(w0 + MOBA_ITEMS.index(("turn", NT * h + t))))
                        pe.wait_ge(*freed(W0["even"] + EVEN_ITEMS.index(("val", h // 2))))
                        pe.matmul(work[:, w % 4, 0:P], val1[:, h, 0, :], prob1[:, h % 2, 0, 0:P], start=True, stop=True)
                        pe.matmul(work[:, w % 4, P:S], val1[:, h, 0, :], prob1[:, h % 2, 0, P:S], start=True, stop=False)
                        pe.matmul(work[:, w % 4, P:S], val1[:, h, 1, :], prob1[:, h % 2, 1, P:S], start=False, stop=True).then_inc(bank_done[w % 4], 1)

            def retention():
                w0 = W0["ret"]
                pe.wait_ge(turned_ready, 16)
                for i, (kind, h) in enumerate(RET_ITEMS):
                    w = w0 + i
                    wait_bank(pe, w)
                    if kind == "inner":
                        q, k = qk1[:, 2 * HEADS + h, :], qk1[:, 3 * HEADS + h, :]
                        pe.matmul(work[:, w % 4, 0:S], k[:, 0:P], q[:, 0:S], start=True, stop=True)
                        pe.matmul(work[:, w % 4, S:S + P], k[:, P:S], q[:, P:S], start=True, stop=True).then_inc(bank_done[w % 4], 1)
                    elif kind == "outer":
                        pe.wait_ge(inner_ready, h + 1)
                        v = val1[:, HEADS + h, :, :]
                        pe.matmul(work[:, w % 4, 0:P], v[:, 0, :], inner1[:, h % 2, 0:P], start=True, stop=True)
                        pe.matmul(work[:, w % 4, P:S], v[:, 0, :], inner1[:, h % 2, P:S], start=True, stop=False)
                        pe.matmul(work[:, w % 4, P:S], v[:, 1, :], inner1[:, h % 2, S:S + P], start=False, stop=True).then_inc(bank_done[w % 4], 1)
                    else:
                        pe.wait_ge(retsq_ready, h + 1)
                        pe.matmul(work[:, w % 4, 0:S], cst("inv_head"), retsq[:, h, :], start=True, stop=True).then_inc(bank_done[w % 4], 1)

            def linear(name, hi, lo, width, blocks=K):
                n = SLOT0[name]
                for c in range(K):
                    w = W0[name] + c
                    wait_bank(pe, w)
                    for k in range(blocks):
                        if k % K == 0:
                            pe.wait_ge(lo_ready, SPLIT[n + k // K] + 1)
                        mm = product3(pe, work[:, w % 4, 0:width], n + k // K, k % K, hi(k), lo(k), k == 0, k == blocks - 1)
                    mm.then_inc(bank_done[w % 4], 1)
                    n += -(-blocks // K)

            def peer(l):
                for j in range(16):
                    project(W0[f"query{l}"] + j, SLOT0[f"query{l}"] + j, XS, 2 * l + 1 if j == 0 else None)
                for t in range(NT):
                    for g in range(4):
                        w = W0[f"subkey{l}"] + 4 * t + g
                        n = SLOT0[f"subkey{l}"] + g // 2
                        wait_bank(pe, w)
                        wait_slot(pe, n)
                        for j in range(4):
                            hp = 4 * g + j
                            pe.wait_ge(*freed(W0[f"query{l}"] + hp))
                            mm = pe.matmul(work[:, w % 4, j * P:(j + 1) * P], query[:, hp, t * P:(t + 1) * P],
                                           slot(n)[:, (hp % 8) * P:(hp % 8 + 1) * P], start=True, stop=True)
                        mm.then_inc(bank_done[w % 4], 1)

                def up(n, w, i=0, slots=4, step=1, coef_item=None):
                    pe.wait_ge(bank_free[w % 4], i * step + w // 4)
                    pe.wait_ge(lo_ready, i * slots + (SPLIT[n] + 1))
                    for k in range(K):
                        mm = product3(pe, work[:, w % 4, 0:S], n, k, normed_hi[:, k, XS], normed_lo[:, k, XS], k == 0, k == K - 1)
                        if coef_item is not None and k == K // 2 - 1:
                            coefficients(*coef_item, i)
                    mm.then_inc(bank_done[w % 4], 1)

                def down(n, e, i=0, slots=4):
                    pe.wait_ge(chunk_ready, i * 4 + (l * CHUNKS + e + 1))
                    pe.wait_ge(lo_ready, i * slots + (SPLIT[n] + 1))
                    for k in range(K):
                        mm = product3(pe, acc[:, k // 2, (k % 2) * S:(k % 2 + 1) * S], n, k, weighed[:, 0, e % 4, :], weighed[:, 1, e % 4, :],
                                      e == 0 and k % 2 == 0, e == CHUNKS - 1, skip_group_check=True)
                    mm.then_inc(chunk_used, 1)

                def coefficients(w, count, i=0, step=3):
                    pe.wait_ge(bank_free[w % 4], i * step + w // 4)
                    for b in range(2):
                        pe.wait_ge(hots_ready, i * 16 + (2 * count + b + 1))
                        for t in range(4):
                            y = 4 * b + t
                            for x in range(3):
                                mm = pe.matmul(work[:, w % 4, y * HALF:(y + 1) * HALF], hot_second[:, b, :, t], hot_gated[:, b, x, :, t], start=(x == 0), stop=(x == 2))
                        mm.then_inc(*((hots_read, 1) if b == 0 else (bank_done[w % 4], 1)))

                built = l * 2 * S // 8
                for x, (kind, e, h, steps) in enumerate(SEGMENTS):
                    if x == 1:
                        for t in range(NT):
                            w = W0[f"turn{l}"] + t
                            wait_bank(pe, w)
                            pe.wait_ge(picks_ready, NT * l + t + 1)
                            for y in range(3):
                                mm = pe.transpose(work[:, w % 4, y * P:(y + 1) * P], chosen[:, t, y, :], ident)
                            mm.then_inc(bank_done[w % 4], 1)
                    w0, base, per, step = W0[f"expert{l}.{x}"], SLOT0[f"expert{l}.{x}"], 4 * SLOTS_OF[kind], ITEMS_OF[kind]

                    def four(at, i):
                        for j in range(at, at + 4):
                            n = base + j * SLOTS_OF[kind]
                            if e is not None:
                                down(n, e + j, i, per)
                                n += 1
                            if kind == "upcoef":
                                up(n, w0 + step * j, i, per, step, (w0 + step * j + 1, built + 2 * j))
                                coefficients(w0 + step * j + 2, built + 2 * j + 1, i)
                            elif h is not None:
                                up(n, w0 + step * j, i, per, step)

                    head = 4 if e == 0 else 0
                    tail = 4 if e is not None and e + steps == CHUNKS else 0
                    if head:
                        four(0, 0)
                    if steps - head - tail:
                        with pe.Fori(0, (steps - head - tail) // 4) as i:
                            four(head, i)
                    if tail:
                        four(steps - tail, 0)
                    if kind == "upcoef":
                        built += S // 8

            def odd():
                for i in range(len(ODD_ITEMS)):
                    project(W0["odd"] + i, SLOT0["odd"] + i, XS, 2 if i == 0 else None)

            def feed_forward(x, n_norm, cols):
                for i in range(len(FFN_ITEMS)):
                    project(W0[f"ffn{x}"] + i, SLOT0[f"ffn{x}"] + i, cols, n_norm - 1 if i == 0 else None)
                pe.wait_ge(ff_ready, FC * x)
                linear(f"ffn{x}out", lambda k: ff_hi[:, k, cols], lambda k: ff_lo[:, k, cols], cols.stop - cols.start, FC)

            def mix():
                w0, n = W0["mix"], SLOT0["mix"]
                for i, (kind, j) in enumerate(MIX_ITEMS):
                    w = w0 + i
                    cols = XS if j < 4 or 8 <= j < 12 else ALL
                    width = cols.stop - cols.start
                    if kind == "forget":
                        pe.wait_ge(const2_in, 16 * 8)
                        wait_bank(pe, w)
                        for k in range(K):
                            mm = pe.matmul(work[0:FOXH, w % 4, 0:TA], w_forget[:, k, :], normed[:, k, ALL], start=(k == 0), stop=(k == K - 1))
                        mm.then_inc(bank_done[w % 4], 1)
                    elif kind == "proj":
                        project(w, n, cols, 5 if j == 0 else None)
                        n += 1
                    elif kind == "mean":
                        wait_bank(pe, w)
                        pe.wait_ge(qksq_ready, j + 1)
                        pe.matmul(work[:, w % 4, 0:width], cst("inv_half"), qk2sq[:, j % 2, 0:width], start=True, stop=True).then_inc(bank_done[w % 4], 1)
                    elif kind == "val":
                        values(w, n, 2, [0, P])
                    elif kind == "lastval":
                        values(w, n, 2, [S])
                        n += 2
                    elif kind == "swaval":
                        values(w, n, 1, [0, P, S])
                        n += 1
                    else:
                        wait_bank(pe, w)
                        lo, hi = ((0, DX), (DX, DTAB))[j]
                        pe.matmul(work[0:FOXH, w % 4, 0:hi - lo], table[0:NB + 1, :], onehot[0:NB + 1, lo:hi], start=True, stop=True).then_inc(bank_done[w % 4], 1)

            def gates():
                for i in range(2 * K):
                    project(W0["gates"] + i, SLOT0["gates"] + i, XS)

            def attend(name, n_before):
                w0 = W0[name]
                fox = name == "fox"
                pe.wait_ge(qk2_ready, QK2)
                if fox:
                    pe.wait_ge(forget_ready, 1)
                for i, (kind, u) in enumerate(FOX_ITEMS):
                    w = w0 + i
                    h, t = u // NT, u % NT
                    keys = META + P * (t + 1)
                    half = slice((h % 2) * HD2, (h % 2 + 1) * HD2)
                    wait_bank(pe, w)
                    if kind == "score":
                        q = qk2[half, (0 if fox else 8) + h // 2, t * P:(t + 1) * P]
                        kk = qk2[half, 4 + h // 2 if fox else 12 + h // 4, 0:keys]
                        mm = pe.matmul(work[:, w % 4, 0:keys], q, kk, start=True, stop=not fox)
                        if fox:
                            pe.matmul(work[:, w % 4, 0:keys], forget[0:FOXH, 0, META + t * P:META + (t + 1) * P], pick_head[0:FOXH, h, 0:keys],
                                      start=False, stop=False)
                            mm = pe.matmul(work[:, w % 4, 0:keys], neg_head[0:FOXH, h, :], forget[0:FOXH, 0, 0:keys], start=False, stop=True)
                        mm.then_inc(bank_done[w % 4], 1)
                    elif kind == "turn":
                        pe.wait_ge(probs_ready, n_before + u + 1)
                        for b in range(t + 2):
                            lo, hi = b * P, min((b + 1) * P, keys)
                            mm = pe.transpose(work[0:hi - lo, w % 4, b * P:(b + 1) * P], scores2[:, u % 4, lo:hi], ident)
                        mm.then_inc(bank_done[w % 4], 1)
                    else:
                        h = u
                        half = slice((h % 2) * HD2, (h % 2 + 1) * HD2)
                        for t in range(NT):
                            pe.wait_ge(*freed(w0 + FOX_ITEMS.index(("turn", NT * h + t))))
                        pe.wait_ge(*freed(W0["mix"] + MIX_ITEMS.index(("swaval", 0))))
                        for t in range(NT):
                            keys = META + P * (t + 1)
                            for b in range(t + 2):
                                rows = min(P, keys - b * P)
                                v = val2[0:rows, h // 2, b, (h % 2) * HD2:(h % 2 + 1) * HD2] if fox else \
                                    val2[0:rows, 4, b, (h // 4) * HD2:(h // 4 + 1) * HD2]
                                mm = pe.matmul(work[half, w % 4, t * P:(t + 1) * P], v, prob2[0:rows, h % 2, b, t, :],
                                               start=(b == 0), stop=(b == t + 1))
                        mm.then_inc(bank_done[w % 4], 1)

            def branch():
                pe.wait_ge(*freed(W0["fox"] + len(FOX_ITEMS) - 1))
                pe.wait_ge(*freed(W0["swa"] + len(FOX_ITEMS) - 1))
                for c in range(K):
                    n = SLOT0["branch"] + c
                    for x in range(2):
                        w = W0["branch"] + 2 * c + x
                        wait_bank(pe, w)
                        pe.wait_ge(lo_ready, SPLIT[n] + 1)
                        for k in range(4):
                            mm = product3(pe, work[:, w % 4, 0:S], n, 4 * x + k, att2_hi[:, x, k, :], att2_lo[:, x, k, :], k == 0, k == 3)
                        mm.then_inc(bank_done[w % 4], 1)

            pe.wait_ge(const_in, 64)
            norm(0, XS)
            even()
            retention()
            moba()
            for h in range(HEADS):
                pe.wait_ge(*freed(W0["moba"] + MOBA_ITEMS.index(("mix", h))))
            pe.wait_ge(mixed_ready, HEADS)
            linear("evenout", lambda k: normed_hi[:, k, XS], lambda k: normed_lo[:, k, XS], S)
            norm(1, XS)
            peer(0)
            norm(2, XS)
            odd()
            pe.wait_ge(zy_ready, K)
            linear("oddout", lambda k: z2_hi[:, k, :], lambda k: z2_lo[:, k, :], S)
            norm(3, XS)
            peer(1)
            norm(4, XS)
            norm(5, ALL)
            feed_forward(1, 5, ALL)
            norm(6, ALL)
            mix()
            attend("fox", HEADS * NT)
            attend("swa", HEADS * NT + FOXH * NT)
            gates()
            branch()
            pe.wait_ge(branch_ready, K)
            linear("mixout", lambda k: normed_hi[:, k, XS], lambda k: normed_lo[:, k, XS], S)
            norm(7, XS)
            feed_forward(2, 7, XS)

        @block.scalar
        def _(act):
            ahead = [0]

            def split_to(n):
                while ahead[0] < len(SLOTS) and ahead[0] <= n + AHEAD:
                    if ahead[0] in SPLIT:
                        split_hi(act, ahead[0])
                    ahead[0] += 1

            def norm(n, cols, written):
                w = W0[f"norm{n}"]
                width = cols.stop - cols.start
                for k in range(K):
                    act.wait_ge(*written(k))
                    act.activation(normed[:, k, cols], stream[:, k, cols], ACT.Square).then_inc(squares_ready, 1)
                act.wait_ge(*done(w))
                act.activation(rstd[:, 0:width], work[:, w % 4, 0:width], ACT.Sqrt, bias=eps_col).then_inc(bank_free[w % 4], 1)
                if n != 4:
                    for k in range(K):
                        x = K * (n - (n > 4)) + k + 1
                        act.wait_ge(plain_ready, x)
                        act.activation(normed_hi[:, k, cols], normed[:, k, cols], ACT.Copy).then_inc(lead_ready, 1)

            def split_all(name, widths=1):
                for c in range(K):
                    split_to(SLOT0[name] + (c + 1) * widths - 1)

            def empty(w, dst, src, func=ACT.Copy):
                act.wait_ge(*done(w))
                act.activation(dst, src, func).then_inc(bank_free[w % 4], 1)

            def even():
                n = SLOT0["even"]
                for i, (kind, j) in enumerate(EVEN_ITEMS):
                    w = W0["even"] + i
                    if kind != "rot":
                        n += 2 if kind == "val" else 1
                        split_to(n - 1)
                    if kind == "proj":
                        if j >= 2:
                            act.wait_ge(*done(W0["even"] + EVEN_ITEMS.index(("rot", j - 2))))
                            act.wait_ge(turned_ready, j - 1)
                        empty(w, qk1raw[:, j % 2, :], work[:, w % 4, 0:S])
                    elif kind == "val":
                        empty(w, val1[:, 2 * j:2 * j + 2, :, :].rearrange("p h t d -> p t h d"), work[:, w % 4, :].rearrange("p (t h d) -> p t h d", t=NT, h=2))
                    elif kind == "gate":
                        empty(w, silu1[:, j, :], work[:, w % 4, 0:S], ACT.Silu)

            def softmax(items, w0, name, scores, n_before, width_of, turn_copy):
                for i, (kind, u) in enumerate(items):
                    w = w0 + i
                    if kind == "score":
                        act.wait_ge(scores_ready, n_before + u + 1)
                        row = scores[:, u % 4, 0:width_of(u)]
                        act.activation(row, row, ACT.Exp, bias=small[:, 8 + u % 4:9 + u % 4], accum_out=small[:, 12 + u % 4:13 + u % 4]).then_inc(exp_ready, 1)
                    elif kind == "turn":
                        turn_copy(w, u, i)

            def moba():
                w0 = W0["moba"]

                def turn_copy(w, u, i):
                    h, t = u // NT, u % NT
                    if h >= 2:
                        act.wait_ge(*done(w0 + MOBA_ITEMS.index(("mix", h - 2))))
                    empty(w, prob1[:, h % 2, 0:t + 1, t * P:(t + 1) * P], work[:, w % 4, 0:(t + 1) * P].rearrange("p (b q) -> p b q", q=P))

                softmax(MOBA_ITEMS, w0, "moba", scores1, 0, lambda u: P * (u % NT + 1), turn_copy)

            def retention():
                for i, (kind, h) in enumerate(RET_ITEMS):
                    w = W0["ret"] + i
                    if kind == "outer":
                        empty(w, ret1[:, h, :], work[:, w % 4, 0:S])
                        act.wait_ge(*freed(w))
                        act.activation(retsq[:, h, :], ret1[:, h, :], ACT.Square).then_inc(retsq_ready, 1)
                    elif kind == "mean":
                        act.wait_ge(*done(w))
                        act.activation(retms[:, h, :], work[:, w % 4, 0:S], ACT.Sqrt, bias=eps_col).then_inc(bank_free[w % 4], 1)

            def peer(l):
                for j in range(16):
                    w = W0[f"query{l}"] + j
                    split_to(SLOT0[f"query{l}"] + j)
                    empty(w, query[:, j, :], work[:, w % 4, 0:S])
                for t in range(NT):
                    for g in range(4):
                        w = W0[f"subkey{l}"] + 4 * t + g
                        empty(w, sub[:, 4 * t + g, :], work[:, w % 4, :])
                split_to(SLOT0[f"expert{l}.0"] - 1)

                def gate_exp(t):
                    act.wait_ge(gate_diff_ready, NT * l + t + 1)
                    act.activation(chosen[:, t, 2, :], pair[:, t, :], ACT.Exp).then_inc(gate_exp_ready, 1)

                def gelu(w, h, i=0, step=1):
                    act.wait_ge(bank_done[w % 4], i * step + (w // 4 + 1))
                    if h >= HELD:
                        act.wait_ge(chunk_ready, i * 4 + (l * CHUNKS + h - HELD + 1))
                    else:
                        act.wait_ge(stream_ready, 2 * l + 1)
                    act.activation(hidden[:, bass.ds(i * 4 + h % HELD, 1), :].squeeze(1) if not isinstance(i, int) else hidden[:, h % HELD, :],
                                   work[:, w % 4, 0:S], ACT.Gelu).then_inc(bank_free[w % 4], 1)

                def store_coef(w, at, i=0, step=3):
                    act.wait_ge(bank_done[w % 4], i * step + (w // 4 + 1))
                    act.activation(arena[:, bass.ds(i * (64 * HALF) + (HELD * S + at * HALF), 8 * HALF)], work[:, w % 4, :], ACT.Copy).then_inc(bank_free[w % 4], 1)

                for x, (kind, e, h, steps) in enumerate(SEGMENTS):
                    if x == 1:
                        gate_exp(1)
                        for t in range(NT):
                            w = W0[f"turn{l}"] + t
                            act.wait_ge(*done(w))
                            act.activation(gate_rest[:, t * P:(t + 1) * P], work[:, w % 4, 2 * P:3 * P], ACT.Copy)
                            act.activation(picks[:, 0:2, t * P:(t + 1) * P], work[:, w % 4, 0:2 * P].rearrange("p (x q) -> p x q", x=2), ACT.Copy).then_inc(bank_free[w % 4], 1)
                    w0, base, slots, step = W0[f"expert{l}.{x}"], SLOT0[f"expert{l}.{x}"], SLOTS_OF[kind], ITEMS_OF[kind]
                    if kind == "upcoef" and x > 1:
                        act.wait_ge(chunk_ready, l * CHUNKS + HALF)

                    def four(at, i):
                        for j in range(at, at + 4):
                            for y in range(slots):
                                n = base + j * slots + AHEAD + y
                                if n in SPLIT:
                                    split_hi(act, n, i, 4 * slots, step)
                            if kind == "upcoef":
                                store_coef(w0 + step * j + 1, 16 * j, i)
                            if h is not None:
                                gelu(w0 + step * j, h + j, i, step)
                            if kind == "upcoef":
                                store_coef(w0 + step * j + 2, 16 * j + 8, i)

                    four(0, 0)
                    if x == 0:
                        with act.Fori(0, 3) as i:
                            four(4, i)
                        gate_exp(0)
                        with act.Fori(0, steps // 4 - 4) as i:
                            four(16, i)
                    else:
                        with act.Fori(0, steps // 4 - 1) as i:
                            four(4, i)
                ahead[0] = SLOT0[f"expert{l}.{len(SEGMENTS) - 1}"] + SEGMENTS[-1][3] + AHEAD

            def odd():
                for i, (kind, c) in enumerate(ODD_ITEMS):
                    split_to(SLOT0["odd"] + i)
                    if kind == "cgate":
                        w = W0["odd"] + i
                        if c >= 2:
                            act.wait_ge(*freed(W0["odd"] + ODD_ITEMS.index(("value", c - 2))))
                        empty(w, cg[:, c % 2, :], work[:, w % 4, 0:S])

            def feed_forward(x, cols):
                width = cols.stop - cols.start
                for i, (kind, c) in enumerate(FFN_ITEMS):
                    split_to(SLOT0[f"ffn{x}"] + i)
                    if kind == "ffgate":
                        w = W0[f"ffn{x}"] + i
                        if c >= 2:
                            act.wait_ge(ff_ready, FC * (x - 1) + c - 1)
                        empty(w, ff_silu[:, c % 2, 0:width], work[:, w % 4, 0:width], ACT.Silu)

            def mix():
                w0, n = W0["mix"], SLOT0["mix"]
                for i, (kind, j) in enumerate(MIX_ITEMS):
                    w = w0 + i
                    cols = XS if j < 4 or 8 <= j < 12 else ALL
                    width = cols.stop - cols.start
                    if kind in ("proj", "val", "swaval"):
                        n += 2 if kind == "val" else 1
                        split_to(n - 1)
                    if kind == "forget":
                        act.wait_ge(forget_in, 1)
                        act.activation(forget[0:FOXH, 2, :], forget[0:FOXH, 1, :], ACT.Abs).then_inc(own.sem, own.up())
                        act.wait_ge(own.sem, own.n)
                        act.activation(forget[0:FOXH, 3, :], forget[0:FOXH, 2, :], ACT.Exp, scale=-1.0).then_inc(own.sem, own.up())
                        act.wait_ge(own.sem, own.n)
                        act.activation(forget[0:FOXH, 4, :], forget[0:FOXH, 3, :], ACT.Ln, bias=1.0).then_inc(forget_out, 1)
                    elif kind == "proj":
                        if j >= 2:
                            act.wait_ge(qk2_ready, j - 1)
                        empty(w, qk2raw[:, j % 2, 0:width], work[:, w % 4, 0:width])
                        act.wait_ge(*freed(w))
                        if j >= 2:
                            act.wait_ge(*done(w0 + MIX_ITEMS.index(("mean", j - 2))))
                        act.activation(qk2sq[:, j % 2, 0:width], qk2raw[:, j % 2, 0:width], ACT.Square).then_inc(qksq_ready, 1)
                    elif kind == "mean":
                        act.wait_ge(*done(w))
                        act.activation(qk2ms[:, j % 2, 0:width], work[:, w % 4, 0:width], ACT.Sqrt, bias=eps_col).then_inc(bank_free[w % 4], 1)
                    elif kind == "val":
                        act.wait_ge(*done(w))
                        act.activation(val2[:, 2 * j:2 * j + 2, 0:2, :].rearrange("p h t d -> p t h d"), work[:, w % 4, :].rearrange("p (t h d) -> p t h d", t=2, h=2), ACT.Copy).then_inc(bank_free[w % 4], 1)
                    elif kind == "lastval":
                        empty(w, val2[0:META, 2 * j:2 * j + 2, 2, :], work[0:META, w % 4, 0:S].rearrange("p (h d) -> p h d", h=2))
                    elif kind == "swaval":
                        act.wait_ge(*done(w))
                        act.activation(val2[:, 4, 0:2, :], work[:, w % 4, 0:S].rearrange("p (t d) -> p t d", t=2), ACT.Copy)
                        act.activation(val2[0:META, 4, 2, :], work[0:META, w % 4, S:S + P], ACT.Copy).then_inc(bank_free[w % 4], 1)

            def gates():
                act.wait_ge(*freed(W0["gates"] - 1))
                for i in range(2 * K):
                    w = W0["gates"] + i
                    split_to(SLOT0["gates"] + i)
                    empty(w, gate2[:, i, :], work[:, w % 4, 0:S], ACT.Sigmoid)

            def attend(name, n_before):
                w0 = W0[name]
                fox = name == "fox"

                def turn_copy(w, u, i):
                    h, t = u // NT, u % NT
                    if h >= 2:
                        act.wait_ge(*done(w0 + FOX_ITEMS.index(("mix", h - 2))))
                    act.wait_ge(*done(w))
                    act.activation(prob2[:, h % 2, 0:t + 1, t, :], work[:, w % 4, 0:(t + 1) * P].rearrange("p (b q) -> p b q", q=P), ACT.Copy)
                    act.activation(prob2[0:META, h % 2, t + 1, t, :], work[0:META, w % 4, (t + 1) * P:(t + 2) * P], ACT.Copy).then_inc(bank_free[w % 4], 1)

                softmax(FOX_ITEMS, w0, name, scores2, n_before, lambda u: META + P * (u % NT + 1) + (0 if fox else 1), turn_copy)

            act.wait_ge(const_in, 64)
            act.wait_ge(memset_done, 1)
            after = lambda name: lambda k: freed(W0[name] + k)
            norm(0, XS, lambda k: (const_in, 64))
            even()
            retention()
            moba()
            split_all("evenout")
            norm(1, XS, after("evenout"))
            peer(0)
            norm(2, XS, lambda k: (stream_block, k + 1))
            odd()
            split_all("oddout")
            norm(3, XS, after("oddout"))
            peer(1)
            norm(4, XS, lambda k: (stream_block, K + k + 1))
            norm(5, ALL, lambda k: (stream_block, 2 * K + k + 1))
            feed_forward(1, ALL)
            split_all("ffn1out", 3)
            norm(6, ALL, after("ffn1out"))
            mix()
            attend("fox", HEADS * NT)
            attend("swa", HEADS * NT + FOXH * NT)
            gates()
            split_all("branch")
            split_all("mixout")
            norm(7, XS, after("mixout"))
            feed_forward(2, XS)
            split_all("ffn2out", 3)

        @block.vector
        def _(dve):
            def step():
                dve.wait_ge(vec.sem, vec.n)

            ahead = [0]

            def split_to(n):
                while ahead[0] < len(SLOTS) and ahead[0] <= n + AHEAD:
                    if ahead[0] in SPLIT and not any(ahead[0] in r for r in POOL_SLOTS):
                        split_lo(dve, ahead[0])
                    ahead[0] += 1

            def parts(k, cols, src, ready, hi=normed_hi, lo=normed_lo):
                dve.tensor_copy(hi[:, k, cols], src).then_inc(vec.sem, vec.up())
                step()
                dve.tensor_tensor(lo[:, k, cols], src, hi[:, k, cols].bitcast(F32), ALU.subtract).then_inc(ready, 1)

            def norm(n, cols, dst=normed):
                w = W0[f"norm{n}"]
                width = cols.stop - cols.start
                dve.wait_ge(*freed(w))
                dve.reciprocal(rstd[:, 0:width], rstd[:, 0:width]).then_inc(vec.sem, vec.up())
                step()
                first = K * (n - (n > 4))
                for k in range(K + 1):
                    if k < K:
                        dve.scalar_tensor_tensor(dst[:, k, cols], stream[:, k, cols], gains[:, n, k:k + 1], rstd[:, 0:width], ALU.mult, ALU.mult
                                                 ).then_inc(stream_block if n == 4 else plain_ready, 1)
                    if k and n != 4:
                        dve.wait_ge(lead_ready, first + k)
                        dve.tensor_tensor(normed_lo[:, k - 1, cols], normed[:, k - 1, cols], normed_hi[:, k - 1, cols].bitcast(F32), ALU.subtract
                                          ).then_inc(normed_ready, 1)

            def even():
                n = SLOT0["even"]
                for i, (kind, j) in enumerate(EVEN_ITEMS):
                    w = W0["even"] + i
                    if kind != "rot":
                        n += 2 if kind == "val" else 1
                        split_to(n - 1)
                    if kind == "rot":
                        dve.wait_ge(*freed(W0["even"] + EVEN_ITEMS.index(("proj", j))))
                        if j >= 2:
                            dve.wait_ge(turned_ready, j - 1)
                        dve.tensor_tensor(qk1[:, j, :], qk1raw[:, j % 2, :], cos, ALU.mult).then_inc(vec.sem, vec.up())
                        dve.wait_ge(*done(w))
                        dve.tensor_tensor(rot_tmp[:, j % 2, :], work[:, w % 4, 0:S], sin, ALU.mult).then_inc(bank_free[w % 4], 1)
                        step()
                        dve.wait_ge(*freed(w))
                        dve.tensor_tensor(qk1[:, j, :], qk1[:, j, :], rot_tmp[:, j % 2, :], ALU.add).then_inc(turned_ready, 1)

            def soft_rows(items, name, scores, n_before, addend, scale, width_of, sink, out):
                w0 = W0[name]
                normalised = [0]

                def normalise_to(last):
                    while normalised[0] <= last:
                        u = normalised[0]
                        dve.wait_ge(exp_ready, n_before + u + 1)
                        total = small[:, 12 + u % 4:13 + u % 4]
                        dve.reciprocal(total, total).then_inc(vec.sem, vec.up())
                        step()
                        row = scores[:, u % 4, 0:width_of(u)]
                        dve.tensor_scalar(row, row, total, None, ALU.mult).then_inc(probs_ready, 1)
                        normalised[0] += 1

                for i, (kind, u) in enumerate(items):
                    w = w0 + i
                    n = width_of(u)
                    row = scores[:, u % 4, 0:n]
                    if kind == "score":
                        normalise_to(u - 2)
                        if u >= 4:
                            dve.wait_ge(*done(w0 + items.index(("turn", u - 4))))
                        dve.wait_ge(*done(w))
                        dve.scalar_tensor_tensor(row, work[:, w % 4, 0:n], scale, addend(u), ALU.mult, ALU.add).then_inc(bank_free[w % 4], 1)
                        if sink:
                            h = u // NT
                            dve.tensor_copy(scores[:, u % 4, n:n + 1], sinks[:, h:h + 1]).then_inc(vec.sem, vec.up())
                            step()
                            row = scores[:, u % 4, 0:n + 1]
                        dve.wait_ge(*freed(w))
                        if n_before + u >= 4:
                            dve.wait_ge(exp_ready, n_before + u - 3)
                        dve.tensor_reduce(small[:, 8 + u % 4:9 + u % 4], row, AX.X, ALU.max, negate=True).then_inc(scores_ready, 1)
                    elif kind == "turn":
                        normalise_to(u)
                    else:
                        dve.wait_ge(*done(w))
                        out(w, u)

            def moba():
                def out(w, h):
                    dve.tensor_copy(normed_hi[:, h, XS], work[:, w % 4, 0:S]).then_inc(vec.sem, vec.up())
                    step()
                    dve.tensor_tensor(normed_lo[:, h, XS], work[:, w % 4, 0:S], normed_hi[:, h, XS].bitcast(F32), ALU.subtract).then_inc(bank_free[w % 4], 1)
                    dve.wait_ge(*freed(W0["ret"] + RET_ITEMS.index(("mean", h))))
                    dve.reciprocal(retms[:, h, :], retms[:, h, :]).then_inc(vec.sem, vec.up())
                    step()
                    dve.tensor_tensor(ret1[:, h, :], ret1[:, h, :], retms[:, h, :], ALU.mult).then_inc(vec.sem, vec.up())
                    step()
                    dve.tensor_tensor(ret1[:, h, :], ret1[:, h, :], silu1[:, h, :], ALU.mult).then_inc(vec.sem, vec.up())
                    step()
                    parts(HEADS + h, XS, ret1[:, h, :], mixed_ready)

                soft_rows(MOBA_ITEMS, "moba", scores1, 0, lambda u: cst("causal")[:, (1 - u % NT) * P:S], P ** -0.5,
                          lambda u: P * (u % NT + 1), False, out)

            def retention():
                for i, (kind, h) in enumerate(RET_ITEMS):
                    w = W0["ret"] + i
                    if kind == "inner":
                        dve.wait_ge(*done(w))
                        if h >= 2:
                            dve.wait_ge(*done(W0["ret"] + RET_ITEMS.index(("outer", h - 2))))
                        dve.tensor_tensor(inner1[:, h % 2, :], work[:, w % 4, 0:384], decay[:, h, :], ALU.mult).then_inc(vec.sem, vec.up())
                        step()
                        dve.engine_nop().then_inc(bank_free[w % 4], 1)
                        dve.engine_nop().then_inc(inner_ready, 1)
            def residual(name, n, cols, scale=1.0, slots=1):
                width = cols.stop - cols.start
                for c in range(K):
                    w = W0[name] + c
                    split_to(SLOT0[name] + (c + 1) * slots - 1)
                    dve.wait_ge(*done(w))
                    dve.scalar_tensor_tensor(stream[:, c, cols], work[:, w % 4, 0:width], scale, stream[:, c, cols], ALU.mult, ALU.add).then_inc(bank_free[w % 4], 1)
                for c in range(K - 4, K):
                    dve.wait_ge(*freed(W0[name] + c))
                dve.engine_nop().then_inc(stream_ready, 1)

            def top16(dst, at, src, tmp, n):
                for r in range(n):
                    ins = dve.max(dst(r)[:, 0:8], src(r))
                ins.then_inc(vec.sem, vec.up())
                step()
                for r in range(n):
                    dve.max_index(at(r)[:, 0:8], dst(r)[:, 0:8], src(r))
                    ins = dve.match_replace(tmp(r), dst(r)[:, 0:8], src(r), -3.0e38)
                ins.then_inc(vec.sem, vec.up())
                step()
                for r in range(n):
                    ins = dve.max(dst(r)[:, 8:16], tmp(r))
                ins.then_inc(vec.sem, vec.up())
                step()
                for r in range(n):
                    ins = dve.max_index(at(r)[:, 8:16], dst(r)[:, 8:16], tmp(r))
                return ins

            def choose(l):
                u32 = lambda v: v.bitcast(U32)
                for t in range(NT):
                    for g in range(4):
                        w = W0[f"subkey{l}"] + 4 * t + g
                        dve.wait_ge(*freed(w))
                        top16(lambda r: best[:, t, 4 * g + r, :], lambda r: u32(best_at[:, 4 * g + r, :]),
                              lambda r: sub[:, 4 * t + g, r * P:(r + 1) * P], lambda r: sub2[:, r * P:(r + 1) * P], 4).then_inc(vec.sem, vec.up())
                        step()
                    dve.tensor_copy(best_f[:, :, :], u32(best_at[:, :, :])).then_inc(vec.sem, vec.up())
                    hp = best[:, t, :, :].rearrange("p (h x) k -> p h x k", x=2)
                    c4 = cand[:, :, :].rearrange("p h (i j) -> p h i j", j=TOPK)
                    shape = [P, PH, TOPK, TOPK]
                    dve.tensor_tensor(c4, hp[:, :, 0, :].unsqueeze(3).to_broadcast(shape), hp[:, :, 1, :].unsqueeze(2).to_broadcast(shape),
                                      ALU.add).then_inc(vec.sem, vec.up())
                    step()
                    top = pair[:, t, :].rearrange("p (h k) -> p h k", k=TOPK)
                    at = pair_at.rearrange("p (h k) -> p h k", k=TOPK)
                    top16(lambda r: top[:, r, :], lambda r: u32(at[:, r, :]), lambda r: cand[:, r, :], lambda r: cand2[:, r, :], PH).then_inc(vec.sem, vec.up())
                    step()
                    dve.tensor_copy(psum8[:, t, 1, :], top[:, :, 0]).then_inc(vec.sem, vec.up())
                    step()
                    dve.tensor_tensor(top, top, psum8[:, t, 1, :].unsqueeze(2).to_broadcast([P, PH, TOPK]), ALU.subtract).then_inc(gate_diff_ready, 1)
                    dve.tensor_scalar(u32(pair_ab[:, 0, :]), u32(pair_at), 4, None, ALU.logical_shift_right).then_inc(vec.sem, vec.up())
                    dve.tensor_scalar(u32(pair_ab[:, 1, :]), u32(pair_at), TOPK - 1, None, ALU.bitwise_and).then_inc(vec.sem, vec.up())
                    step()
                    dve.tensor_copy(pair_f[:, :, :], u32(pair_ab[:, :, :])).then_inc(vec.sem, vec.up())
                    step()
                    for x in range(2):
                        ranks = iota[:, 0:TOPK].unsqueeze(1).to_broadcast([P, PH * TOPK, TOPK])
                        dve.tensor_tensor(eq[:, :, :], pair_f[:, x, :].unsqueeze(2).to_broadcast([P, PH * TOPK, TOPK]), ranks, ALU.is_equal).then_inc(vec.sem, vec.up())
                        step()
                        keys = best_f[:, :, :].rearrange("p (h x) k -> p h x k", x=2)[:, :, x, :]
                        dve.tensor_tensor(ev[:, :, :].rearrange("p (h k) r -> p h k r", k=TOPK), eq[:, :, :].rearrange("p (h k) r -> p h k r", k=TOPK),
                                          keys.unsqueeze(2).to_broadcast(shape), ALU.mult).then_inc(vec.sem, vec.up())
                        step()
                        dve.tensor_reduce(chosen[:, t, x, :], ev[:, :, :], AX.X, ALU.add).then_inc(vec.sem, vec.up())
                        step()
                    gate = chosen[:, t, 2, :].rearrange("p (h k) -> p h k", k=TOPK)
                    dve.wait_ge(gate_exp_ready, NT * l + t + 1)
                    dve.tensor_reduce(psum8[:, t, 0, :], gate, AX.X, ALU.add).then_inc(vec.sem, vec.up())
                    step()
                    dve.reciprocal(psum8[:, t, 0, :], psum8[:, t, 0, :]).then_inc(vec.sem, vec.up())
                    step()
                    dve.tensor_tensor(gate, gate, psum8[:, t, 0, :].unsqueeze(2).to_broadcast([P, PH, TOPK]), ALU.mult).then_inc(picks_ready, 1)

            def peer(l):
                for j in range(16):
                    split_to(SLOT0[f"query{l}"] + j)
                split_to(SLOT0[f"expert{l}.0"] - 1)
                choose(l)
                for t in range(NT):
                    dve.wait_ge(*freed(W0[f"turn{l}"] + t))
                for x in range(2, 5):
                    dve.tensor_copy(picks[:, x, :], gate_rest).then_inc(vec.sem, vec.up())
                    step()
                    if x < 4:
                        dve.tensor_tensor(gate_rest, gate_rest, picks[:, x, :], ALU.subtract).then_inc(vec.sem, vec.up())
                        step()
                c0 = l * CHUNKS

                def one_hots(count, tok, h0, w, i, pace=3):
                    for b in range(2):
                        if w is not None:
                            if b == 0:
                                dve.wait_ge(hots_read, i * 8 + count)
                            else:
                                dve.wait_ge(bank_done[w % 4], i * pace + (w // 4 + 1))
                        of = lambda x, n: picks[:, x:x + n, bass.ds(i * 64 + (tok + 4 * b), 4)]
                        first, second = hot_first[:, b, :, :], hot_second[:, b, :, :]
                        dve.tensor_tensor(first, keys4[:, h0:h0 + HALF, :], of(0, 1).to_broadcast([P, HALF, 4]), ALU.is_equal).then_inc(hots_used, 1)
                        dve.tensor_tensor(second, keys4[:, :, :], of(1, 1).to_broadcast([P, P, 4]), ALU.is_equal)
                        dve.wait_ge(hots_used, i * 16 + (2 * count + b + 1))
                        shape = [P, 3, HALF, 4]
                        dve.tensor_tensor(hot_gated[:, b, :, :, :], first.unsqueeze(1).to_broadcast(shape), of(2, 3).unsqueeze(2).to_broadcast(shape), ALU.mult).then_inc(hots_ready, 1)

                def weigh(e, i):
                    if l or e >= 4:
                        dve.wait_ge(chunk_used, i * 4 + (c0 + e - 3))
                    if isinstance(i, int):
                        hid, co = hidden[:, e % HELD, :], coef[:, :, e % HALF]
                    else:
                        hid, co = hidden[:, bass.ds(i * 4 + e % HELD, 1), :].squeeze(1), coef[:, :, bass.ds(i * 4 + e % HALF, 1)].squeeze(2)
                    at = 2 * (c0 + e)
                    dve.tensor_tensor(product[:, e % 2, :], hid, co, ALU.mult).then_inc(coef_read, 1)
                    dve.wait_ge(coef_read, i * 8 + (at + 1))
                    dve.tensor_copy(weighed[:, 0, e % 4, :], product[:, e % 2, :]).then_inc(coef_read, 1)
                    dve.wait_ge(coef_read, i * 8 + (at + 2))
                    dve.tensor_tensor(weighed[:, 1, e % 4, :], product[:, e % 2, :], weighed[:, 0, e % 4, :].bitcast(F32), ALU.subtract).then_inc(chunk_ready, 1)

                built = l * 2 * S // 8
                for x, (kind, e, h, steps) in enumerate(SEGMENTS):
                    if x == 0:
                        continue
                    w0, base, slots, pace = W0[f"expert{l}.{x}"], SLOT0[f"expert{l}.{x}"], SLOTS_OF[kind], ITEMS_OF[kind]
                    h0 = 0 if x == 1 else HALF
                    if x == 2:
                        dve.wait_ge(lo_ready, SPLIT[base])
                        ahead[0] = base
                        split_to(base - 1)
                    if x == 6:
                        dve.wait_ge(lo_ready, SPLIT[base + AHEAD])
                    if x in (2, 6):
                        for b in range(4):
                            dve.wait_ge(*freed(w0 - 4 + b))
                    elif e is not None:
                        last = max(W0[f"expert{l}.{z}"] + (c - h2) * ITEMS_OF[kind2] for z, (kind2, _, h2, steps2) in enumerate(SEGMENTS)
                                   if h2 is not None for c in range(e, e + steps) if h2 <= c < h2 + steps2)
                        for b in range(4):
                            dve.wait_ge(*freed(last - b))

                    def four(at, i):
                        for j in range(at, at + 4):
                            if e is not None:
                                weigh(e + j, i)
                            if kind != "upcoef":
                                for y in range(slots):
                                    n = base + j * slots + AHEAD + y
                                    if n in SPLIT:
                                        split_lo(dve, n, i, 4 * slots)
                            if kind == "upcoef":
                                for y in range(2):
                                    w = w0 + pace * j + (1 if y else -1) if y or j else None
                                    one_hots(built + 2 * j + y, 16 * j + 8 * y, h0, w, i)

                    four(0, 0)
                    with dve.Fori(0, steps // 4 - 1) as i:
                        four(4, i)
                    if kind == "upcoef":
                        built += S // 8
                ahead[0] = SLOT0[f"expert{l}.{len(SEGMENTS) - 1}"] + SEGMENTS[-1][3] + AHEAD
                dve.wait_ge(chunk_used, c0 + CHUNKS)
                for k in range(K):
                    dve.tensor_tensor(stream[:, k, XS], stream[:, k, XS], acc[:, k // 2, (k % 2) * S:(k % 2 + 1) * S], ALU.add).then_inc(stream_block, 1)
                dve.wait_ge(stream_block, K * (l + 1))
                dve.engine_nop().then_inc(stream_ready, 1)

            def odd():
                split_to(SLOT0["odd"])
                for b in range(2):
                    ins = dve.memset(u_pad[:, b, 0:2], 0.0)
                ins.then_inc(vec.sem, vec.up())
                for i, (kind, c) in enumerate(ODD_ITEMS):
                    w = W0["odd"] + i
                    split_to(SLOT0["odd"] + i)
                    b = c % 2
                    if kind == "value":
                        dve.wait_ge(*freed(w - 1))
                        dve.wait_ge(*done(w))
                        if c >= 2:
                            dve.wait_ge(zy_ready, c - 1)
                        dve.tensor_tensor(u_pad[:, b, 2:S + 2], work[:, w % 4, 0:S], cg[:, b, :], ALU.mult).then_inc(bank_free[w % 4], 1)
                        step()
                        dve.wait_ge(*freed(w))
                        dve.tensor_scalar(y_tmp[:, b, 0, :], u_pad[:, b, 0:S], conv[:, 0, c:c + 1], None, ALU.mult).then_inc(vec.sem, vec.up())
                        step()
                        dve.scalar_tensor_tensor(y_tmp[:, b, 1, :], u_pad[:, b, 1:S + 1], conv[:, 1, c:c + 1], y_tmp[:, b, 0, :], ALU.mult, ALU.add).then_inc(vec.sem, vec.up())
                        step()
                        dve.scalar_tensor_tensor(y_tmp[:, b, 0, :], u_pad[:, b, 2:S + 2], conv[:, 2, c:c + 1], y_tmp[:, b, 1, :], ALU.mult, ALU.add).then_inc(vec.sem, vec.up())
                        step()
                    elif kind == "bgate":
                        dve.wait_ge(*done(w))
                        dve.tensor_tensor(y_tmp[:, b, 1, :], work[:, w % 4, 0:S], y_tmp[:, b, 0, :], ALU.mult).then_inc(bank_free[w % 4], 1)
                        dve.wait_ge(*freed(w))
                        parts(c, slice(0, S), y_tmp[:, b, 1, :], zy_ready, z2_hi, z2_lo)

            def feed_forward(x, cols):
                width = cols.stop - cols.start
                for i, (kind, c) in enumerate(FFN_ITEMS):
                    split_to(SLOT0[f"ffn{x}"] + i)
                    if kind == "ffup":
                        w = W0[f"ffn{x}"] + i
                        dve.wait_ge(*freed(w - 1))
                        dve.wait_ge(*done(w))
                        dve.tensor_tensor(ff_hid[:, c % 2, 0:width], work[:, w % 4, 0:width], ff_silu[:, c % 2, 0:width], ALU.mult).then_inc(bank_free[w % 4], 1)
                        dve.wait_ge(*freed(w))
                        parts(c, cols, ff_hid[:, c % 2, 0:width], ff_ready, ff_hi, ff_lo)

            def mix():
                w0, n = W0["mix"], SLOT0["mix"]
                dve.wait_ge(const2_in, 16 * 8)
                for i, (kind, j) in enumerate(MIX_ITEMS):
                    w = w0 + i
                    cols = XS if j < 4 or 8 <= j < 12 else ALL
                    width = cols.stop - cols.start
                    if kind in ("proj", "val", "swaval"):
                        n += 2 if kind == "val" else 1
                        split_to(n - 1)
                    if kind == "forget":
                        dve.wait_ge(*done(w))
                        dve.tensor_scalar(forget[0:FOXH, 1, :], work[0:FOXH, w % 4, 0:TA], small[0:FOXH, 4:5], None, ALU.add).then_inc(bank_free[w % 4], 1)
                        dve.wait_ge(*freed(w))
                        dve.engine_nop().then_inc(forget_in, 1)
                        dve.tensor_scalar(forget[0:FOXH, 5, :], forget[0:FOXH, 1, :], 0.0, None, ALU.min).then_inc(vec.sem, vec.up())
                        step()
                        dve.wait_ge(forget_out, 1)
                        dve.tensor_tensor(forget[0:FOXH, 6, :], forget[0:FOXH, 5, :], forget[0:FOXH, 4, :], ALU.subtract).then_inc(vec.sem, vec.up())
                        step()
                        dve.tensor_tensor_scan(forget[0:FOXH, 0, :], forget[0:FOXH, 6, :], forget[0:FOXH, 7, :], 0.0, ALU.add, ALU.add).then_inc(forget_ready, 1)
                    elif kind == "mean":
                        dve.wait_ge(*freed(w))
                        ms = qk2ms[:, j % 2, 0:width]
                        dve.reciprocal(ms, ms).then_inc(vec.sem, vec.up())
                        step()
                        dve.scalar_tensor_tensor(qk2[:, j, 0:width], qk2raw[:, j % 2, 0:width], cst("headgain")[:, j:j + 1], ms, ALU.mult, ALU.mult).then_inc(qk2_ready, 1)
                    elif kind == "table":
                        lo, hi = ((0, DX), (DX, DTAB))[j]
                        dve.wait_ge(*done(w))
                        dve.tensor_copy(table_out[0:FOXH, lo:hi], work[0:FOXH, w % 4, 0:hi - lo]).then_inc(bank_free[w % 4], 1)
                        dve.wait_ge(*freed(w))
                        dve.engine_nop().then_inc(table_ready, 1)

            def attend(name, n_before):
                fox = name == "fox"
                if not fox:
                    dve.wait_ge(bias_in, 64)

                def out(w, h):
                    half = slice((h % 2) * HD2, (h % 2 + 1) * HD2)
                    x, src = 0 if fox else 1, work[half, w % 4, 0:S]
                    dve.tensor_copy(att2_hi[half, x, h // 2, :], src).then_inc(vec.sem, vec.up())
                    step()
                    dve.tensor_tensor(att2_lo[half, x, h // 2, :], src, att2_hi[half, x, h // 2, :].bitcast(F32), ALU.subtract).then_inc(bank_free[w % 4], 1)

                def addend(u):
                    h, t = u // NT, u % NT
                    n = META + P * (t + 1)
                    return mask2[:, t, 0:n] if fox else bias2[:, t, h, 0:n]

                soft_rows(FOX_ITEMS, name, scores2, n_before, addend, HD2 ** -0.5, lambda u: META + P * (u % NT + 1), not fox, out)

            def branch():
                for c in range(K):
                    w = W0["branch"] + 2 * c
                    b = c % 2
                    split_to(SLOT0["branch"] + c)
                    dve.wait_ge(*freed(W0["gates"] + 2 * K - 1))
                    for x in range(2):
                        dve.wait_ge(*done(w + x))
                        dve.tensor_tensor(mix_t[:, b, x, :], work[:, (w + x) % 4, 0:S], gate2[:, x * K + c, :], ALU.mult).then_inc(bank_free[(w + x) % 4], 1)
                    for x in range(2):
                        dve.wait_ge(*freed(w + x))
                    dve.tensor_tensor(mix_y[:, b, :], mix_t[:, b, 0, :], mix_t[:, b, 1, :], ALU.add).then_inc(vec.sem, vec.up())
                    step()
                    parts(c, XS, mix_y[:, b, :], branch_ready)

            dve.wait_ge(const_in, 64)
            dve.tensor_copy(keys4[:, :, :], iota.unsqueeze(2).to_broadcast([P, NKEYS, 4]))
            for x in normed_parts:
                dve.memset(x[:, K * TA:].bitcast(F32), 0.0)
            norm(0, XS)
            even()
            retention()
            moba()
            residual("evenout", 1, XS)
            norm(1, XS)
            peer(0)
            norm(2, XS)
            odd()
            residual("oddout", 3, XS)
            norm(3, XS)
            peer(1)
            norm(4, XS, stream)
            norm(5, ALL)
            feed_forward(1, ALL)
            residual("ffn1out", 5, ALL, 0.5, 3)
            norm(6, ALL)
            mix()
            attend("fox", HEADS * NT)
            attend("swa", HEADS * NT + FOXH * NT)
            for i in range(2 * K):
                split_to(SLOT0["gates"] + i)
            branch()
            residual("mixout", 6, XS)
            norm(7, XS)
            feed_forward(2, XS)
            residual("ffn2out", 7, XS, 0.5, 3)


def fixed_arrays():
    f = np.float32
    c = {"ident": np.eye(P, dtype=f), "inv_d": np.full((P, P), 1.0 / D, f), "inv_head": np.full((P, P), 1.0 / P, f)}
    rot = np.zeros((P, P), f)
    half = P // 2
    rot[np.arange(half) + half, np.arange(half)] = -1.0
    rot[np.arange(half), np.arange(half) + half] = 1.0
    c["rot"] = rot
    c["inv_half"] = np.kron(np.eye(2), np.full((HD2, HD2), 1.0 / HD2)).astype(f)
    c["iota"] = np.tile(np.arange(P, dtype=f), (P, 1))
    inv = f(10000.0) ** (-np.arange(half, dtype=f) / f(half))
    ang = (np.arange(S, dtype=f)[:, None] * inv[None, :]).astype(f)
    c["cos"] = np.tile(np.cos(ang).astype(f).T, (2, 1))
    c["sin"] = np.tile(np.sin(ang).astype(f).T, (2, 1))
    log_g = np.log(1.0 - 2.0 ** (-5.0 - np.arange(HEADS)))
    diff = np.arange(S)[None, :] - np.arange(P)[:, None]
    dec = np.where(diff >= 0, np.exp(log_g[:, None, None] * np.maximum(diff, 0)), 0.0) * P ** -0.5
    c["decay"] = np.concatenate([dec, dec[:, :, :P]], axis=2).transpose(1, 0, 2).reshape(P, -1).astype(f)
    q, k = np.arange(P)[:, None], np.arange(P)[None, :]
    c["causal"] = np.concatenate([np.zeros((P, P)), np.where(k <= q, 0.0, NEG)], axis=1).astype(f)
    cols = np.arange(TA)
    late = {"foxmask": np.stack([np.where(cols[None, :] <= META + P * t + q, 0.0, NEG) for t in range(NT)], axis=1).astype(f)}
    eye = np.eye(FOXH)
    late["pick_head"] = np.repeat(HD2 ** 0.5 * eye[:, :, None], TA, axis=2).astype(f)
    late["neg_head"] = np.repeat(-HD2 ** 0.5 * eye[:, :, None], P, axis=2).astype(f)

    def bucket(d):
        exact = NB // 2
        large = exact + (np.log(np.maximum(d, 1).astype(f) / f(exact)) / f(np.log(P / exact)) * (NB - exact)).astype(np.int32)
        return np.where(d < exact, d, np.minimum(large, NB - 1))

    r = np.arange(DX) - 255
    x = np.where((r <= 0) & (r > -P), bucket(np.maximum(-r, 0)), NB)
    m = bucket(np.maximum(META - (np.arange(DM) - 255), 0))
    onehot = np.zeros((NB + 1, DTAB), f)
    onehot[np.concatenate([x, m]), np.arange(DTAB)] = 1.0
    late["onehot"] = onehot
    return c, late


def kernel(**inputs):
    import concourse.bacc as bacc
    from concourse.bass_utils import run_bass_kernel_spmd

    x = {k: np.asarray(v) for k, v in inputs.items()}

    def blocks(w):
        n = w.shape[1] // P
        return w.reshape(-1, P, n, P).transpose(2, 1, 0, 3).reshape(n, P, -1)

    def cols(v):
        return v.reshape(-1, P).T

    const, late = fixed_arrays()
    gains = [x["norm_mix"][0], x["norm_ffn"][0], x["norm_mix"][1], x["norm_ffn"][1], x["final_norm"],
             x["ffn1_norm_2"][0], x["mix_norm_2"][0], x["ffn2_norm_2"][0]]
    const["gains"] = np.concatenate([cols(g) for g in gains], axis=1)
    const["conv"] = np.concatenate([cols(w) for w in x["odd_conv"][0]], axis=1)
    twice = lambda g: np.tile(g, 2)[:, None]
    const["headgain"] = np.concatenate([twice(x["fox_q_norm_2"][0])] * 4 + [twice(x["fox_k_norm_2"][0])] * 4
                                       + [twice(x["swa_q_norm_2"][0])] * 4 + [twice(x["swa_k_norm_2"][0])] * 2, axis=1)
    arrays = {"const": np.concatenate([const[name] for name in CONST], axis=1),
              "early": np.concatenate([const[name] for name, _ in EARLY], axis=1)}
    arrays.update(late)
    arrays["x"] = x["x"][0].T.reshape(K, P, S).transpose(1, 0, 2)
    arrays["meta"] = x["meta_tokens_2"].T.reshape(K, P, META).transpose(1, 0, 2)
    w = blocks(x["even_w_in"][0])
    arrays["even_in"] = w[list(range(8)) + list(range(12, 20)) + list(range(8, 12)) + list(range(20, 28))]
    arrays["even_out"] = blocks(x["even_w_out"][0])
    w = blocks(x["odd_w_in"][0])
    arrays["odd_in"] = w[[j for c in range(K) for j in (K + c, 2 * K + c, c)]]
    arrays["odd_out"] = blocks(x["odd_w_out"][0])
    for l in range(2):
        arrays[f"query{l}"] = blocks(x["peer_w_q"][l])
        arrays[f"subkey{l}"] = x["peer_sub_keys"][l].reshape(2, 8, NKEYS, P).transpose(0, 3, 1, 2).reshape(2, P, D)
        arrays[f"u{l}"] = x["peer_u"][l].reshape(CHUNKS, P, K, P).transpose(0, 3, 2, 1).reshape(CHUNKS, P, D)
        arrays[f"v{l}"] = x["peer_v"][l].reshape(CHUNKS, P, D)
    for n in (1, 2):
        w = blocks(x[f"ffn{n}_w_in_2"][0])
        arrays[f"ffn{n}_in"] = w[[j for c in range(FC) for j in (c, FC + c)]]
        arrays[f"ffn{n}_out"] = blocks(x[f"ffn{n}_w_out_2"][0])
    w = x["w_in_2"][0]
    qa, ka, va, fa, qb, kb, vb, ga, gb = np.split(w, np.cumsum([512, 512, 512, FOXH, 512, 128, 128, D]), axis=1)
    arrays["mix_in"] = blocks(np.concatenate([qa, ka, qb, kb[:, :HD2], kb[:, :HD2], kb[:, HD2:], kb[:, HD2:], va, vb], axis=1))
    arrays["gate_in"] = blocks(np.concatenate([ga, gb], axis=1))
    arrays["w_forget"] = fa.reshape(K, P, FOXH).transpose(1, 0, 2)
    arrays["forget_bias"] = x["forget_bias_2"][0][:, None]
    arrays["table"] = x["rel_bias_table_2"]
    arrays["sinks"] = x["swa_sinks_2"][0]
    arrays["branch"] = blocks(np.concatenate([x["w_branch_fox_2"][0], x["w_branch_swa_2"][0]], axis=0))
    arrays["mix_out"] = blocks(x["w_out_2"][0])

    nc = bacc.Bacc("TRN2", target_bir_lowering=False, num_devices=1)
    aps, maps = {}, {}
    for name, v in arrays.items():
        v = np.ascontiguousarray(v)
        maps["in_" + name] = v
        aps[name] = nc.dram_tensor("in_" + name, list(v.shape), mybir.dt.from_np(v.dtype), kind="ExternalInput").ap()
    aps["scratch"] = nc.dram_tensor("bias_by_distance", [P, FOXH, DTAB], F32, kind="Internal").ap()
    aps["out"] = nc.dram_tensor("out", [P, K, S], F32, kind="ExternalOutput").ap()
    build(nc, aps)
    r = run_bass_kernel_spmd(nc, [maps], core_ids=[0])
    return r.results[0]["out"].transpose(1, 0, 2).reshape(D, S).T[None]
```

```python
from contextlib import ExitStack

import numpy as np

import concourse.bass as bass
from concourse import mybir

ALU = mybir.AluOpType
ACT = mybir.ActivationFunctionType
AX = mybir.AxisListType
F32 = mybir.dt.float32
F32R = mybir.dt.float32r
BF16 = mybir.dt.bfloat16
U32 = mybir.dt.uint32

P = 128
D = 1024
K = D // P
S = 256
META = 16
TA = META + S
XS = slice(META, TA)
ALL = slice(0, TA)
NT = S // P
EPS = 1e-6
NEG = -1e30
HEADS = 4
RING = 4
AHEAD = 2
HELD = 40
HALF = 64
NKEYS = 128
PH = 8
TOPK = 16
CANDS = 4 * TOPK + 4 * (TOPK - 4)
CHUNKS = NKEYS
FF = 2816
FC = FF // P
FOXH = 8
HD2 = 64
DX = 384
DM = 272
DTAB = DX + DM
NB = 32

EVEN_ITEMS = [("proj", 0)]
for _j in range(1, 16):
    EVEN_ITEMS += [("proj", _j), ("rot", _j - 1)]
EVEN_ITEMS += [("rot", 15)] + [("val", j) for j in range(4)]


def attention_items(units, lag=3):
    items = []
    for u in range(units + lag + 1):
        if u < units:
            items.append(("score", u))
        if u > lag and (u - lag) % NT == 0:
            items.append(("mix", (u - lag) // NT - 1))
        if lag <= u < units + lag:
            items.append(("turn", u - lag))
    return items


MOBA_ITEMS = attention_items(HEADS * NT)
RET_ITEMS = [("inner", 0), ("inner", 1), ("outer", 0), ("inner", 2), ("outer", 1), ("gate", 0), ("inner", 3), ("outer", 2), ("gate", 1), ("outer", 3)]
RET_ITEMS += [("mean", j) for j in range(HEADS)] + [("gate", 2), ("gate", 3)]
ODD_ITEMS = [(kind, c) for c in range(K) for kind in ("cgate", "value", "bgate")]
FFN_ITEMS = [(kind, c) for c in range(FC) for kind in ("ffgate", "ffup")]
QK2 = 14
MIX_ITEMS = [("proj", 0), ("proj", 1), ("forget", 0), ("mean", 0)]
for _j in range(2, QK2):
    MIX_ITEMS += [("proj", _j), ("mean", _j - 1)]
MIX_ITEMS += [("mean", QK2 - 1), ("val", 0), ("lastval", 0), ("val", 1), ("lastval", 1), ("swaval", 0), ("table", 0), ("table", 1)]
FOX_ITEMS = attention_items(FOXH * NT)
GATE_ITEMS = [("gate", j) for j in range(2 * K)]
BRANCH_ITEMS = [(kind, c) for c in range(K) for kind in ("foxout", "swaout")]

SEGMENTS = [("up", None, 0, 24), ("upcoef", None, 24, 16), ("pair", 0, 40, 40), ("pair", 40, 80, 8),
            ("down", 48, None, 16), ("upcoef", None, 88, 16), ("pair", 64, 104, 16), ("pair", 80, 120, 8),
            ("down", 88, None, 32), ("down", 120, None, 8)]
QUERY_ITEMS = []
for _j in range(16):
    QUERY_ITEMS.append(("query", _j))
    if _j and _j % 4 == 0:
        QUERY_ITEMS += [("score", (t, _j // 4 - 1)) for t in range(NT)]
QUERY_ITEMS += [("score", (t, 3)) for t in range(NT)]
ITEMS_OF = {"up": 1, "upcoef": 3, "pair": 1, "down": 0}
SLOTS_OF = {"up": 1, "upcoef": 1, "pair": 2, "down": 1}

STAGES = [("norm0", 1), ("even", len(EVEN_ITEMS)), ("ret", len(RET_ITEMS)), ("moba", len(MOBA_ITEMS)),
          ("evenout", K)]
for _l in range(2):
    if _l == 1:
        STAGES += [("norm2", 1), ("odd", len(ODD_ITEMS)), ("oddout", K)]
    STAGES += [(f"norm{2 * _l + 1}", 1), (f"query{_l}", len(QUERY_ITEMS))]
    for _x, (_kind, _e, _h, _steps) in enumerate(SEGMENTS):
        if _x == 1:
            STAGES += [(f"turn{_l}", 2)]
        STAGES += [(f"expert{_l}.{_x}", _steps * ITEMS_OF[_kind])]
STAGES += [("norm4", 1), ("norm5", 1), ("ffn1", len(FFN_ITEMS)), ("ffn1out", K),
           ("norm6", 1), ("mix", len(MIX_ITEMS)), ("fox", len(FOX_ITEMS)), ("swa", len(FOX_ITEMS)), ("gates", len(GATE_ITEMS)),
           ("branch", len(BRANCH_ITEMS)), ("mixout", K),
           ("norm7", 1), ("ffn2", len(FFN_ITEMS)), ("ffn2out", K)]
W0 = {}
_n = 0
for _name, _count in STAGES:
    W0[_name] = _n
    _n += _count


def plan_slots():
    slots, base = [], {}

    def linear(name, items, kinds, array, first=0):
        base[name] = len(slots)
        n = first
        for i, (kind, j) in enumerate(items):
            if kind in kinds:
                last = i + (kind == "val" and items[i + 1:i + 2] == [("lastval", j)])
                for _ in range(2 if kind == "val" else 1):
                    slots.append((array, n, D, ("item", W0[name] + last)))
                    n += 1

    def out(name, array, widths):
        base[name] = len(slots)
        for c in range(K):
            for part, width in enumerate(widths):
                slots.append((array, (c, part), width, ("item", W0[name] + c)))

    linear("even", EVEN_ITEMS, ("proj", "val"), "even_in")
    linear("ret", RET_ITEMS, ("gate",), "even_in", 24)
    out("evenout", "even_out", [D])
    for l in range(2):
        if l == 1:
            linear("odd", ODD_ITEMS, ("cgate", "value", "bgate"), "odd_in")
            out("oddout", "odd_out", [D])
        linear(f"query{l}", QUERY_ITEMS, ("query",), f"query{l}")
        for x, (kind, e, h, steps) in enumerate(SEGMENTS):
            base[f"expert{l}.{x}"] = len(slots)
            for k in range(steps):
                if h is not None:
                    slots.append((f"u{l}", h + k, D, ("item", W0[f"expert{l}.{x}"] + k * ITEMS_OF[kind])))
                if e is not None:
                    slots.append((f"v{l}", e + k, D, ("chunk", l * CHUNKS + e + k)))
    ff_out = [D, D, (FC - 16) * P]
    linear("ffn1", FFN_ITEMS, ("ffgate", "ffup"), "ffn1_in")
    out("ffn1out", "ffn1_out", ff_out)
    linear("mix", MIX_ITEMS, ("proj", "val", "swaval"), "mix_in")
    linear("gates", GATE_ITEMS, ("gate",), "gate_in")
    base["branch"] = len(slots)
    for c in range(K):
        slots.append(("branch", c, D, ("item", W0["branch"] + 2 * c + 1)))
    out("mixout", "mix_out", [D])
    linear("ffn2", FFN_ITEMS, ("ffgate", "ffup"), "ffn2_in")
    out("ffn2out", "ffn2_out", ff_out)
    return slots, base


SLOTS, SLOT0 = plan_slots()
POOL_SLOTS = []
for _l in range(2):
    POOL_SLOTS += [range(SLOT0[f"query{_l}"] + AHEAD, SLOT0[f"expert{_l}.2"]),
                   range(SLOT0[f"expert{_l}.5"] + AHEAD, SLOT0[f"expert{_l}.6"] + AHEAD)]

HEAD_SLOTS = range(SLOT0["mix"] + AHEAD, SLOT0["mix"] + QK2)

CONST = {}
_n = 0
for _name, _count in [("ident", P), ("rot", P), ("inv_d", P), ("inv_head", P), ("inv_half", P), ("iota", P),
                      ("causal", S), ("gains", 8 * K),
                      ("conv", 3 * K), ("headgain", QK2)]:
    CONST[_name] = (_n, _n + _count)
    _n += _count
N_CONST = _n
ARENA = (HELD + HALF) * S
EARLY = [("cos", S), ("sin", S), ("decay", HEADS * 384)]


class Tally:

    def __init__(self, sem):
        self.sem, self.n = sem, 0

    def up(self):
        self.n += 1
        return 1


def build(nc, a):
    with ExitStack() as ctx:
        def sb(name, shape, dt=F32):
            return ctx.enter_context(nc.sbuf_tensor(name, shape, dt))

        def sem(name):
            return ctx.enter_context(nc.semaphore(name))

        stream = sb("stream", [P, K, TA])
        normed_parts = [sb(f"normed_{x}", [P, K * TA + P - META], F32R) for x in ("hi", "lo")]
        normed_hi, normed_lo = [x[:, 0:K * TA].rearrange("p (k t) -> p k t", k=K) for x in normed_parts]
        ring = sb("ring", [P, RING, D])
        ring_hi = sb("ring_hi", [P, RING, D], F32R)
        ring_lo = sb("ring_lo", [P, RING, D], F32R)
        const = sb("const", [P, N_CONST])
        rstd = sb("rstd", [P, TA])
        desk = sb("desk", [P, 3 * 2 * (P + 4 * HALF)])
        normed = desk[:, 0:K * TA].rearrange("p (k t) -> p k t", k=K)
        product = sb("product", [P, 2, S])
        sub_keys = desk[:, 0:16 * NKEYS].rearrange("p (h e) -> p h e", e=NKEYS)
        rows = desk[:, :].bitcast(BF16).rearrange("p (b e t) -> p b e t", b=3, t=4)
        last = product[:, :, :].rearrange("p b t -> p (b t)").bitcast(BF16).rearrange("p (e t) -> p e t", t=4)
        hot_second = [rows[:, b, 0:P, :] for b in range(3)] + [rstd[:, 0:2 * P].bitcast(BF16).rearrange("p (e t) -> p e t", t=4)]
        hot_first = [rows[:, b, P:P + HALF, :] for b in range(3)] + [last[:, 0:HALF, :]]
        hot_gated = [x.rearrange("p (x e) t -> p x e t", x=3) for x in [rows[:, b, P + HALF:, :] for b in range(3)] + [last[:, HALF:, :]]]
        weighed = sb("weighed", [P, 2, 4, S], F32R)
        picks = sb("picks", [P, 5, S], BF16)
        gate_rest = rstd[:, 0:S]
        keys4 = sb("keys4", [P, NKEYS, 4], BF16)
        small = sb("small", [P, 16])
        with nc.sbuf_tensor("arena", [P, ARENA], F32) as arena:
            pass
        arena_parts = sb("arena_parts", [P, ARENA], F32R)
        acc = ctx.enter_context(nc.psum_tensor("acc", [P, 4, 512], F32))
        work = ctx.enter_context(nc.psum_tensor("work", [P, 4, 512], F32))

        def cst(name, rows=P):
            lo, hi = CONST[name]
            return const[0:rows, lo:hi]

        ident, iota = cst("ident"), cst("iota")
        gains = cst("gains").rearrange("p (n k) -> p n k", k=K)
        conv = cst("conv").rearrange("p (w k) -> p w k", k=K)
        eps_col = small[:, 0:1]

        used = {}

        def view(group, shape, arena=arena):
            n = int(np.prod(shape))
            at = used.get(group, 0)
            used[group] = at + n
            assert used[group] <= ARENA, group
            v = arena[:, at:at + n]
            names = "abcd"[:len(shape)]
            if len(shape) > 1:
                v = v.rearrange(f"p ({' '.join(names)}) -> p {' '.join(names)}",
                                **{x: s for x, s in zip(names[1:], shape[1:])})
            return v

        early = view("even", [2 * S + HEADS * 384])
        cos, sin = early[:, 0:S], early[:, S:2 * S]
        decay = early[:, 2 * S:].rearrange("p (h n) -> p h n", h=HEADS)
        qk1 = view("even", [16, S])
        qk1raw = view("even", [2, S])
        rot_tmp = view("even", [2, S])
        val1 = view("even", [8, NT, P])
        silu1 = view("even", [HEADS, S])
        scores1 = view("even", [4, S])
        prob1 = view("even", [2, NT, S])
        inner1 = view("even", [2, 384])
        ret1 = view("even", [HEADS, S])
        retsq = view("even", [HEADS, S])
        retms = view("even", [HEADS, S])
        cg = view("odd", [2, S])
        u_pad = view("odd", [2, S + 2])
        y_tmp = view("odd", [2, 2, S])
        z2_hi, z2_lo = [view("odd", [K, S], arena_parts) for _ in range(2)]
        used["peer"] = HELD * S
        query = view("peer", [16, S])
        sub = view("peer", [8, 512])
        sub2 = view("peer", [512])
        best = view("peer", [NT, 16, TOPK])
        best_at = view("peer", [NT, 16, TOPK])
        best_f = view("peer", [NT, 16, TOPK])
        cand = view("peer", [PH, TOPK * TOPK])
        cand2 = view("peer", [PH, TOPK * TOPK])
        eq = cand.rearrange("p h (i r) -> p (h i) r", r=TOPK)
        ev = cand2.rearrange("p h (i r) -> p (h i) r", r=TOPK)
        pair = view("peer", [NT, PH * TOPK])
        pair_at = view("peer", [PH * TOPK])
        pair_ab = cand2.rearrange("p h n -> p (h n)")[:, 0:4 * PH * TOPK].rearrange("p (x k) -> p x k", x=4)
        pair_f = view("peer", [4, PH * TOPK])
        chosen = view("peer", [NT, 3, PH * TOPK])
        psum8 = view("peer", [NT, 2, PH])
        hidden = arena[:, 0:HELD * S].rearrange("p (h t) -> p h t", t=S)
        coef = arena[:, HELD * S:].rearrange("p (t e) -> p t e", e=HALF)
        ff_hi, ff_lo = [view("ffn", [FC, TA], arena_parts) for _ in range(2)]
        ff_hid = view("ffn", [2, TA])
        ff_silu = view("ffn", [2, TA])
        qk2 = view("mix", [QK2, TA])
        qk2raw = view("mix", [2, TA])
        qk2sq = view("mix", [2, TA])
        qk2ms = view("mix", [2, TA])
        bias2 = view("mix", [NT, FOXH, TA])
        val2 = view("mix", [5, 3, P])
        scores2 = view("mix", [4, TA + 4])
        prob2 = view("mix", [2, 3, 2, P])
        att2_hi, att2_lo = [view("mix", [2, 4, S], arena_parts) for _ in range(2)]
        mask2 = view("mix", [NT, TA])
        forget = view("mix", [8, TA])
        pick_head = view("mix", [FOXH, TA])
        neg_head = view("mix", [FOXH, P])
        table = view("mix", [FOXH])
        onehot = view("mix", [DTAB])
        table_out = view("mix", [DTAB])
        sinks = view("mix", [FOXH])
        w_forget = view("mix", [K, FOXH])
        gate2 = view("after", [2 * K, S])
        mix_y = view("after", [2, S])
        mix_t = view("after", [2, 2, S])

        x_in, early_in, meta_in = sem("x_in"), sem("early_in"), sem("meta_in")
        const_in, const2_in, keys_in = sem("const_in"), sem("const2_in"), sem("keys_in")
        landed = [sem(f"landed{r}") for r in range(RING)]
        bank_done = [sem(f"bank_done{b}") for b in range(4)]
        bank_free = [sem(f"bank_free{b}") for b in range(4)]
        chunk_ready, chunk_used = sem("chunk_ready"), sem("chunk_used")
        hi_ready, lo_ready = sem("hi_ready"), sem("lo_ready")
        squares_ready, plain_ready, lead_ready = sem("squares_ready"), sem("plain_ready"), sem("lead_ready")
        coef_read, hots_used = sem("coef_read"), sem("hots_used")
        stream_block = sem("stream_block")
        normed_ready, stream_ready = sem("normed_ready"), sem("stream_ready")
        turned_ready = sem("turned_ready")
        scores_ready, exp_ready, probs_ready = sem("scores_ready"), sem("exp_ready"), sem("probs_ready")
        inner_ready = sem("inner_ready")
        retsq_ready, retstd_ready = sem("retsq_ready"), sem("retstd_ready")
        mixed_ready = sem("mixed_ready")
        zy_ready = sem("zy_ready")
        gate_diff_ready, gate_exp_ready, picks_ready = sem("gate_diff_ready"), sem("gate_exp_ready"), sem("picks_ready")
        hots_ready, hots_read = sem("hots_ready"), sem("hots_read")
        ff_ready = sem("ff_ready")
        qksq_ready, qkstd_ready, qk2_ready = sem("qksq_ready"), sem("qkstd_ready"), sem("qk2_ready")
        forget_in, forget_out, forget_ready = sem("forget_in"), sem("forget_out"), sem("forget_ready")
        table_ready, table_stored, bias_in = sem("table_ready"), sem("table_stored"), sem("bias_in")
        branch_ready = sem("branch_ready")
        memset_done = sem("memset_done")
        stored = sem("stored")
        vec = Tally(sem("vec_step"))
        own = Tally(sem("act_step"))

        def done(w):
            return bank_done[w % 4], w // 4 + 1

        def freed(w):
            return bank_free[w % 4], w // 4 + 1

        def wait_bank(pe, w):
            if w >= 4:
                pe.wait_ge(*freed(w - 4))

        def used_by_pe(n, i=0, step=1):
            kind, x = SLOTS[n][3]
            if kind == "item":
                return bank_done[x % 4], i * step + (x // 4 + 1)
            return chunk_used, i * 4 + (x + 1)

        def split_hi(act, n, i=0, slots=4, step=1):
            if n >= RING:
                act.wait_ge(*used_by_pe(n - RING, i, step))
            act.wait_ge(landed[n % RING], i * (16 * slots // RING) + 16 * (n // RING + 1))
            width = SLOTS[n][2]
            act.activation(ring_hi[:, n % RING, 0:width], ring[:, n % RING, 0:width], ACT.Copy).then_inc(hi_ready, 1)

        def split_lo(eng, n, i=0, slots=4):
            eng.wait_ge(hi_ready, i * slots + (n + 1))
            width = SLOTS[n][2]
            eng.tensor_tensor(ring_lo[:, n % RING, 0:width], ring[:, n % RING, 0:width], ring_hi[:, n % RING, 0:width].bitcast(F32), ALU.subtract).then_inc(lo_ready, 1)

        def product3(pe, out, n, k, hi, lo, start, stop, **more):
            m = n % RING
            w_hi, w_lo = ring_hi[:, m, k * P:(k + 1) * P], ring_lo[:, m, k * P:(k + 1) * P]
            pe.matmul(out, w_hi, hi, start=start, stop=False, **more)
            pe.matmul(out, w_hi, lo, start=False, stop=False, **more)
            return pe.matmul(out, w_lo, hi, start=False, stop=stop, **more)

        def source(n):
            array, index, width, _ = SLOTS[n]
            if isinstance(index, tuple):
                c, part = index
                return a[array][c][:, part * D:part * D + width], width
            return a[array][index], width

        block = ctx.enter_context(nc.Block())

        @block.sync
        def _(sp):
            def load(n):
                src, width = source(n)
                if n >= RING:
                    sp.wait_ge(lo_ready, n - RING + 1)
                sp.dma_start(ring[:, n % RING, 0:width], src).then_inc(landed[n % RING], 16)

            def expert_loads(l):
                for x, (kind, e, h, steps) in enumerate(SEGMENTS):
                    base, per = SLOT0[f"expert{l}.{x}"], 4 * SLOTS_OF[kind]
                    for q in range(per):
                        load(base + q)
                    with sp.Fori(0, steps // 4 - 1) as i:
                        for q in range(per, 2 * per):
                            n = base + q
                            array, index, _, _ = SLOTS[n]
                            sp.wait_ge(lo_ready, i * per + (n - RING + 1))
                            sp.dma_start(ring[:, n % RING, :], a[array][i * 4 + index]).then_inc(landed[n % RING], 16)

            sp.dma_start(stream[:, :, XS], a["x"]).then_inc(x_in, 16)
            sp.dma_start(const[:, :], a["const"]).then_inc(const_in, 16)
            for n in range(RING):
                load(n)
            sp.dma_start(early, a["early"]).then_inc(early_in, 16)
            sp.dma_start(stream[:, :, 0:META], a["meta"]).then_inc(meta_in, 16)
            n = RING
            for l in range(2):
                while n < SLOT0[f"expert{l}.0"]:
                    load(n)
                    n += 1
                expert_loads(l)
                n += 2 * CHUNKS
            while n < len(SLOTS):
                load(n)
                n += 1
            sp.wait_ge(stream_ready, 7)
            sp.dma_start(a["out"], stream[:, :, XS]).then_inc(stored, 16)
            sp.wait_ge(stored, 16)

        @block.gpsimd
        def _(pool):
            pool.memset(eps_col, EPS).then_inc(memset_done, 1)
            for x, slots in enumerate(POOL_SLOTS):
                if x % 2 == 0:
                    pool.wait_ge(normed_ready, K * (x + 2))
                    pool.dma_start(desk[:, 0:16 * NKEYS], a[f"subkey{x // 2}"]).then_inc(keys_in, 16)
                pool.wait_ge(lo_ready, slots[0])
                with pool.Fori(0, len(slots) // RING) as i:
                    for q in range(RING):
                        split_lo(pool, slots[q], i)
                for n in slots[len(slots) - len(slots) % RING:]:
                    split_lo(pool, n)
            pool.wait_ge(stream_ready, 5)
            pool.memset(table[:, :], NEG).then_inc(memset_done, 1)
            pool.memset(forget[:, :, :], 0.0).then_inc(memset_done, 1)
            pool.wait_ge(memset_done, 3)
            for dst, src in [(mask2[:, :, :], a["foxmask"]), (w_forget[:, :, :], a["w_forget"]),
                             (pick_head[0:FOXH, :, :], a["pick_head"]), (neg_head[0:FOXH, :, :], a["neg_head"]),
                             (table[0:NB, :], a["table"]), (onehot[0:NB + 1, :], a["onehot"]),
                             (sinks[:, :], a["sinks"].partition_broadcast(P)),
                             (small[0:FOXH, 4:5], a["forget_bias"])]:
                pool.dma_start(dst, src).then_inc(const2_in, 16)
            pool.wait_ge(lo_ready, HEAD_SLOTS[0])
            for n in HEAD_SLOTS:
                split_lo(pool, n)
            pool.wait_ge(table_ready, 2)
            pool.dma_start(a["scratch"].rearrange("q h d -> h q d"),
                           table_out[0:FOXH, :].unsqueeze(1).to_broadcast([FOXH, P, DTAB])).then_inc(table_stored, 16)
            pool.wait_ge(table_stored, 16)
            for t in range(NT):
                n = P * (t + 1)
                for lo, width, first, col in ((META, n, 255 - P * t, 0), (0, META, DX + 255 - P * t, 0)):
                    src = bass.AP(a["scratch"].tensor, first, [[FOXH * DTAB - 1, P], [DTAB, FOXH], [1, width]])
                    pool.dma_start(bias2[:, t, :, lo:lo + width], src).then_inc(bias_in, 16)

        @block.tensor
        def _(pe):
            def norm(n, cols):
                w = W0[f"norm{n}"]
                wait_bank(pe, w)
                width = cols.stop - cols.start
                for k in range(K):
                    pe.wait_ge(squares_ready, K * n + k + 1)
                    mm = pe.matmul(work[:, w % 4, 0:width], cst("inv_d"), normed[:, k, cols], start=(k == 0), stop=(k == K - 1))
                mm.then_inc(bank_done[w % 4], 1)

            def project(w, n, cols):
                width = cols.stop - cols.start
                wait_bank(pe, w)
                pe.wait_ge(lo_ready, n + 1)
                for k in range(K):
                    mm = product3(pe, work[:, w % 4, 0:width], n, k, normed_hi[:, k, cols], normed_lo[:, k, cols], k == 0, k == K - 1)
                mm.then_inc(bank_done[w % 4], 1)

            def project_two(w, n, cols, norm):
                width = cols.stop - cols.start
                wait_bank(pe, w)
                wait_bank(pe, w + 1)
                pe.wait_ge(lo_ready, n + 2)
                for k in range(K):
                    pe.wait_ge(normed_ready, K * norm + k + 1)
                    for x in range(2):
                        mm = product3(pe, work[:, (w + x) % 4, 0:width], n + x, k, normed_hi[:, k, cols], normed_lo[:, k, cols], k == 0, k == K - 1)
                        if k == K - 1:
                            mm.then_inc(bank_done[(w + x) % 4], 1)

            def values(w, n, slots, tiles):
                wait_bank(pe, w)
                pe.wait_ge(lo_ready, n + slots)
                m = n % RING
                assert m + slots <= RING
                for t, lo in enumerate(tiles):
                    for k in range(K):
                        w_hi, w_lo = [x[:, m:m + slots, k * P:(k + 1) * P] for x in (ring_hi, ring_lo)]
                        out = work[:, w % 4, t * slots * P:(t + 1) * slots * P]
                        x_hi, x_lo = [x[:, k * TA + lo:k * TA + lo + P] for x in normed_parts]
                        pe.matmul(out, x_hi, w_hi, start=(k == 0), stop=False)
                        pe.matmul(out, x_hi, w_lo, start=False, stop=False)
                        mm = pe.matmul(out, x_lo, w_hi, start=False, stop=(k == K - 1))
                mm.then_inc(bank_done[w % 4], 1)

            def even():
                w, n = W0["even"], SLOT0["even"]
                for kind, j in EVEN_ITEMS:
                    if kind == "proj":
                        if j == 0:
                            project_two(w, n, XS, 0)
                        elif j > 1:
                            project(w, n, XS)
                        n += 1
                    elif kind == "rot":
                        pe.wait_ge(*freed(W0["even"] + EVEN_ITEMS.index(("proj", j))))
                        wait_bank(pe, w)
                        pe.matmul(work[:, w % 4, 0:S], cst("rot"), qk1raw[:, j % 2, :], start=True, stop=True).then_inc(bank_done[w % 4], 1)
                    else:
                        values(w, n, 2, [META, META + P])
                        n += 2
                    w += 1

            def moba():
                w0 = W0["moba"]
                for i, (kind, u) in enumerate(MOBA_ITEMS):
                    w = w0 + i
                    h, t = u // NT, u % NT
                    wait_bank(pe, w)
                    if kind == "score":
                        pe.matmul(work[:, w % 4, 0:P * (t + 1)], qk1[:, h, t * P:(t + 1) * P], qk1[:, HEADS + h, 0:P * (t + 1)],
                                  start=True, stop=True).then_inc(bank_done[w % 4], 1)
                    elif kind == "turn":
                        pe.wait_ge(probs_ready, u + 1)
                        for b in range(t + 1):
                            mm = pe.transpose(work[:, w % 4, b * P:(b + 1) * P], scores1[:, u % 4, b * P:(b + 1) * P], ident)
                        mm.then_inc(bank_done[w % 4], 1)
                    else:
                        h = u
                        for t in range(NT):
                            pe.wait_ge(*freed(w0 + MOBA_ITEMS.index(("turn", NT * h + t))))
                        pe.wait_ge(*freed(W0["even"] + EVEN_ITEMS.index(("val", h // 2))))
                        pe.matmul(work[:, w % 4, 0:P], val1[:, h, 0, :], prob1[:, h % 2, 0, 0:P], start=True, stop=True)
                        pe.matmul(work[:, w % 4, P:S], val1[:, h, 0, :], prob1[:, h % 2, 0, P:S], start=True, stop=False)
                        pe.matmul(work[:, w % 4, P:S], val1[:, h, 1, :], prob1[:, h % 2, 1, P:S], start=False, stop=True).then_inc(bank_done[w % 4], 1)

            def retention():
                w0, n = W0["ret"], SLOT0["ret"]
                pe.wait_ge(turned_ready, 16)
                for i, (kind, h) in enumerate(RET_ITEMS):
                    w = w0 + i
                    if kind == "gate":
                        project(w, n, XS)
                        n += 1
                        continue
                    wait_bank(pe, w)
                    if kind == "inner":
                        q, k = qk1[:, 2 * HEADS + h, :], qk1[:, 3 * HEADS + h, :]
                        pe.matmul(work[:, w % 4, 0:S], k[:, 0:P], q[:, 0:S], start=True, stop=True)
                        pe.matmul(work[:, w % 4, S:S + P], k[:, P:S], q[:, P:S], start=True, stop=True).then_inc(bank_done[w % 4], 1)
                    elif kind == "outer":
                        pe.wait_ge(inner_ready, h + 1)
                        pe.wait_ge(*freed(W0["even"] + EVEN_ITEMS.index(("val", (HEADS + h) // 2))))
                        v = val1[:, HEADS + h, :, :]
                        pe.matmul(work[:, w % 4, 0:P], v[:, 0, :], inner1[:, h % 2, 0:P], start=True, stop=True)
                        pe.matmul(work[:, w % 4, P:S], v[:, 0, :], inner1[:, h % 2, P:S], start=True, stop=False)
                        pe.matmul(work[:, w % 4, P:S], v[:, 1, :], inner1[:, h % 2, S:S + P], start=False, stop=True).then_inc(bank_done[w % 4], 1)
                    else:
                        pe.wait_ge(retsq_ready, h + 1)
                        pe.matmul(work[:, w % 4, 0:S], cst("inv_head"), retsq[:, h, :], start=True, stop=True).then_inc(bank_done[w % 4], 1)

            def linear(name, hi, lo, width, blocks=K):
                n = SLOT0[name]
                for c in range(K):
                    w = W0[name] + c
                    wait_bank(pe, w)
                    for k in range(blocks):
                        if k % K == 0:
                            pe.wait_ge(lo_ready, n + k // K + 1)
                        mm = product3(pe, work[:, w % 4, 0:width], n + k // K, k % K, hi(k), lo(k), k == 0, k == blocks - 1)
                    mm.then_inc(bank_done[w % 4], 1)
                    n += -(-blocks // K)

            def peer(l):
                n = SLOT0[f"query{l}"]
                for i, (kind, j) in enumerate(QUERY_ITEMS):
                    w = W0[f"query{l}"] + i
                    if kind == "query":
                        if j == 0:
                            project_two(w, n, XS, 2 * l + 1)
                        elif j > 1:
                            project(w, n, XS)
                        n += 1
                    else:
                        t, g = j
                        wait_bank(pe, w)
                        pe.wait_ge(keys_in, 16 * (l + 1))
                        for y in range(4):
                            hp = 4 * g + y
                            pe.wait_ge(*freed(W0[f"query{l}"] + QUERY_ITEMS.index(("query", hp))))
                            mm = pe.matmul(work[:, w % 4, y * P:(y + 1) * P], query[:, hp, t * P:(t + 1) * P], sub_keys[:, hp, :], start=True, stop=True)
                        mm.then_inc(bank_done[w % 4], 1)

                def up(n, w, i=0, slots=4, step=1, coef_item=None):
                    pe.wait_ge(bank_free[w % 4], i * step + w // 4)
                    pe.wait_ge(lo_ready, i * slots + (n + 1))
                    for k in range(K):
                        mm = product3(pe, work[:, w % 4, 0:S], n, k, normed_hi[:, k, XS], normed_lo[:, k, XS], k == 0, k == K - 1)
                        if coef_item is not None and k == K // 2 - 1:
                            coefficients(*coef_item, i)
                    mm.then_inc(bank_done[w % 4], 1)

                def down(n, e, i=0, slots=4):
                    pe.wait_ge(chunk_ready, i * 4 + (l * CHUNKS + e + 1))
                    pe.wait_ge(lo_ready, i * slots + (n + 1))
                    for k in range(K):
                        mm = product3(pe, acc[:, k // 2, (k % 2) * S:(k % 2 + 1) * S], n, k, weighed[:, 0, e % 4, :], weighed[:, 1, e % 4, :],
                                      e == 0 and k % 2 == 0, e == CHUNKS - 1, skip_group_check=True)
                    mm.then_inc(chunk_used, 1)

                def coefficients(w, count, i=0, step=3):
                    pe.wait_ge(bank_free[w % 4], i * step + w // 4)
                    for b in range(2):
                        pe.wait_ge(hots_ready, i * 16 + (2 * count + b + 1))
                        for t in range(4):
                            y = 4 * b + t
                            for x in range(3):
                                at = (2 * count + b) % 4
                                mm = pe.matmul(work[:, w % 4, y * HALF:(y + 1) * HALF], hot_second[at][:, :, t], hot_gated[at][:, x, :, t], start=(x == 0), stop=(x == 2))
                        mm.then_inc(*((hots_read, 1) if b == 0 else (bank_done[w % 4], 1)))

                built = l * 2 * S // 8
                for x, (kind, e, h, steps) in enumerate(SEGMENTS):
                    if x == 1:
                        for t in range(NT):
                            w = W0[f"turn{l}"] + t
                            wait_bank(pe, w)
                            pe.wait_ge(picks_ready, NT * l + t + 1)
                            for y in range(3):
                                mm = pe.transpose(work[:, w % 4, y * P:(y + 1) * P], chosen[:, t, y, :], ident)
                            mm.then_inc(bank_done[w % 4], 1)
                    w0, base, per, step = W0[f"expert{l}.{x}"], SLOT0[f"expert{l}.{x}"], 4 * SLOTS_OF[kind], ITEMS_OF[kind]

                    def four(at, i):
                        for j in range(at, at + 4):
                            n = base + j * SLOTS_OF[kind]
                            if kind == "upcoef":
                                up(n, w0 + step * j, i, per, step, (w0 + step * j + 1, built + 2 * j))
                                coefficients(w0 + step * j + 2, built + 2 * j + 1, i)
                            elif h is not None:
                                up(n, w0 + step * j, i, per, step)
                                n += 1
                            if e is not None:
                                down(n, e + j, i, per)

                    head = 4 if e == 0 else 0
                    tail = 4 if e is not None and e + steps == CHUNKS else 0
                    if head:
                        four(0, 0)
                    if steps - head - tail:
                        with pe.Fori(0, (steps - head - tail) // 4) as i:
                            four(head, i)
                    if tail:
                        four(steps - tail, 0)
                    if kind == "upcoef":
                        built += S // 8

            def odd():
                project_two(W0["odd"], SLOT0["odd"], XS, 2)
                for i in range(2, len(ODD_ITEMS)):
                    project(W0["odd"] + i, SLOT0["odd"] + i, XS)

            def feed_forward(x, n_norm, cols):
                project_two(W0[f"ffn{x}"], SLOT0[f"ffn{x}"], cols, n_norm - 1)
                for i in range(2, len(FFN_ITEMS)):
                    project(W0[f"ffn{x}"] + i, SLOT0[f"ffn{x}"] + i, cols)
                pe.wait_ge(ff_ready, FC * x)
                linear(f"ffn{x}out", lambda k: ff_hi[:, k, cols], lambda k: ff_lo[:, k, cols], cols.stop - cols.start, FC)

            def mix():
                w0, n = W0["mix"], SLOT0["mix"]
                for i, (kind, j) in enumerate(MIX_ITEMS):
                    w = w0 + i
                    cols = XS if j < 4 or 8 <= j < 12 else ALL
                    width = cols.stop - cols.start
                    if kind == "forget":
                        pe.wait_ge(const2_in, 16 * 8)
                        wait_bank(pe, w)
                        for k in range(K):
                            mm = pe.matmul(work[0:FOXH, w % 4, 0:TA], w_forget[:, k, :], normed[:, k, ALL], start=(k == 0), stop=(k == K - 1))
                        mm.then_inc(bank_done[w % 4], 1)
                    elif kind == "proj":
                        if j == 0:
                            project_two(w, n, cols, 5)
                        elif j > 1:
                            project(w, n, cols)
                        n += 1
                    elif kind == "mean":
                        wait_bank(pe, w)
                        pe.wait_ge(qksq_ready, j + 1)
                        pe.matmul(work[:, w % 4, 0:width], cst("inv_half"), qk2sq[:, j % 2, 0:width], start=True, stop=True).then_inc(bank_done[w % 4], 1)
                    elif kind == "val":
                        values(w, n, 2, [0, P])
                    elif kind == "lastval":
                        values(w, n, 2, [S])
                        n += 2
                    elif kind == "swaval":
                        values(w, n, 1, [0, P, S])
                        n += 1
                    else:
                        wait_bank(pe, w)
                        lo, hi = ((0, DX), (DX, DTAB))[j]
                        pe.matmul(work[0:FOXH, w % 4, 0:hi - lo], table[0:NB + 1, :], onehot[0:NB + 1, lo:hi], start=True, stop=True).then_inc(bank_done[w % 4], 1)

            def gates():
                for i in range(2 * K):
                    project(W0["gates"] + i, SLOT0["gates"] + i, XS)

            def attend(name, n_before):
                w0 = W0[name]
                fox = name == "fox"
                pe.wait_ge(qk2_ready, QK2)
                if fox:
                    pe.wait_ge(forget_ready, 1)
                for i, (kind, u) in enumerate(FOX_ITEMS):
                    w = w0 + i
                    h, t = u // NT, u % NT
                    keys = META + P * (t + 1)
                    half = slice((h % 2) * HD2, (h % 2 + 1) * HD2)
                    wait_bank(pe, w)
                    if kind == "score":
                        q = qk2[half, (0 if fox else 8) + h // 2, t * P:(t + 1) * P]
                        kk = qk2[half, 4 + h // 2 if fox else 12 + h // 4, 0:keys]
                        mm = pe.matmul(work[:, w % 4, 0:keys], q, kk, start=True, stop=not fox)
                        if fox:
                            pe.matmul(work[:, w % 4, 0:keys], forget[0:FOXH, 0, META + t * P:META + (t + 1) * P], pick_head[0:FOXH, h, 0:keys],
                                      start=False, stop=False)
                            mm = pe.matmul(work[:, w % 4, 0:keys], neg_head[0:FOXH, h, :], forget[0:FOXH, 0, 0:keys], start=False, stop=True)
                        mm.then_inc(bank_done[w % 4], 1)
                    elif kind == "turn":
                        pe.wait_ge(probs_ready, n_before + u + 1)
                        for b in range(t + 2):
                            lo, hi = b * P, min((b + 1) * P, keys)
                            mm = pe.transpose(work[0:hi - lo, w % 4, b * P:(b + 1) * P], scores2[:, u % 4, lo:hi], ident)
                        mm.then_inc(bank_done[w % 4], 1)
                    else:
                        h = u
                        half = slice((h % 2) * HD2, (h % 2 + 1) * HD2)
                        for t in range(NT):
                            pe.wait_ge(*freed(w0 + FOX_ITEMS.index(("turn", NT * h + t))))
                        pe.wait_ge(*freed(W0["mix"] + MIX_ITEMS.index(("swaval", 0))))
                        for t in range(NT):
                            keys = META + P * (t + 1)
                            for b in range(t + 2):
                                rows = min(P, keys - b * P)
                                v = val2[0:rows, h // 2, b, (h % 2) * HD2:(h % 2 + 1) * HD2] if fox else \
                                    val2[0:rows, 4, b, (h // 4) * HD2:(h // 4 + 1) * HD2]
                                mm = pe.matmul(work[half, w % 4, t * P:(t + 1) * P], v, prob2[0:rows, h % 2, b, t, :],
                                               start=(b == 0), stop=(b == t + 1))
                        mm.then_inc(bank_done[w % 4], 1)

            def branch():
                pe.wait_ge(*freed(W0["fox"] + len(FOX_ITEMS) - 1))
                pe.wait_ge(*freed(W0["swa"] + len(FOX_ITEMS) - 1))
                for c in range(K):
                    n = SLOT0["branch"] + c
                    for x in range(2):
                        w = W0["branch"] + 2 * c + x
                        wait_bank(pe, w)
                        pe.wait_ge(lo_ready, n + 1)
                        for k in range(4):
                            mm = product3(pe, work[:, w % 4, 0:S], n, 4 * x + k, att2_hi[:, x, k, :], att2_lo[:, x, k, :], k == 0, k == 3)
                        mm.then_inc(bank_done[w % 4], 1)

            pe.wait_ge(const_in, 16)
            norm(0, XS)
            even()
            retention()
            moba()
            for h in range(HEADS):
                pe.wait_ge(*freed(W0["moba"] + MOBA_ITEMS.index(("mix", h))))
            pe.wait_ge(mixed_ready, HEADS)
            linear("evenout", lambda k: normed_hi[:, k, XS], lambda k: normed_lo[:, k, XS], S)
            norm(1, XS)
            peer(0)
            norm(2, XS)
            odd()
            pe.wait_ge(zy_ready, K)
            linear("oddout", lambda k: z2_hi[:, k, :], lambda k: z2_lo[:, k, :], S)
            norm(3, XS)
            peer(1)
            norm(4, XS)
            norm(5, ALL)
            feed_forward(1, 5, ALL)
            norm(6, ALL)
            mix()
            attend("fox", HEADS * NT)
            attend("swa", HEADS * NT + FOXH * NT)
            gates()
            branch()
            pe.wait_ge(branch_ready, K)
            linear("mixout", lambda k: normed_hi[:, k, XS], lambda k: normed_lo[:, k, XS], S)
            norm(7, XS)
            feed_forward(2, 7, XS)

        @block.scalar
        def _(act):
            ahead = [0]

            def split_to(n):
                while ahead[0] < len(SLOTS) and ahead[0] <= n + AHEAD:
                    split_hi(act, ahead[0])
                    ahead[0] += 1

            def norm(n, cols, written):
                w = W0[f"norm{n}"]
                width = cols.stop - cols.start
                for k in range(K):
                    act.wait_ge(*written(k))
                    act.activation(normed[:, k, cols], stream[:, k, cols], ACT.Square).then_inc(squares_ready, 1)
                if n == 0:
                    split_to(-1)
                act.wait_ge(*done(w))
                act.activation(rstd[:, 0:width], work[:, w % 4, 0:width], ACT.Sqrt, bias=eps_col).then_inc(bank_free[w % 4], 1)
                if n != 4:
                    for k in range(K):
                        x = K * (n - (n > 4)) + k + 1
                        act.wait_ge(plain_ready, x)
                        act.activation(normed_hi[:, k, cols], normed[:, k, cols], ACT.Copy).then_inc(lead_ready, 1)

            def split_all(name, widths=1):
                for c in range(K):
                    split_to(SLOT0[name] + (c + 1) * widths - 1)

            def empty(w, dst, src, func=ACT.Copy):
                act.wait_ge(*done(w))
                act.activation(dst, src, func).then_inc(bank_free[w % 4], 1)

            def even():
                n = SLOT0["even"]
                for i, (kind, j) in enumerate(EVEN_ITEMS):
                    w = W0["even"] + i
                    if kind != "rot":
                        n += 2 if kind == "val" else 1
                        split_to(n - 1)
                    if kind == "proj":
                        if j >= 2:
                            act.wait_ge(*done(W0["even"] + EVEN_ITEMS.index(("rot", j - 2))))
                            act.wait_ge(turned_ready, j - 1)
                        empty(w, qk1raw[:, j % 2, :], work[:, w % 4, 0:S])
                    elif kind == "val":
                        empty(w, val1[:, 2 * j:2 * j + 2, :, :].rearrange("p h t d -> p t h d"), work[:, w % 4, :].rearrange("p (t h d) -> p t h d", t=NT, h=2))

            def softmax(items, w0, name, scores, n_before, width_of, turn_copy):
                for i, (kind, u) in enumerate(items):
                    w = w0 + i
                    if kind == "score":
                        act.wait_ge(scores_ready, n_before + u + 1)
                        row = scores[:, u % 4, 0:width_of(u)]
                        act.activation(row, row, ACT.Exp, bias=small[:, 8 + u % 4:9 + u % 4], accum_out=small[:, 12 + u % 4:13 + u % 4]).then_inc(exp_ready, 1)
                    elif kind == "turn":
                        turn_copy(w, u, i)

            def moba():
                w0 = W0["moba"]

                def turn_copy(w, u, i):
                    h, t = u // NT, u % NT
                    if h >= 2:
                        act.wait_ge(*done(w0 + MOBA_ITEMS.index(("mix", h - 2))))
                    empty(w, prob1[:, h % 2, 0:t + 1, t * P:(t + 1) * P], work[:, w % 4, 0:(t + 1) * P].rearrange("p (b q) -> p b q", q=P))

                softmax(MOBA_ITEMS, w0, "moba", scores1, 0, lambda u: P * (u % NT + 1), turn_copy)

            def retention():
                n = SLOT0["ret"]
                for i, (kind, h) in enumerate(RET_ITEMS):
                    w = W0["ret"] + i
                    if kind == "gate":
                        split_to(n)
                        n += 1
                        empty(w, silu1[:, h, :], work[:, w % 4, 0:S], ACT.Silu)
                    elif kind == "outer":
                        empty(w, ret1[:, h, :], work[:, w % 4, 0:S])
                        act.wait_ge(*freed(w))
                        act.activation(retsq[:, h, :], ret1[:, h, :], ACT.Square).then_inc(retsq_ready, 1)
                    elif kind == "mean":
                        act.wait_ge(*done(w))
                        act.activation(retms[:, h, :], work[:, w % 4, 0:S], ACT.Sqrt, bias=eps_col).then_inc(bank_free[w % 4], 1)

            def peer(l):
                n = SLOT0[f"query{l}"]
                for i, (kind, j) in enumerate(QUERY_ITEMS):
                    w = W0[f"query{l}"] + i
                    if kind == "query":
                        split_to(n)
                        n += 1
                        empty(w, query[:, j, :], work[:, w % 4, 0:S])
                    else:
                        empty(w, sub[:, 4 * j[0] + j[1], :], work[:, w % 4, :])

                def gate_exp(t):
                    act.wait_ge(gate_diff_ready, NT * l + t + 1)
                    act.activation(chosen[:, t, 2, :], pair[:, t, :], ACT.Exp).then_inc(gate_exp_ready, 1)

                def gelu(w, h, i=0, step=1):
                    act.wait_ge(bank_done[w % 4], i * step + (w // 4 + 1))
                    if h >= HELD:
                        act.wait_ge(chunk_ready, i * 4 + (l * CHUNKS + h - HELD + 1))
                    else:
                        act.wait_ge(stream_ready, 2 * l + 1)
                    act.activation(hidden[:, bass.ds(i * 4 + h % HELD, 1), :].squeeze(1) if not isinstance(i, int) else hidden[:, h % HELD, :],
                                   work[:, w % 4, 0:S], ACT.Gelu).then_inc(bank_free[w % 4], 1)

                def store_coef(w, at, i=0, step=3):
                    act.wait_ge(bank_done[w % 4], i * step + (w // 4 + 1))
                    act.activation(arena[:, bass.ds(i * (64 * HALF) + (HELD * S + at * HALF), 8 * HALF)], work[:, w % 4, :], ACT.Copy).then_inc(bank_free[w % 4], 1)

                for x, (kind, e, h, steps) in enumerate(SEGMENTS):
                    if x == 1:
                        gate_exp(1)
                        for t in range(NT):
                            w = W0[f"turn{l}"] + t
                            act.wait_ge(*done(w))
                            act.activation(gate_rest[:, t * P:(t + 1) * P], work[:, w % 4, 2 * P:3 * P], ACT.Copy)
                            act.activation(picks[:, 0:2, t * P:(t + 1) * P], work[:, w % 4, 0:2 * P].rearrange("p (x q) -> p x q", x=2), ACT.Copy).then_inc(bank_free[w % 4], 1)
                    w0, base, slots, step = W0[f"expert{l}.{x}"], SLOT0[f"expert{l}.{x}"], SLOTS_OF[kind], ITEMS_OF[kind]
                    if kind == "upcoef" and x > 1:
                        act.wait_ge(chunk_ready, l * CHUNKS + HALF)

                    def four(at, i):
                        for j in range(at, at + 4):
                            for y in range(slots):
                                n = base + j * slots + AHEAD + y
                                split_hi(act, n, i, 4 * slots, step)
                            if kind == "upcoef":
                                store_coef(w0 + step * j + 1, 16 * j, i)
                            if h is not None:
                                gelu(w0 + step * j, h + j, i, step)
                            if kind == "upcoef":
                                store_coef(w0 + step * j + 2, 16 * j + 8, i)

                    four(0, 0)
                    if x == 0:
                        four(4, 0)
                        gate_exp(0)
                        four(8, 0)
                        with act.Fori(0, steps // 4 - 3) as i:
                            four(12, i)
                    else:
                        with act.Fori(0, steps // 4 - 1) as i:
                            four(4, i)
                ahead[0] = SLOT0[f"expert{l}.{len(SEGMENTS) - 1}"] + SEGMENTS[-1][3] + AHEAD

            def odd():
                for i, (kind, c) in enumerate(ODD_ITEMS):
                    split_to(SLOT0["odd"] + i)
                    if kind == "cgate":
                        w = W0["odd"] + i
                        if c >= 2:
                            act.wait_ge(*freed(W0["odd"] + ODD_ITEMS.index(("value", c - 2))))
                        empty(w, cg[:, c % 2, :], work[:, w % 4, 0:S])

            def feed_forward(x, cols):
                width = cols.stop - cols.start
                for i, (kind, c) in enumerate(FFN_ITEMS):
                    split_to(SLOT0[f"ffn{x}"] + i)
                    if kind == "ffgate":
                        w = W0[f"ffn{x}"] + i
                        if c >= 2:
                            act.wait_ge(ff_ready, FC * (x - 1) + c - 1)
                        empty(w, ff_silu[:, c % 2, 0:width], work[:, w % 4, 0:width], ACT.Silu)

            def mix():
                w0, n = W0["mix"], SLOT0["mix"]
                for i, (kind, j) in enumerate(MIX_ITEMS):
                    w = w0 + i
                    cols = XS if j < 4 or 8 <= j < 12 else ALL
                    width = cols.stop - cols.start
                    if kind in ("proj", "val", "swaval"):
                        n += 2 if kind == "val" else 1
                        split_to(n - 1)
                    if kind == "forget":
                        act.wait_ge(forget_in, 1)
                        act.activation(forget[0:FOXH, 2, :], forget[0:FOXH, 1, :], ACT.Abs).then_inc(own.sem, own.up())
                        act.wait_ge(own.sem, own.n)
                        act.activation(forget[0:FOXH, 3, :], forget[0:FOXH, 2, :], ACT.Exp, scale=-1.0).then_inc(own.sem, own.up())
                        act.wait_ge(own.sem, own.n)
                        act.activation(forget[0:FOXH, 4, :], forget[0:FOXH, 3, :], ACT.Ln, bias=1.0).then_inc(forget_out, 1)
                    elif kind == "proj":
                        if j >= 2:
                            act.wait_ge(qk2_ready, j - 1)
                        empty(w, qk2raw[:, j % 2, 0:width], work[:, w % 4, 0:width])
                        act.wait_ge(*freed(w))
                        if j >= 2:
                            act.wait_ge(*done(w0 + MIX_ITEMS.index(("mean", j - 2))))
                        act.activation(qk2sq[:, j % 2, 0:width], qk2raw[:, j % 2, 0:width], ACT.Square).then_inc(qksq_ready, 1)
                    elif kind == "mean":
                        act.wait_ge(*done(w))
                        act.activation(qk2ms[:, j % 2, 0:width], work[:, w % 4, 0:width], ACT.Sqrt, bias=eps_col).then_inc(bank_free[w % 4], 1)
                    elif kind == "val":
                        act.wait_ge(*done(w))
                        act.activation(val2[:, 2 * j:2 * j + 2, 0:2, :].rearrange("p h t d -> p t h d"), work[:, w % 4, :].rearrange("p (t h d) -> p t h d", t=2, h=2), ACT.Copy).then_inc(bank_free[w % 4], 1)
                    elif kind == "lastval":
                        empty(w, val2[0:META, 2 * j:2 * j + 2, 2, :], work[0:META, w % 4, 0:S].rearrange("p (h d) -> p h d", h=2))
                    elif kind == "swaval":
                        act.wait_ge(*done(w))
                        act.activation(val2[:, 4, 0:2, :], work[:, w % 4, 0:S].rearrange("p (t d) -> p t d", t=2), ACT.Copy)
                        act.activation(val2[0:META, 4, 2, :], work[0:META, w % 4, S:S + P], ACT.Copy).then_inc(bank_free[w % 4], 1)

            def gates():
                act.wait_ge(*freed(W0["gates"] - 1))
                for i in range(2 * K):
                    w = W0["gates"] + i
                    split_to(SLOT0["gates"] + i)
                    empty(w, gate2[:, i, :], work[:, w % 4, 0:S], ACT.Sigmoid)

            def attend(name, n_before):
                w0 = W0[name]
                fox = name == "fox"

                def turn_copy(w, u, i):
                    h, t = u // NT, u % NT
                    if h >= 2:
                        act.wait_ge(*done(w0 + FOX_ITEMS.index(("mix", h - 2))))
                    act.wait_ge(*done(w))
                    act.activation(prob2[:, h % 2, 0:t + 1, t, :], work[:, w % 4, 0:(t + 1) * P].rearrange("p (b q) -> p b q", q=P), ACT.Copy)
                    act.activation(prob2[0:META, h % 2, t + 1, t, :], work[0:META, w % 4, (t + 1) * P:(t + 2) * P], ACT.Copy).then_inc(bank_free[w % 4], 1)

                softmax(FOX_ITEMS, w0, name, scores2, n_before, lambda u: META + P * (u % NT + 1) + (0 if fox else 1), turn_copy)

            act.wait_ge(memset_done, 1)
            after = lambda name: lambda k: freed(W0[name] + k)
            norm(0, XS, lambda k: (x_in, 16))
            even()
            retention()
            moba()
            split_all("evenout")
            norm(1, XS, after("evenout"))
            peer(0)
            norm(2, XS, lambda k: (stream_block, k + 1))
            odd()
            split_all("oddout")
            norm(3, XS, after("oddout"))
            peer(1)
            norm(4, XS, lambda k: (stream_block, K + k + 1))
            act.wait_ge(meta_in, 16)
            norm(5, ALL, lambda k: (stream_block, 2 * K + k + 1))
            feed_forward(1, ALL)
            split_all("ffn1out", 3)
            norm(6, ALL, after("ffn1out"))
            mix()
            attend("fox", HEADS * NT)
            attend("swa", HEADS * NT + FOXH * NT)
            gates()
            split_all("branch")
            split_all("mixout")
            norm(7, XS, after("mixout"))
            feed_forward(2, XS)
            split_all("ffn2out", 3)

        @block.vector
        def _(dve):
            def step():
                dve.wait_ge(vec.sem, vec.n)

            ahead = [0]

            def split_to(n):
                while ahead[0] < len(SLOTS) and ahead[0] <= n + AHEAD:
                    if not any(ahead[0] in r for r in POOL_SLOTS + [HEAD_SLOTS]):
                        if ahead[0] == HEAD_SLOTS[-1] + 1:
                            dve.wait_ge(lo_ready, ahead[0])
                        split_lo(dve, ahead[0])
                    ahead[0] += 1

            def parts(k, cols, src, ready, hi=normed_hi, lo=normed_lo):
                dve.tensor_copy(hi[:, k, cols], src).then_inc(vec.sem, vec.up())
                step()
                dve.tensor_tensor(lo[:, k, cols], src, hi[:, k, cols].bitcast(F32), ALU.subtract).then_inc(ready, 1)

            def norm(n, cols, dst=normed):
                w = W0[f"norm{n}"]
                width = cols.stop - cols.start
                dve.wait_ge(*freed(w))
                dve.reciprocal(rstd[:, 0:width], rstd[:, 0:width]).then_inc(vec.sem, vec.up())
                step()
                first = K * (n - (n > 4))
                for k in range(K + 1):
                    if k < K:
                        dve.scalar_tensor_tensor(dst[:, k, cols], stream[:, k, cols], gains[:, n, k:k + 1], rstd[:, 0:width], ALU.mult, ALU.mult
                                                 ).then_inc(stream_block if n == 4 else plain_ready, 1)
                    if k and n != 4:
                        dve.wait_ge(lead_ready, first + k)
                        dve.tensor_tensor(normed_lo[:, k - 1, cols], normed[:, k - 1, cols], normed_hi[:, k - 1, cols].bitcast(F32), ALU.subtract
                                          ).then_inc(normed_ready, 1)

            def even():
                n = SLOT0["even"]
                for i, (kind, j) in enumerate(EVEN_ITEMS):
                    w = W0["even"] + i
                    if kind != "rot":
                        n += 2 if kind == "val" else 1
                        split_to(n - 1)
                    if kind == "rot":
                        dve.wait_ge(*freed(W0["even"] + EVEN_ITEMS.index(("proj", j))))
                        if j >= 2:
                            dve.wait_ge(turned_ready, j - 1)
                        dve.tensor_tensor(qk1[:, j, :], qk1raw[:, j % 2, :], cos, ALU.mult).then_inc(vec.sem, vec.up())
                        dve.wait_ge(*done(w))
                        dve.tensor_tensor(rot_tmp[:, j % 2, :], work[:, w % 4, 0:S], sin, ALU.mult).then_inc(bank_free[w % 4], 1)
                        step()
                        dve.wait_ge(*freed(w))
                        dve.tensor_tensor(qk1[:, j, :], qk1[:, j, :], rot_tmp[:, j % 2, :], ALU.add).then_inc(turned_ready, 1)

            def soft_rows(items, name, scores, n_before, addend, scale, width_of, sink, out):
                w0 = W0[name]
                normalised = [0]

                def normalise_to(last):
                    while normalised[0] <= last:
                        u = normalised[0]
                        dve.wait_ge(exp_ready, n_before + u + 1)
                        total = small[:, 12 + u % 4:13 + u % 4]
                        dve.reciprocal(total, total).then_inc(vec.sem, vec.up())
                        step()
                        row = scores[:, u % 4, 0:width_of(u)]
                        dve.tensor_scalar(row, row, total, None, ALU.mult).then_inc(probs_ready, 1)
                        normalised[0] += 1

                for i, (kind, u) in enumerate(items):
                    w = w0 + i
                    n = width_of(u)
                    row = scores[:, u % 4, 0:n]
                    if kind == "score":
                        normalise_to(u - 2)
                        if u >= 4:
                            dve.wait_ge(*done(w0 + items.index(("turn", u - 4))))
                        dve.wait_ge(*done(w))
                        dve.scalar_tensor_tensor(row, work[:, w % 4, 0:n], scale, addend(u), ALU.mult, ALU.add).then_inc(bank_free[w % 4], 1)
                        if sink:
                            h = u // NT
                            dve.tensor_copy(scores[:, u % 4, n:n + 1], sinks[:, h:h + 1]).then_inc(vec.sem, vec.up())
                            step()
                            row = scores[:, u % 4, 0:n + 1]
                        dve.wait_ge(*freed(w))
                        if n_before + u >= 4:
                            dve.wait_ge(exp_ready, n_before + u - 3)
                        dve.tensor_reduce(small[:, 8 + u % 4:9 + u % 4], row, AX.X, ALU.max, negate=True).then_inc(scores_ready, 1)
                    elif kind == "turn":
                        normalise_to(u)
                    else:
                        dve.wait_ge(*done(w))
                        out(w, u)

            def moba():
                def out(w, h):
                    dve.tensor_copy(normed_hi[:, h, XS], work[:, w % 4, 0:S]).then_inc(vec.sem, vec.up())
                    step()
                    dve.tensor_tensor(normed_lo[:, h, XS], work[:, w % 4, 0:S], normed_hi[:, h, XS].bitcast(F32), ALU.subtract).then_inc(bank_free[w % 4], 1)
                    dve.wait_ge(*freed(W0["ret"] + RET_ITEMS.index(("gate", h))))
                    dve.tensor_tensor(ret1[:, h, :], ret1[:, h, :], silu1[:, h, :], ALU.mult).then_inc(vec.sem, vec.up())
                    step()
                    parts(HEADS + h, XS, ret1[:, h, :], mixed_ready)

                soft_rows(MOBA_ITEMS, "moba", scores1, 0, lambda u: cst("causal")[:, (1 - u % NT) * P:S], P ** -0.5,
                          lambda u: P * (u % NT + 1), False, out)

            def retention():
                n = SLOT0["ret"]
                for i, (kind, h) in enumerate(RET_ITEMS):
                    w = W0["ret"] + i
                    if kind == "gate":
                        split_to(n)
                        n += 1
                    elif kind == "mean":
                        dve.wait_ge(*freed(w))
                        dve.reciprocal(retms[:, h, :], retms[:, h, :]).then_inc(vec.sem, vec.up())
                        step()
                        dve.tensor_tensor(ret1[:, h, :], ret1[:, h, :], retms[:, h, :], ALU.mult).then_inc(vec.sem, vec.up())
                        step()
                    elif kind == "inner":
                        dve.wait_ge(*done(w))
                        if h >= 2:
                            dve.wait_ge(*done(W0["ret"] + RET_ITEMS.index(("outer", h - 2))))
                        dve.tensor_tensor(inner1[:, h % 2, :], work[:, w % 4, 0:384], decay[:, h, :], ALU.mult).then_inc(vec.sem, vec.up())
                        step()
                        dve.engine_nop().then_inc(bank_free[w % 4], 1)
                        dve.engine_nop().then_inc(inner_ready, 1)
            def residual(name, n, cols, scale=1.0, slots=1):
                width = cols.stop - cols.start
                for c in range(K):
                    w = W0[name] + c
                    split_to(SLOT0[name] + (c + 1) * slots - 1)
                    dve.wait_ge(*done(w))
                    dve.scalar_tensor_tensor(stream[:, c, cols], work[:, w % 4, 0:width], scale, stream[:, c, cols], ALU.mult, ALU.add).then_inc(bank_free[w % 4], 1)
                for c in range(K - 4, K):
                    dve.wait_ge(*freed(W0[name] + c))
                dve.engine_nop().then_inc(stream_ready, 1)

            def top16(dst, at, src, tmp, n):
                for r in range(n):
                    ins = dve.max(dst(r)[:, 0:8], src(r))
                ins.then_inc(vec.sem, vec.up())
                step()
                for r in range(n):
                    dve.max_index(at(r)[:, 0:8], dst(r)[:, 0:8], src(r))
                    ins = dve.match_replace(tmp(r), dst(r)[:, 0:8], src(r), -3.0e38)
                ins.then_inc(vec.sem, vec.up())
                step()
                for r in range(n):
                    ins = dve.max(dst(r)[:, 8:16], tmp(r))
                ins.then_inc(vec.sem, vec.up())
                step()
                for r in range(n):
                    ins = dve.max_index(at(r)[:, 8:16], dst(r)[:, 8:16], tmp(r))
                return ins

            def choose(l):
                u32 = lambda v: v.bitcast(U32)
                for g in range(4):
                    for t in range(NT):
                        dve.wait_ge(*freed(W0[f"query{l}"] + QUERY_ITEMS.index(("score", (t, g)))))
                        top16(lambda r: best[:, t, 4 * g + r, :], lambda r: u32(best_at[:, t, 4 * g + r, :]),
                              lambda r: sub[:, 4 * t + g, r * P:(r + 1) * P], lambda r: sub2[:, r * P:(r + 1) * P], 4).then_inc(vec.sem, vec.up())
                        step()
                for t in range(NT):
                    dve.tensor_copy(best_f[:, t, :, :], u32(best_at[:, t, :, :])).then_inc(vec.sem, vec.up())
                    hp = best[:, t, :, :].rearrange("p (h x) k -> p h x k", x=2)
                    for lo, i0, rows, width in ((0, 0, 4, TOPK), (4 * TOPK, 4, TOPK - 4, 4)):
                        part = cand[:, :, lo:lo + rows * width].rearrange("p h (i j) -> p h i j", j=width)
                        part_shape = [P, PH, rows, width]
                        dve.tensor_tensor(part, hp[:, :, 0, i0:i0 + rows].unsqueeze(3).to_broadcast(part_shape),
                                          hp[:, :, 1, 0:width].unsqueeze(2).to_broadcast(part_shape), ALU.add).then_inc(vec.sem, vec.up())
                    shape = [P, PH, TOPK, TOPK]
                    step()
                    top = pair[:, t, :].rearrange("p (h k) -> p h k", k=TOPK)
                    at = pair_at.rearrange("p (h k) -> p h k", k=TOPK)
                    top16(lambda r: top[:, r, :], lambda r: u32(at[:, r, :]), lambda r: cand[:, r, 0:CANDS], lambda r: cand2[:, r, 0:CANDS], PH).then_inc(vec.sem, vec.up())
                    step()
                    dve.tensor_copy(psum8[:, t, 1, :], top[:, :, 0]).then_inc(vec.sem, vec.up())
                    step()
                    dve.tensor_tensor(top, top, psum8[:, t, 1, :].unsqueeze(2).to_broadcast([P, PH, TOPK]), ALU.subtract).then_inc(gate_diff_ready, 1)
                    for y, (op, amount) in enumerate(((ALU.logical_shift_right, 4), (ALU.bitwise_and, TOPK - 1), (ALU.logical_shift_right, 2), (ALU.bitwise_and, 3))):
                        dve.tensor_scalar(u32(pair_ab[:, y, :]), u32(pair_at), amount, None, op).then_inc(vec.sem, vec.up())
                    step()
                    dve.tensor_copy(pair_f[:, :, :], u32(pair_ab[:, :, :])).then_inc(vec.sem, vec.up())
                    step()
                    dve.scalar_tensor_tensor(pair_ab[:, 0, :], pair_f[:, 2, :], 4.0 - TOPK, pair_f[:, 0, :], ALU.add, ALU.subtract).then_inc(vec.sem, vec.up())
                    dve.tensor_tensor(pair_ab[:, 1, :], pair_f[:, 3, :], pair_f[:, 1, :], ALU.subtract).then_inc(vec.sem, vec.up())
                    step()
                    for x in range(2):
                        dve.scalar_tensor_tensor(pair_ab[:, 2 + x, :], pair_f[:, 2, :], float(TOPK), pair_ab[:, x, :], ALU.is_ge, ALU.mult).then_inc(vec.sem, vec.up())
                    step()
                    dve.tensor_tensor(pair_f[:, 0:2, :], pair_f[:, 0:2, :], pair_ab[:, 2:4, :], ALU.add).then_inc(vec.sem, vec.up())
                    step()
                    for x in range(2):
                        ranks = iota[:, 0:TOPK].unsqueeze(1).to_broadcast([P, PH * TOPK, TOPK])
                        dve.tensor_tensor(eq[:, :, :], pair_f[:, x, :].unsqueeze(2).to_broadcast([P, PH * TOPK, TOPK]), ranks, ALU.is_equal).then_inc(vec.sem, vec.up())
                        step()
                        keys = best_f[:, t, :, :].rearrange("p (h x) k -> p h x k", x=2)[:, :, x, :]
                        dve.tensor_tensor(ev[:, :, :].rearrange("p (h k) r -> p h k r", k=TOPK), eq[:, :, :].rearrange("p (h k) r -> p h k r", k=TOPK),
                                          keys.unsqueeze(2).to_broadcast(shape), ALU.mult).then_inc(vec.sem, vec.up())
                        step()
                        dve.tensor_reduce(chosen[:, t, x, :], ev[:, :, :], AX.X, ALU.add).then_inc(vec.sem, vec.up())
                        step()
                    gate = chosen[:, t, 2, :].rearrange("p (h k) -> p h k", k=TOPK)
                    dve.wait_ge(gate_exp_ready, NT * l + t + 1)
                    dve.tensor_reduce(psum8[:, t, 0, :], gate, AX.X, ALU.add).then_inc(vec.sem, vec.up())
                    step()
                    dve.reciprocal(psum8[:, t, 0, :], psum8[:, t, 0, :]).then_inc(vec.sem, vec.up())
                    step()
                    dve.tensor_tensor(gate, gate, psum8[:, t, 0, :].unsqueeze(2).to_broadcast([P, PH, TOPK]), ALU.mult).then_inc(picks_ready, 1)

            def peer(l):
                split_to(SLOT0[f"query{l}"])
                choose(l)
                for t in range(NT):
                    dve.wait_ge(*freed(W0[f"turn{l}"] + t))
                for x in range(2, 5):
                    dve.tensor_copy(picks[:, x, :], gate_rest).then_inc(vec.sem, vec.up())
                    step()
                    if x < 4:
                        dve.tensor_tensor(gate_rest, gate_rest, picks[:, x, :], ALU.subtract).then_inc(vec.sem, vec.up())
                        step()
                c0 = l * CHUNKS

                def one_hots(count, tok, h0, w, i, pace=3):
                    for b in range(2):
                        if w is not None:
                            if b == 0:
                                dve.wait_ge(hots_read, i * 8 + (count - 1))
                            else:
                                dve.wait_ge(bank_done[w % 4], i * pace + (w // 4 + 1))
                        of = lambda x, n: picks[:, x:x + n, bass.ds(i * 64 + (tok + 4 * b), 4)]
                        at = (2 * count + b) % 4
                        first, second = hot_first[at], hot_second[at]
                        dve.tensor_tensor(first, keys4[:, h0:h0 + HALF, :], of(0, 1).to_broadcast([P, HALF, 4]), ALU.is_equal).then_inc(hots_used, 1)
                        dve.tensor_tensor(second, keys4[:, :, :], of(1, 1).to_broadcast([P, P, 4]), ALU.is_equal)
                        dve.wait_ge(hots_used, i * 16 + (2 * count + b + 1))
                        shape = [P, 3, HALF, 4]
                        dve.tensor_tensor(hot_gated[at], first.unsqueeze(1).to_broadcast(shape), of(2, 3).unsqueeze(2).to_broadcast(shape), ALU.mult).then_inc(hots_ready, 1)

                def weigh(e, i):
                    if l or e >= 4:
                        dve.wait_ge(chunk_used, i * 4 + (c0 + e - 3))
                    if isinstance(i, int):
                        hid, co = hidden[:, e % HELD, :], coef[:, :, e % HALF]
                    else:
                        hid, co = hidden[:, bass.ds(i * 4 + e % HELD, 1), :].squeeze(1), coef[:, :, bass.ds(i * 4 + e % HALF, 1)].squeeze(2)
                    at = 2 * (c0 + e)
                    dve.tensor_tensor(product[:, e % 2, :], hid, co, ALU.mult).then_inc(coef_read, 1)
                    dve.wait_ge(coef_read, i * 8 + (at + 1))
                    dve.tensor_copy(weighed[:, 0, e % 4, :], product[:, e % 2, :]).then_inc(coef_read, 1)
                    dve.wait_ge(coef_read, i * 8 + (at + 2))
                    dve.tensor_tensor(weighed[:, 1, e % 4, :], product[:, e % 2, :], weighed[:, 0, e % 4, :].bitcast(F32), ALU.subtract).then_inc(chunk_ready, 1)

                built = l * 2 * S // 8
                for x, (kind, e, h, steps) in enumerate(SEGMENTS):
                    if x == 0:
                        continue
                    w0, base, slots, pace = W0[f"expert{l}.{x}"], SLOT0[f"expert{l}.{x}"], SLOTS_OF[kind], ITEMS_OF[kind]
                    h0 = 0 if x == 1 else HALF
                    if x == 2:
                        dve.wait_ge(lo_ready, base)
                        ahead[0] = base
                        split_to(base - 1)
                    if x == 6:
                        dve.wait_ge(lo_ready, base + AHEAD)
                    if x in (2, 6):
                        for b in range(4):
                            dve.wait_ge(*freed(w0 - 4 + b))
                    elif kind == "upcoef" and (l or x > 1):
                        dve.wait_ge(chunk_ready, c0 + h0)
                    elif e is not None:
                        last = max(W0[f"expert{l}.{z}"] + (c - h2) * ITEMS_OF[kind2] for z, (kind2, _, h2, steps2) in enumerate(SEGMENTS)
                                   if h2 is not None for c in range(e, e + steps) if h2 <= c < h2 + steps2)
                        for b in range(4):
                            dve.wait_ge(*freed(last - b))

                    def four(at, i):
                        for j in range(at, at + 4):
                            if e is not None:
                                weigh(e + j, i)
                            if kind != "upcoef":
                                for y in range(slots):
                                    n = base + j * slots + AHEAD + y
                                    split_lo(dve, n, i, 4 * slots)
                            if kind == "upcoef":
                                for y in range(2):
                                    w = w0 + pace * (j - 1) + 1 + y if j else None
                                    one_hots(built + 2 * j + y, 16 * j + 8 * y, h0, w, i)

                    four(0, 0)
                    with dve.Fori(0, steps // 4 - 1) as i:
                        four(4, i)
                    if kind == "upcoef":
                        built += S // 8
                ahead[0] = SLOT0[f"expert{l}.{len(SEGMENTS) - 1}"] + SEGMENTS[-1][3] + AHEAD
                dve.wait_ge(chunk_used, c0 + CHUNKS)
                for k in range(K):
                    dve.tensor_tensor(stream[:, k, XS], stream[:, k, XS], acc[:, k // 2, (k % 2) * S:(k % 2 + 1) * S], ALU.add).then_inc(stream_block, 1)
                dve.wait_ge(stream_block, K * (l + 1))
                dve.engine_nop().then_inc(stream_ready, 1)

            def odd():
                split_to(SLOT0["odd"])
                for b in range(2):
                    ins = dve.memset(u_pad[:, b, 0:2], 0.0)
                ins.then_inc(vec.sem, vec.up())
                for i, (kind, c) in enumerate(ODD_ITEMS):
                    w = W0["odd"] + i
                    split_to(SLOT0["odd"] + i)
                    b = c % 2
                    if kind == "value":
                        dve.wait_ge(*freed(w - 1))
                        dve.wait_ge(*done(w))
                        if c >= 2:
                            dve.wait_ge(zy_ready, c - 1)
                        dve.tensor_tensor(u_pad[:, b, 2:S + 2], work[:, w % 4, 0:S], cg[:, b, :], ALU.mult).then_inc(bank_free[w % 4], 1)
                        step()
                        dve.wait_ge(*freed(w))
                        dve.tensor_scalar(y_tmp[:, b, 0, :], u_pad[:, b, 0:S], conv[:, 0, c:c + 1], None, ALU.mult).then_inc(vec.sem, vec.up())
                        step()
                        dve.scalar_tensor_tensor(y_tmp[:, b, 1, :], u_pad[:, b, 1:S + 1], conv[:, 1, c:c + 1], y_tmp[:, b, 0, :], ALU.mult, ALU.add).then_inc(vec.sem, vec.up())
                        step()
                        dve.scalar_tensor_tensor(y_tmp[:, b, 0, :], u_pad[:, b, 2:S + 2], conv[:, 2, c:c + 1], y_tmp[:, b, 1, :], ALU.mult, ALU.add).then_inc(vec.sem, vec.up())
                        step()
                    elif kind == "bgate":
                        dve.wait_ge(*done(w))
                        dve.tensor_tensor(y_tmp[:, b, 1, :], work[:, w % 4, 0:S], y_tmp[:, b, 0, :], ALU.mult).then_inc(bank_free[w % 4], 1)
                        dve.wait_ge(*freed(w))
                        parts(c, slice(0, S), y_tmp[:, b, 1, :], zy_ready, z2_hi, z2_lo)

            def feed_forward(x, cols):
                width = cols.stop - cols.start
                for i, (kind, c) in enumerate(FFN_ITEMS):
                    split_to(SLOT0[f"ffn{x}"] + i)
                    if kind == "ffup":
                        w = W0[f"ffn{x}"] + i
                        dve.wait_ge(*freed(w - 1))
                        dve.wait_ge(*done(w))
                        dve.tensor_tensor(ff_hid[:, c % 2, 0:width], work[:, w % 4, 0:width], ff_silu[:, c % 2, 0:width], ALU.mult).then_inc(bank_free[w % 4], 1)
                        dve.wait_ge(*freed(w))
                        parts(c, cols, ff_hid[:, c % 2, 0:width], ff_ready, ff_hi, ff_lo)

            def mix():
                w0, n = W0["mix"], SLOT0["mix"]
                dve.wait_ge(const2_in, 16 * 8)
                for i, (kind, j) in enumerate(MIX_ITEMS):
                    w = w0 + i
                    cols = XS if j < 4 or 8 <= j < 12 else ALL
                    width = cols.stop - cols.start
                    if kind in ("proj", "val", "swaval"):
                        n += 2 if kind == "val" else 1
                        split_to(n - 1)
                    if kind == "forget":
                        dve.wait_ge(*done(w))
                        dve.tensor_scalar(forget[0:FOXH, 1, :], work[0:FOXH, w % 4, 0:TA], small[0:FOXH, 4:5], None, ALU.add).then_inc(bank_free[w % 4], 1)
                        dve.wait_ge(*freed(w))
                        dve.engine_nop().then_inc(forget_in, 1)
                        dve.tensor_scalar(forget[0:FOXH, 5, :], forget[0:FOXH, 1, :], 0.0, None, ALU.min).then_inc(vec.sem, vec.up())
                        step()
                        dve.wait_ge(forget_out, 1)
                        dve.tensor_tensor(forget[0:FOXH, 6, :], forget[0:FOXH, 5, :], forget[0:FOXH, 4, :], ALU.subtract).then_inc(vec.sem, vec.up())
                        step()
                        dve.tensor_tensor_scan(forget[0:FOXH, 0, :], forget[0:FOXH, 6, :], forget[0:FOXH, 7, :], 0.0, ALU.add, ALU.add).then_inc(forget_ready, 1)
                    elif kind == "mean":
                        dve.wait_ge(*freed(w))
                        ms = qk2ms[:, j % 2, 0:width]
                        dve.reciprocal(ms, ms).then_inc(vec.sem, vec.up())
                        step()
                        dve.scalar_tensor_tensor(qk2[:, j, 0:width], qk2raw[:, j % 2, 0:width], cst("headgain")[:, j:j + 1], ms, ALU.mult, ALU.mult).then_inc(qk2_ready, 1)
                    elif kind == "table":
                        lo, hi = ((0, DX), (DX, DTAB))[j]
                        dve.wait_ge(*done(w))
                        dve.tensor_copy(table_out[0:FOXH, lo:hi], work[0:FOXH, w % 4, 0:hi - lo]).then_inc(bank_free[w % 4], 1)
                        dve.wait_ge(*freed(w))
                        dve.engine_nop().then_inc(table_ready, 1)

            def attend(name, n_before):
                fox = name == "fox"
                if not fox:
                    dve.wait_ge(bias_in, 64)

                def out(w, h):
                    half = slice((h % 2) * HD2, (h % 2 + 1) * HD2)
                    x, src = 0 if fox else 1, work[half, w % 4, 0:S]
                    dve.tensor_copy(att2_hi[half, x, h // 2, :], src).then_inc(vec.sem, vec.up())
                    step()
                    dve.tensor_tensor(att2_lo[half, x, h // 2, :], src, att2_hi[half, x, h // 2, :].bitcast(F32), ALU.subtract).then_inc(bank_free[w % 4], 1)

                def addend(u):
                    h, t = u // NT, u % NT
                    n = META + P * (t + 1)
                    return mask2[:, t, 0:n] if fox else bias2[:, t, h, 0:n]

                soft_rows(FOX_ITEMS, name, scores2, n_before, addend, HD2 ** -0.5, lambda u: META + P * (u % NT + 1), not fox, out)

            def branch():
                for c in range(K):
                    w = W0["branch"] + 2 * c
                    b = c % 2
                    split_to(SLOT0["branch"] + c)
                    dve.wait_ge(*freed(W0["gates"] + 2 * K - 1))
                    for x in range(2):
                        dve.wait_ge(*done(w + x))
                        dve.tensor_tensor(mix_t[:, b, x, :], work[:, (w + x) % 4, 0:S], gate2[:, x * K + c, :], ALU.mult).then_inc(bank_free[(w + x) % 4], 1)
                    for x in range(2):
                        dve.wait_ge(*freed(w + x))
                    dve.tensor_tensor(mix_y[:, b, :], mix_t[:, b, 0, :], mix_t[:, b, 1, :], ALU.add).then_inc(vec.sem, vec.up())
                    step()
                    parts(c, XS, mix_y[:, b, :], branch_ready)

            dve.wait_ge(const_in, 16)
            dve.tensor_copy(keys4[:, :, :], iota.unsqueeze(2).to_broadcast([P, NKEYS, 4]))
            for x in normed_parts:
                dve.memset(x[:, K * TA:].bitcast(F32), 0.0)
            split_to(-1)
            dve.wait_ge(x_in, 16)
            norm(0, XS)
            dve.wait_ge(early_in, 16)
            even()
            retention()
            moba()
            residual("evenout", 1, XS)
            norm(1, XS)
            peer(0)
            norm(2, XS)
            odd()
            residual("oddout", 3, XS)
            norm(3, XS)
            peer(1)
            norm(4, XS, stream)
            dve.wait_ge(meta_in, 16)
            norm(5, ALL)
            feed_forward(1, ALL)
            residual("ffn1out", 5, ALL, 0.5, 3)
            norm(6, ALL)
            mix()
            attend("fox", HEADS * NT)
            attend("swa", HEADS * NT + FOXH * NT)
            for i in range(2 * K):
                split_to(SLOT0["gates"] + i)
            branch()
            residual("mixout", 6, XS)
            norm(7, XS)
            feed_forward(2, XS)
            residual("ffn2out", 7, XS, 0.5, 3)


def fixed_arrays():
    f = np.float32
    c = {"ident": np.eye(P, dtype=f), "inv_d": np.full((P, P), 1.0 / D, f), "inv_head": np.full((P, P), 1.0 / P, f)}
    rot = np.zeros((P, P), f)
    half = P // 2
    rot[np.arange(half) + half, np.arange(half)] = -1.0
    rot[np.arange(half), np.arange(half) + half] = 1.0
    c["rot"] = rot
    c["inv_half"] = np.kron(np.eye(2), np.full((HD2, HD2), 1.0 / HD2)).astype(f)
    c["iota"] = np.tile(np.arange(P, dtype=f), (P, 1))
    inv = f(10000.0) ** (-np.arange(half, dtype=f) / f(half))
    ang = (np.arange(S, dtype=f)[:, None] * inv[None, :]).astype(f)
    c["cos"] = np.tile(np.cos(ang).astype(f).T, (2, 1))
    c["sin"] = np.tile(np.sin(ang).astype(f).T, (2, 1))
    log_g = np.log(1.0 - 2.0 ** (-5.0 - np.arange(HEADS)))
    diff = np.arange(S)[None, :] - np.arange(P)[:, None]
    dec = np.where(diff >= 0, np.exp(log_g[:, None, None] * np.maximum(diff, 0)), 0.0) * P ** -0.5
    c["decay"] = np.concatenate([dec, dec[:, :, :P]], axis=2).transpose(1, 0, 2).reshape(P, -1).astype(f)
    q, k = np.arange(P)[:, None], np.arange(P)[None, :]
    c["causal"] = np.concatenate([np.zeros((P, P)), np.where(k <= q, 0.0, NEG)], axis=1).astype(f)
    cols = np.arange(TA)
    late = {"foxmask": np.stack([np.where(cols[None, :] <= META + P * t + q, 0.0, NEG) for t in range(NT)], axis=1).astype(f)}
    eye = np.eye(FOXH)
    late["pick_head"] = np.repeat(HD2 ** 0.5 * eye[:, :, None], TA, axis=2).astype(f)
    late["neg_head"] = np.repeat(-HD2 ** 0.5 * eye[:, :, None], P, axis=2).astype(f)

    def bucket(d):
        exact = NB // 2
        large = exact + (np.log(np.maximum(d, 1).astype(f) / f(exact)) / f(np.log(P / exact)) * (NB - exact)).astype(np.int32)
        return np.where(d < exact, d, np.minimum(large, NB - 1))

    r = np.arange(DX) - 255
    x = np.where((r <= 0) & (r > -P), bucket(np.maximum(-r, 0)), NB)
    m = bucket(np.maximum(META - (np.arange(DM) - 255), 0))
    onehot = np.zeros((NB + 1, DTAB), f)
    onehot[np.concatenate([x, m]), np.arange(DTAB)] = 1.0
    late["onehot"] = onehot
    return c, late


def kernel(**inputs):
    import concourse.bacc as bacc
    from concourse.bass_utils import run_bass_kernel_spmd

    x = {k: np.asarray(v) for k, v in inputs.items()}

    def blocks(w):
        n = w.shape[1] // P
        return w.reshape(-1, P, n, P).transpose(2, 1, 0, 3).reshape(n, P, -1)

    def cols(v):
        return v.reshape(-1, P).T

    const, late = fixed_arrays()
    gains = [x["norm_mix"][0], x["norm_ffn"][0], x["norm_mix"][1], x["norm_ffn"][1], x["final_norm"],
             x["ffn1_norm_2"][0], x["mix_norm_2"][0], x["ffn2_norm_2"][0]]
    const["gains"] = np.concatenate([cols(g) for g in gains], axis=1)
    const["conv"] = np.concatenate([cols(w) for w in x["odd_conv"][0]], axis=1)
    twice = lambda g: np.tile(g, 2)[:, None]
    const["headgain"] = np.concatenate([twice(x["fox_q_norm_2"][0])] * 4 + [twice(x["fox_k_norm_2"][0])] * 4
                                       + [twice(x["swa_q_norm_2"][0])] * 4 + [twice(x["swa_k_norm_2"][0])] * 2, axis=1)
    arrays = {"const": np.concatenate([const[name] for name in CONST], axis=1),
              "early": np.concatenate([const[name] for name, _ in EARLY], axis=1)}
    arrays.update(late)
    arrays["x"] = x["x"][0].T.reshape(K, P, S).transpose(1, 0, 2)
    arrays["meta"] = x["meta_tokens_2"].T.reshape(K, P, META).transpose(1, 0, 2)
    w = blocks(x["even_w_in"][0])
    arrays["even_in"] = w[list(range(8)) + list(range(12, 20)) + list(range(8, 12)) + list(range(20, 28))]
    arrays["even_out"] = blocks(x["even_w_out"][0])
    w = blocks(x["odd_w_in"][0])
    arrays["odd_in"] = w[[j for c in range(K) for j in (K + c, 2 * K + c, c)]]
    arrays["odd_out"] = blocks(x["odd_w_out"][0])
    for l in range(2):
        arrays[f"query{l}"] = blocks(x["peer_w_q"][l])
        arrays[f"subkey{l}"] = x["peer_sub_keys"][l].reshape(16, NKEYS, P).transpose(2, 0, 1).reshape(P, -1)
        arrays[f"u{l}"] = x["peer_u"][l].reshape(CHUNKS, P, K, P).transpose(0, 3, 2, 1).reshape(CHUNKS, P, D)
        arrays[f"v{l}"] = x["peer_v"][l].reshape(CHUNKS, P, D)
    for n in (1, 2):
        w = blocks(x[f"ffn{n}_w_in_2"][0])
        arrays[f"ffn{n}_in"] = w[[j for c in range(FC) for j in (c, FC + c)]]
        arrays[f"ffn{n}_out"] = blocks(x[f"ffn{n}_w_out_2"][0])
    w = x["w_in_2"][0]
    qa, ka, va, fa, qb, kb, vb, ga, gb = np.split(w, np.cumsum([512, 512, 512, FOXH, 512, 128, 128, D]), axis=1)
    arrays["mix_in"] = blocks(np.concatenate([qa, ka, qb, kb[:, :HD2], kb[:, :HD2], kb[:, HD2:], kb[:, HD2:], va, vb], axis=1))
    arrays["gate_in"] = blocks(np.concatenate([ga, gb], axis=1))
    arrays["w_forget"] = fa.reshape(K, P, FOXH).transpose(1, 0, 2)
    arrays["forget_bias"] = x["forget_bias_2"][0][:, None]
    arrays["table"] = x["rel_bias_table_2"]
    arrays["sinks"] = x["swa_sinks_2"][0]
    arrays["branch"] = blocks(np.concatenate([x["w_branch_fox_2"][0], x["w_branch_swa_2"][0]], axis=0))
    arrays["mix_out"] = blocks(x["w_out_2"][0])

    nc = bacc.Bacc("TRN2", target_bir_lowering=False, num_devices=1)
    aps, maps = {}, {}
    for name, v in arrays.items():
        v = np.ascontiguousarray(v)
        maps["in_" + name] = v
        aps[name] = nc.dram_tensor("in_" + name, list(v.shape), mybir.dt.from_np(v.dtype), kind="ExternalInput").ap()
    aps["scratch"] = nc.dram_tensor("bias_by_distance", [P, FOXH, DTAB], F32, kind="Internal").ap()
    aps["out"] = nc.dram_tensor("out", [P, K, S], F32, kind="ExternalOutput").ap()
    build(nc, aps)
    r = run_bass_kernel_spmd(nc, [maps], core_ids=[0])
    return r.results[0]["out"].transpose(1, 0, 2).reshape(D, S).T[None]
```
